# Optimizing a Trainium2 kernel written in Bass

```python
import jax
import jax.numpy as jnp
from jax import lax
import numpy as np

D_MODEL = 1024
BATCH = 1
SEQ = 128
DEPTH = 2
DEC_BATCH = 1
DEC_SEQ = 512
PAST_LEN = 128

GRID_W = 64
N_EVEN = (DEPTH + 1) // 2
N_ODD = DEPTH // 2
HA_HEADS = 4
HA_DK = 128
HA_DV = 128
HA_W = HA_HEADS * HA_DK
CHUNK = 32
MLA_HEADS = 8
MLA_DN = 64
MLA_DR = 32
MLA_DV = 64
MLA_Q_RANK = 384
MLA_KV_RANK = 256
ROPE_BASE = 10000.0
Q_BLOCK = 128
AB_IN = 5 * HA_W + MLA_Q_RANK + MLA_KV_RANK + MLA_DR
AB_OUT = HA_HEADS * HA_DV + MLA_HEADS * MLA_DV
AB_SPLITS = (HA_W, 2 * HA_W, 3 * HA_W, 4 * HA_W, 5 * HA_W, 5 * HA_W + MLA_Q_RANK, 5 * HA_W + MLA_Q_RANK + MLA_KV_RANK)
SC_W = 512
SC_K = 3
CF_W = 512
CF_K = 31
CD_IN = 3 * SC_W + 2 * CF_W
CD_OUT = SC_W + CF_W
CD_SPLITS = (SC_W, 2 * SC_W, 3 * SC_W, 3 * SC_W + CF_W)
N_GROUPS = 4
EXP_PER_GROUP = 8
N_EXPERTS = N_GROUPS * EXP_PER_GROUP
EXP_FF = 128
TOP_K = 2
ALPHA = (2.0 * DEPTH) ** 0.25
BETA = (8.0 * DEPTH) ** -0.25
LN_EPS = 1e-5
RMS_EPS = 1e-6
F32 = jnp.float32

kernel_name = 'hybrid_dit_hgrn2_mla_conv_hmoe_step'

def _layer_norm(x, g, b):
    x32 = x.astype(F32)
    mu = jnp.mean(x32, axis=-1, keepdims=True)
    var = jnp.mean(jnp.square(x32 - mu), axis=-1, keepdims=True)
    y = (x32 - mu) * lax.rsqrt(var + LN_EPS)
    return (y * g.astype(F32) + b.astype(F32)).astype(x.dtype)

def _rms_norm(x, g):
    x32 = x.astype(F32)
    y = x32 * lax.rsqrt(jnp.mean(jnp.square(x32), axis=-1, keepdims=True) + RMS_EPS)
    return (y * g.astype(F32)).astype(x.dtype)

def _modulate(x, shift, scale):
    return x * (1.0 + scale) + shift

def _dwconv(x, w):
    k, ch = w.shape
    return lax.conv_general_dilated(x, w[:, None, :].astype(x.dtype), window_strides=(1,),
                                    padding=[(k // 2, k // 2)],
                                    dimension_numbers=('NWC', 'WIO', 'NWC'),
                                    feature_group_count=ch)

def _axial_rope_tables(n_tok):
    rows = n_tok // GRID_W
    pos_r = jnp.repeat(jnp.arange(rows, dtype=F32), GRID_W)
    pos_c = (jnp.arange(rows * GRID_W) % GRID_W).astype(F32)
    n_freq = MLA_DR // 4
    inv = ROPE_BASE ** (-jnp.arange(n_freq, dtype=F32) / n_freq)
    ang = jnp.stack([pos_r[:, None] * inv, pos_c[:, None] * inv], axis=1)
    return jnp.cos(ang), jnp.sin(ang)

def _rope_2d(x, cos, sin):
    xs = x.reshape(x.shape[:-1] + (2, 2, MLA_DR // 4))
    x1, x2 = xs[..., 0, :], xs[..., 1, :]
    cos = cos.astype(x.dtype)
    sin = sin.astype(x.dtype)
    out = jnp.stack([x1 * cos - x2 * sin, x1 * sin + x2 * cos], axis=-2)
    return out.reshape(x.shape)

def _chunk_scan(q, k, v, log_f, s0):
    B, L, H, _ = q.shape
    dv = v.shape[-1]
    n = L // CHUNK

    def to_chunks(t):
        return t.reshape(B, n, CHUNK, H, t.shape[-1]).transpose(1, 0, 3, 2, 4)

    tri = jnp.tril(jnp.ones((CHUNK, CHUNK), dtype=bool))[:, :, None]

    def step(S, blk):
        qc, kc, vc, gc = blk
        b = jnp.cumsum(gc, axis=2)
        diff = b[:, :, :, None, :] - b[:, :, None, :, :]
        decay = jnp.exp(jnp.where(tri, diff, -jnp.inf))
        scores = jnp.einsum('bhtk,bhsk,bhtsk->bhts', qc, kc, decay)
        o = scores @ vc + jnp.einsum('bhtk,bhkv->bhtv', qc * jnp.exp(b), S)
        b_last = b[:, :, -1:, :]
        S_new = jnp.exp(b_last[:, :, 0, :])[..., None] * S + jnp.einsum('bhsk,bhsv->bhkv', kc * jnp.exp(b_last - b), vc)
        return S_new, o

    S_fin, o = lax.scan(step, s0.astype(F32), (to_chunks(q), to_chunks(k), to_chunks(v), to_chunks(log_f)))
    return o.transpose(1, 0, 3, 2, 4).reshape(B, L, H, dv), S_fin

def _flip(t):
    return jnp.flip(t, axis=1)

def _hgrn2(q_lin, f_lin_f, f_lin_b, i_lin, g_lin, lb_f, lb_b, g_norm, s0_f, s0_b):
    B, L, _ = q_lin.shape

    def heads(t):
        return t.astype(F32).reshape(B, L, HA_HEADS, -1)

    q = jax.nn.silu(heads(q_lin))
    v = heads(i_lin)

    def forget(f_lin, lb):
        lb = lb.reshape(HA_HEADS, HA_DK)
        f = lb + (1.0 - lb) * jax.nn.sigmoid(heads(f_lin))
        return jnp.log(f), 1.0 - f

    logf_f, k_f = forget(f_lin_f, lb_f)
    logf_b, k_b = forget(f_lin_b, lb_b)
    o_f, s_f = _chunk_scan(q, k_f, v, logf_f, s0_f)
    o_b, s_b = _chunk_scan(_flip(q), _flip(k_b), _flip(v), _flip(logf_b), s0_b)
    o = _rms_norm(o_f + _flip(o_b), g_norm) * jax.nn.silu(heads(g_lin))
    return o.reshape(B, L, HA_HEADS * HA_DV).astype(q_lin.dtype), s_f, s_b

def _attend(q_nope, q_rope, k_nope, k_rope, v):
    B, L, H, _ = q_nope.shape
    nb = L // Q_BLOCK
    scale = (MLA_DN + MLA_DR) ** -0.5

    def blocks(t):
        return t.reshape(B, nb, Q_BLOCK, H, t.shape[-1]).transpose(1, 0, 2, 3, 4)

    def one_block(qb):
        qn, qr = qb
        s = jnp.einsum('bqhd,bkhd->bhqk', qn, k_nope) + jnp.einsum('bqhr,bkr->bhqk', qr, k_rope)
        p = jax.nn.softmax(s.astype(F32) * scale, axis=-1)
        return jnp.einsum('bhqk,bkhd->bqhd', p.astype(v.dtype), v)

    o = lax.map(one_block, (blocks(q_nope), blocks(q_rope)))
    return o.transpose(1, 0, 2, 3, 4).reshape(B, L, H, MLA_DV)

def _mla(cq_raw, ckv_raw, kr, q_norm_g, w_uq, kv_norm_g, w_ukv, rope, ctx_ckv, ctx_kr):
    B, L, _ = cq_raw.shape
    q = (_rms_norm(cq_raw, q_norm_g) @ w_uq).reshape(B, L, MLA_HEADS, MLA_DN + MLA_DR)
    q_nope, q_rope = q[..., :MLA_DN], q[..., MLA_DN:]
    ckv = _rms_norm(ckv_raw, kv_norm_g)
    if rope is None:
        ckv_keys, kr_keys = ckv, kr
    else:
        cos, sin = rope
        q_rope = _rope_2d(q_rope, cos[:, None], sin[:, None])
        ckv_keys = jnp.concatenate([ckv, ctx_ckv.astype(ckv.dtype)], axis=1)
        kr_keys = jnp.concatenate([_rope_2d(kr, cos, sin), ctx_kr.astype(kr.dtype)], axis=1)
    kv = (ckv_keys @ w_ukv).reshape(B, ckv_keys.shape[1], MLA_HEADS, MLA_DN + MLA_DV)
    o = _attend(q_nope, q_rope, kv[..., :MLA_DN], kr_keys, kv[..., MLA_DN:])
    return o.reshape(B, L, MLA_HEADS * MLA_DV), ckv

def _ab_mixer(h, s0_f, s0_b, rope, ctx_ckv, ctx_kr, w_in, w_out, lb_f, lb_b, g_norm,
              q_norm_g, w_uq, kv_norm_g, w_ukv):
    q_a, f_f, f_b, i_a, g_a, cq, ckv_raw, kr = jnp.split(h @ w_in, AB_SPLITS, axis=-1)
    o_a, s_f, s_b = _hgrn2(q_a, f_f, f_b, i_a, g_a, lb_f, lb_b, g_norm, s0_f, s0_b)
    o_b, ckv = _mla(cq, ckv_raw, kr, q_norm_g, w_uq, kv_norm_g, w_ukv, rope, ctx_ckv, ctx_kr)
    y = jnp.concatenate([o_a, o_b], axis=-1) @ w_out
    return y, s_f, s_b, ckv, kr

def _cd_mixer(h, w_in, w_out, sc_w, cf_w, cf_b, cf_g, cf_beta):
    bg, cg, xv, ga, gb = jnp.split(h @ w_in, CD_SPLITS, axis=-1)
    y_sc = bg * _dwconv(cg * xv, sc_w)
    u = ga * jax.nn.sigmoid(gb)
    u = _layer_norm(_dwconv(u, cf_w) + cf_b, cf_g, cf_beta)
    y_cf = jax.nn.silu(u)
    return jnp.concatenate([y_sc, y_cf], axis=-1) @ w_out

def _hier_moe(h, w_group, w_expert, w_gate, w_up, w_down):
    B, L, D = h.shape
    t = h.reshape(B * L, D)
    p_group = jax.nn.softmax((t @ w_group).astype(F32), axis=-1)
    g_sel = jnp.argmax(p_group, axis=-1)
    p_g = jnp.max(p_group, axis=-1, keepdims=True)
    e_logits = (t @ w_expert).astype(F32).reshape(-1, N_GROUPS, EXP_PER_GROUP)
    e_in = jnp.einsum('tg,tge->te', jax.nn.one_hot(g_sel, N_GROUPS, dtype=F32), e_logits)
    top_v, top_i = lax.top_k(e_in, TOP_K)
    w_top = jax.nn.softmax(top_v, axis=-1) * p_g
    expert_id = g_sel[:, None] * EXP_PER_GROUP + top_i
    combine = jnp.einsum('tk,tke->te', w_top, jax.nn.one_hot(expert_id, N_EXPERTS, dtype=F32))
    hid = jax.nn.silu(jnp.einsum('td,edf->tef', t, w_gate)) * jnp.einsum('td,edf->tef', t, w_up)
    out = jnp.einsum('tef,efd->td', hid * combine.astype(h.dtype)[:, :, None], w_down)
    return out.reshape(B, L, D)

def setup_inputs(seed: int = 0) -> dict:
    key = jax.random.key(seed)
    ks = iter(jax.random.split(key, 40))

    def nrm(shape, scale):
        return scale * jax.random.normal(next(ks), shape, F32)

    return {
        'x_prompt': nrm((BATCH, SEQ, D_MODEL), 1.0),
        'x_sample': nrm((DEC_BATCH, DEC_SEQ, D_MODEL), 1.0),
        'state_hgrn_fwd': nrm((DEC_BATCH, N_EVEN, HA_HEADS, HA_DK, HA_DV), 0.5),
        'state_hgrn_bwd': nrm((DEC_BATCH, N_EVEN, HA_HEADS, HA_DK, HA_DV), 0.5),
        'cache_mla_ckv': nrm((DEC_BATCH, N_EVEN, PAST_LEN, MLA_KV_RANK), 1.0),
        'cache_mla_krope': nrm((DEC_BATCH, N_EVEN, PAST_LEN, MLA_DR), 1.0),
        'c': nrm((DEC_BATCH, D_MODEL), 1.0),
        'c_ctx': nrm((D_MODEL,), 1.0),
        'mod_w': nrm((DEPTH, D_MODEL, 6 * D_MODEL), 0.5 * D_MODEL ** -0.5),
        'mod_b': nrm((DEPTH, 6 * D_MODEL), 0.02),
        'ln_g': 1.0 + nrm((DEPTH, 2, D_MODEL), 0.05),
        'ln_b': nrm((DEPTH, 2, D_MODEL), 0.02),
        'ab_w_in': nrm((N_EVEN, D_MODEL, AB_IN), D_MODEL ** -0.5),
        'ab_w_out': nrm((N_EVEN, AB_OUT, D_MODEL), BETA * AB_OUT ** -0.5),
        'hgrn_lb_logits': nrm((N_EVEN + 1, 2, HA_W), 0.5),
        'hgrn_norm_g': 1.0 + nrm((N_EVEN, HA_DV), 0.05),
        'mla_q_norm_g': 1.0 + nrm((N_EVEN, MLA_Q_RANK), 0.05),
        'mla_w_uq': nrm((N_EVEN, MLA_Q_RANK, MLA_HEADS * (MLA_DN + MLA_DR)), MLA_Q_RANK ** -0.5),
        'mla_kv_norm_g': 1.0 + nrm((N_EVEN, MLA_KV_RANK), 0.05),
        'mla_w_ukv': nrm((N_EVEN, MLA_KV_RANK, MLA_HEADS * (MLA_DN + MLA_DV)), MLA_KV_RANK ** -0.5),
        'cd_w_in': nrm((N_ODD, D_MODEL, CD_IN), D_MODEL ** -0.5),
        'cd_w_out': nrm((N_ODD, CD_OUT, D_MODEL), BETA * CD_OUT ** -0.5),
        'sc_conv_w': nrm((N_ODD, SC_K, SC_W), SC_K ** -0.5),
        'cf_conv_w': nrm((N_ODD, CF_K, CF_W), CF_K ** -0.5),
        'cf_conv_b': nrm((N_ODD, CF_W), 0.02),
        'cf_ln_g': 1.0 + nrm((N_ODD, CF_W), 0.05),
        'cf_ln_b': nrm((N_ODD, CF_W), 0.02),
        'moe_w_group': nrm((DEPTH, D_MODEL, N_GROUPS), D_MODEL ** -0.5),
        'moe_w_expert': nrm((DEPTH, D_MODEL, N_EXPERTS), D_MODEL ** -0.5),
        'moe_w_gate': nrm((DEPTH, N_EXPERTS, D_MODEL, EXP_FF), D_MODEL ** -0.5),
        'moe_w_up': nrm((DEPTH, N_EXPERTS, D_MODEL, EXP_FF), D_MODEL ** -0.5),
        'moe_w_down': nrm((DEPTH, N_EXPERTS, EXP_FF, D_MODEL), BETA * EXP_FF ** -0.5),
    }

def reference(x_prompt, x_sample, state_hgrn_fwd, state_hgrn_bwd, cache_mla_ckv, cache_mla_krope,
              c, c_ctx, mod_w, mod_b, ln_g, ln_b, ab_w_in, ab_w_out, hgrn_lb_logits, hgrn_norm_g,
              mla_q_norm_g, mla_w_uq, mla_kv_norm_g, mla_w_ukv, cd_w_in, cd_w_out, sc_conv_w,
              cf_conv_w, cf_conv_b, cf_ln_g, cf_ln_b, moe_w_group, moe_w_expert, moe_w_gate,
              moe_w_up, moe_w_down):
    lb_all = jnp.cumsum(jax.nn.softmax(hgrn_lb_logits.astype(F32), axis=0), axis=0)[:N_EVEN]
    rope = _axial_rope_tables(x_sample.shape[1])
    bp = x_prompt.shape[0]
    xp, xs = x_prompt, x_sample
    new_sf, new_sb, new_ckv, new_kr = [], [], [], []
    for l in range(DEPTH):
        m_ctx = jnp.split(jax.nn.silu(c_ctx) @ mod_w[l] + mod_b[l], 6, axis=-1)
        m_lat = jnp.split((jax.nn.silu(c) @ mod_w[l] + mod_b[l])[:, None, :], 6, axis=-1)
        hp = _modulate(xp, m_ctx[0], m_ctx[1])
        hs = _modulate(xs, m_lat[0], m_lat[1])
        if l % 2 == 0:
            e = l // 2
            ab = (ab_w_in[e], ab_w_out[e], lb_all[e, 0], lb_all[e, 1], hgrn_norm_g[e],
                  mla_q_norm_g[e], mla_w_uq[e], mla_kv_norm_g[e], mla_w_ukv[e])
            zeros = jnp.zeros((bp, HA_HEADS, HA_DK, HA_DV), F32)
            yp, sf, sb, ckv, kr = _ab_mixer(hp, zeros, zeros, None, None, None, *ab)
            ys, _, _, _, _ = _ab_mixer(hs, state_hgrn_fwd[:, e], state_hgrn_bwd[:, e], rope,
                                       cache_mla_ckv[:, e], cache_mla_krope[:, e], *ab)
            new_sf.append(sf.astype(x_prompt.dtype))
            new_sb.append(sb.astype(x_prompt.dtype))
            new_ckv.append(ckv)
            new_kr.append(kr)
        else:
            j = l // 2
            cd = (cd_w_in[j], cd_w_out[j], sc_conv_w[j], cf_conv_w[j], cf_conv_b[j], cf_ln_g[j], cf_ln_b[j])
            yp = _cd_mixer(hp, *cd)
            ys = _cd_mixer(hs, *cd)
        xp = _layer_norm(ALPHA * xp + m_ctx[2] * yp, ln_g[l, 0], ln_b[l, 0])
        xs = _layer_norm(ALPHA * xs + m_lat[2] * ys, ln_g[l, 0], ln_b[l, 0])
        moe = (moe_w_group[l], moe_w_expert[l], moe_w_gate[l], moe_w_up[l], moe_w_down[l])
        xp = _layer_norm(ALPHA * xp + m_ctx[5] * _hier_moe(_modulate(xp, m_ctx[3], m_ctx[4]), *moe), ln_g[l, 1], ln_b[l, 1])
        xs = _layer_norm(ALPHA * xs + m_lat[5] * _hier_moe(_modulate(xs, m_lat[3], m_lat[4]), *moe), ln_g[l, 1], ln_b[l, 1])
    new_state_hgrn_fwd = jnp.stack(new_sf, axis=1)
    new_state_hgrn_bwd = jnp.stack(new_sb, axis=1)
    new_cache_mla_ckv = jnp.stack(new_ckv, axis=1)
    new_cache_mla_krope = jnp.stack(new_kr, axis=1)
    return (xp, xs, new_state_hgrn_fwd, new_state_hgrn_bwd, new_cache_mla_ckv, new_cache_mla_krope)


_drawn_inputs = setup_inputs


def setup_inputs(seed=0):
    import zlib

    import numpy as np

    out = dict(_drawn_inputs(seed))
    spreads = {}
    factors = {'state_hgrn_fwd': 25.708,
     'state_hgrn_bwd': 25.277,
     'cache_mla_ckv': 8.0,
     'cache_mla_krope': 8.0,
     'hgrn_norm_g': 24.483,
     'mla_q_norm_g': 8.0,
     'mla_w_uq': 5.998,
     'cf_conv_b': 8.0,
     'cf_ln_g': 23.805,
     'cf_ln_b': 58.049}
    for name, (base, spread) in spreads.items():
        noise = np.random.default_rng([zlib.crc32(name.encode()), seed]).standard_normal(out[name].shape)
        drawn = base * np.exp(spread * noise) if base else spread * noise
        out[name] = jnp.asarray(drawn.astype(out[name].dtype))
    for name, factor in factors.items():
        out[name] = (out[name] * factor).astype(out[name].dtype)
    return out
```

```python
import concourse.bass as bass
from concourse import mybir
from contextlib import ExitStack
import numpy as np

D = 1024
KD = D // 128
NT = 5
NLAT = 512
NTOK = 640
CH = 32
HA, DK = 4, 128
MH, DN, DR, DV = 8, 64, 32, 64
QR, KVR = 384, 256
AB_IN = 5 * 512 + QR + KVR + DR
NE, NG, EG, FF = 32, 4, 8, 128
ALPHA = 4.0 ** 0.25
LN_EPS, RMS_EPS = 1e-5, 1e-6
SCALE = float(DN + DR) ** -0.5
CFK, SCK = 31, 3
PADW = 15
CXW = 15 + 512 + 15 + 128 + 15
COW = 656
NOROW = 4096.0

CONST_COLS = [("ident", 128), ("mask_f", 128), ("mask_b", 128), ("tri", 128), ("ones", 128), ("iota", 128),
              ("scan", 640), ("perm", 32), ("cos", 512), ("sin", 512), ("sel0", 128), ("sel1", 128),
              ("pidx", 1), ("prio4", 4), ("prio8", 8)]
COFF = {}
_at = 0
for _n, _w in CONST_COLS:
    COFF[_n] = (_at, _at + _w)
    _at += _w
NCONST = _at


def constants():
    c = np.zeros((128, NCONST), np.float32)

    def put(name, rows, value):
        a, b = COFF[name]
        c[rows, a:b] = value
    p = np.arange(128)
    same = (p[:, None] // CH) == (p[None, :] // CH)
    put("ident", slice(None), np.eye(128))
    put("mask_f", slice(None), same & (p[:, None] <= p[None, :]))
    put("mask_b", slice(None), same & (p[:, None] >= p[None, :]))
    put("tri", slice(None), p[:, None] < p[None, :])
    put("ones", slice(None), 1.0)
    put("iota", slice(None), p[None, :])
    put("scan", slice(None), (np.arange(NTOK) % CH != 0)[None, :])
    perm = np.zeros((32, 32))
    for a in range(2):
        for f in range(8):
            perm[a * 16 + 8 + f, a * 16 + f] = -1.0
            perm[a * 16 + f, a * 16 + 8 + f] = 1.0
    put("perm", slice(64, 96), perm)
    inv = np.float32(10000.0) ** (-np.arange(8, dtype=np.float32) / np.float32(8))
    tok = np.arange(NLAT)
    pos = np.stack([tok // 64, tok % 64]).astype(np.float32)
    ang = (pos[:, None, :] * inv[None, :, None]).astype(np.float32)
    ang = np.stack([ang, ang], axis=1).reshape(32, NLAT)
    put("cos", slice(64, 96), np.cos(ang))
    put("sin", slice(64, 96), np.sin(ang))
    put("sel0", slice(0, 1), 1.0)
    put("sel1", slice(1, 2), 1.0)
    put("pidx", slice(None), p[:, None])
    put("prio4", slice(None), np.arange(4, 0, -1)[None, :])
    put("prio8", slice(None), np.arange(8, 0, -1)[None, :])
    return c


def psum_groups():
    g = [("vec",)]

    def mod(l, c):
        g.append(("mod", l, c))
        g.append(("modb", l, c))
    for l in range(2):
        for c in range(4):
            mod(l, c)
        g += [("xT", l, k) for k in range(KD)]
        if l == 0:
            g += [("cq", t) for t in range(NT)]
            g += [("cqT", r) for r in range(3)] + [("ckvT", r) for r in range(2)] + [("krT",), ("krP",)]
            g += [("v", t) for t in range(6)]
            g += [("k", 0), ("q", 0), ("qP", 0)]
            steps = [(h, t) for h in range(MH) for t in range(NT)]
            g.append(("s",) + steps[0])
            for n, (h, t) in enumerate(steps):
                if h + 1 < MH and t == 0:
                    g += [("k", h + 1), ("q", h + 1)]
                if h + 1 < MH and t == 2:
                    g.append(("qP", h + 1))
                if n + 1 < len(steps):
                    g.append(("s",) + steps[n + 1])
                g += [("pt", h, t), ("o", h, t)]
            g += [("obT", j) for j in range(4)]
            g += [("hq", c, j) for c in range(3) for j in range(4)]
            g += [("hv", c, t) for c in range(2) for t in range(NT)]
            for u in range(4):
                g += [("hs", u, 0), ("hk", u, 0), ("hd", u, 0)]
                for n in range(NT):
                    if n + 1 < NT:
                        g += [("hs", u, n + 1), ("hk", u, n + 1), ("hd", u, n + 1)]
                    g.append(("ho", u, n))
            g += [("oaT", j) for j in range(4)]
        else:
            g += [("cd", c, j) for c in range(5) for j in range(4)]
            g += [("mean",), ("var",)]
        for c in range(4, 12):
            mod(l, c)
        g += [("y", l, t) for t in range(NT)]
        g += [("hT", l, t) for t in range(NT)]
        g += [("lg", l), ("ct", l)]
    return {name: n for n, name in enumerate(g)}


def build(nc, A, O):
    f32, i32, bf16 = mybir.dt.float32, mybir.dt.int32, mybir.dt.bfloat16
    ALU = mybir.AluOpType
    ACT = mybir.ActivationFunctionType
    AX = mybir.AxisListType
    GROUP = psum_groups()
    ctx = ExitStack()
    with ctx:
        def sb(name, shape, dt=f32):
            return ctx.enter_context(nc.sbuf_tensor(name, shape, dt))

        def sem(name):
            return ctx.enter_context(nc.semaphore(name))

        C = sb("consts", [128, NCONST])
        X = sb("x_tm", [128, NT, D])
        HT = sb("h_cm", [128, KD, NTOK])
        OT = sb("mix_cm", [128, KD, NTOK])
        W = sb("weights", [128, 3 * 4096])
        GR = sb("gate_rows", [128, 2048])
        LNR = sb("ln_rows", [128, 2, 1024])
        Z = sb("scratch", [128, 15360])
        MB2 = sb("mod_bias2", [2, 512])
        MR = sb("mod_row", [2, 2, 512])
        MC = sb("mod_cols", [128, 2, KD, 2])
        CT = sb("c_cm", [128, 16])
        VC = sb("vectors_cm", [128, 43])
        CW = sb("taps_cm", [128, 124])
        LBT = sb("lower_bound", [128, 2, 8])
        LBS = sb("lower_bound_work", [128, 3, 8])
        HNG = sb("hgrn_norm_row", [128, DK])
        SS = sb("square_sums", [128, NT, 2])
        RR = sb("rms_scale", [128, NT, 2])
        MXS = sb("softmax_max", [128, 2, 2])
        SUM = sb("softmax_sum", [128, 2, 2])
        DEC = sb("chunk_decay", [128, 2, 20])
        ZERO = sb("zero_state", [128, 128])
        HSS = sb("head_square_sums", [128, 20])
        ST6 = sb("ln_stats", [128, 2, 2, 6])
        MV = sb("ln_mean_var", [128, 2, 2])
        RSD = sb("ln_rstd", [128, 2, 2])
        WR = sb("router_w", [128, KD, 36])
        RS = sb("router_small", [128, 10, 8])
        O4 = sb("group_onehot", [128, NT, 4])
        W12 = sb("pair_weights", [128, 2, NT])
        RUN = sb("running_count", [128, NE])
        VAL = sb("slot_values", [128, NT, 4, NE], bf16)
        TI = sb("gather_rows", [128, 34], i32)
        TY = sb("scatter_rows", [128, 34], i32)
        RI = sb("rounds", [128, 1], i32)
        IXG = sb("gather_now", [128, 2], i32)
        IXY = sb("scatter_now", [128, 2], i32)
        PS = ctx.enter_context(nc.psum_tensor("ps", [128, 4, 1024], f32))

        def const(name, rows=slice(0, 128)):
            a, b = COFF[name]
            return C[rows, a:b]

        ident = const("ident")

        HD = nc.dram_tensor("h_rows", [NTOK, D], f32).ap()
        YD = nc.dram_tensor("expert_rows", [2 * NTOK, D], f32).ap()

        slot_full = [sem(f"slot_full{i}") for i in range(4)]
        slot_free = [sem(f"slot_free{i}") for i in range(4)]
        w_full = [sem(f"w_full{i}") for i in range(3)]
        vec_step, act_step, pool_step = sem("vec_step"), sem("act_step"), sem("pool_step")
        d_const, d_vec, d_x, d_rows = sem("d_const"), sem("d_vec"), sem("d_x"), sem("d_rows")
        d_cache, d_kv_out, d_xr = sem("d_cache"), sem("d_kv_out"), sem("d_xr")
        c_silu, lb_exp_in, lb_exp = sem("c_silu"), sem("lb_exp_in"), sem("lb_exp")
        sq_ready, rms_in, rms_sd, norm_ready = sem("sq_ready"), sem("rms_in"), sem("rms_sd"), sem("norm_ready")
        kr_ready, q_raw, q_rot = sem("kr_ready"), sem("q_raw"), sem("q_rot")
        max_ready, exp_ready = sem("max_ready"), sem("exp_ready")
        h_zero, h_f, h_l, h_arg, h_exp, h_mul = (sem("h_zero"), sem("h_f"), sem("h_l"), sem("h_arg"),
                                                 sem("h_exp"), sem("h_mul"))
        h_vm, h_s0, d_state = sem("h_vm"), sem("h_s0"), sem("d_state")
        o_var, o_sd, o_ready = sem("o_var"), sem("o_sd"), sem("o_ready")
        ln_var, ln_sd, x_ready, h_ready = sem("ln_var"), sem("ln_sd"), sem("x_ready"), sem("h_ready")
        d_ln = sem("d_ln")
        d_hst = [sem(f"d_hst{i}") for i in range(2)]
        d_wr = sem("d_wr")
        rt_exp_in, rt_exp, rt_mask, rt_ready = sem("rt_exp_in"), sem("rt_exp"), sem("rt_mask"), sem("rt_ready")
        d_yl = [sem(f"d_yl{i}") for i in range(2)]
        y_used = sem("y_used")
        moe_done = sem("moe_done")
        cd_pad, cd_conv, cd_sq, cd_sd, cd_u = (sem("cd_pad"), sem("cd_conv"), sem("cd_sq"), sem("cd_sd"), sem("cd_u"))
        cd_out = sem("cd_out_a")
        cd_out_v = sem("cd_out_v")
        d_out = sem("d_out")

        def moe_sems(l):
            names = ["w0", "w1", "w2", "w3", "g0", "g1", "t", "xa", "xv", "gu", "sg", "hid", "ht", "hidt",
                     "down", "ya", "yv", "s0", "s1", "mask", "mtab", "table", "s_ix", "pe_passed", "pool_passed"]
            return {n: sem(f"moe{l}_{n}") for n in names}
        MS = [moe_sems(l) for l in range(2)]

        def ps(*name):
            return PS[:, GROUP[name] % 4, :]

        def open_group(pe, *name):
            n = GROUP[name]
            if n >= 4:
                pe.wait_ge(slot_free[n % 4], n // 4)

        def close_group(ins, *name):
            ins.then_inc(slot_full[GROUP[name] % 4], 1)

        def filled(eng, *name):
            eng.wait_ge(slot_full[GROUP[name] % 4], GROUP[name] // 4 + 1)

        def release(ins, *name):
            ins.then_inc(slot_free[GROUP[name] % 4], 1)

        def emptied(eng, *name):
            eng.wait_ge(slot_free[GROUP[name] % 4], GROUP[name] // 4 + 1)

        def bank(b):
            return PS[:, b // 2, (b % 2) * 512:(b % 2) * 512 + 512]

        MB = [C[0:2, COFF["cos"][0]:COFF["cos"][1]], C[0:2, COFF["sin"][0]:COFF["sin"][1]], MB2[:, :]]
        V1, V2, V3 = GR[0:16, 0:128], GR[0:43, 128:256], GR[0:124, 256:384]
        def z(a, n):
            return Z[:, a:a + n]

        CQ = z(0, 3360).rearrange("p (t c) -> p t c", t=NT)
        CQT = z(3360, 1920).rearrange("p (r t) -> p r t", r=3)
        CKVT = z(5280, 1536).rearrange("p (r t) -> p r t", r=2)
        VT = z(6816, 3072).rearrange("p (t c) -> p t c", t=6)
        KT = z(9888, 1536).rearrange("p (b t) -> p b t", b=2)
        QT = z(11424, 1280).rearrange("p (b t) -> p b t", b=2)
        KRS, ROT1, ROT2 = z(12704, 512), z(13216, 512), z(13728, 512)
        CC = z(14240, 288)
        CKG = z(14528, KVR)
        LNF = LNR[:, :, :].rearrange("p a b -> p (a b)")
        PB = LNF[:, 0:1280].rearrange("p (b t) -> p b t", b=2)
        PTS = GR[:, 0:1280].rearrange("p (b t) -> p b t", b=2)
        OTF = OT[:, :, :].rearrange("p a b -> p (a b)")
        OB = OTF[:, 0:2560].rearrange("p (t c) -> p t c", t=NT)

        HQ = z(0, 2560).rearrange("p (h t) -> p h t", h=4)
        HF = [z(2560 + 2560 * d, 2560).rearrange("p (h t) -> p h t", h=4) for d in range(2)]
        HV = z(7680, 2560).rearrange("p (t c) -> p t c", t=NT)
        HG = z(10240, 2560).rearrange("p (t c) -> p t c", t=NT)
        HO = z(12800, 2560).rearrange("p (t c) -> p t c", t=NT)
        HTF = HT[:, :, :].rearrange("p a b -> p (a b)")
        QHAT, KHAT, QTIL, KTIL = [HTF[:, 1280 * i:1280 * (i + 1)].rearrange("p (h t) -> p h t", h=2)
                                  for i in range(4)]
        XF = X[:, :, :].rearrange("p a b -> p (a b)")
        BUFB = XF[:, 0:1280].rearrange("p (h t) -> p h t", h=2)
        BUFA = XF[:, 1280:2560].rearrange("p (h t) -> p h t", h=2)
        VM = XF[:, 2560:4608].rearrange("p (b h j v) -> p b h j v", b=2, h=2, j=4)
        BUFL = LNF[:, 0:1280].rearrange("p (h t) -> p h t", h=2)
        SC = GR[:, 0:1024].rearrange("p (d b h t) -> p d b h t", d=2, b=2, h=2)
        KTT = GR[:, 1024:1536].rearrange("p (b c) -> p b c", b=2)
        ST = OTF[:, 0:1536].rearrange("p (b h n v) -> p b h n v", b=2, h=2, n=3)
        CAR = OTF[:, 1536:2304].rearrange("p (b h v) -> p b h v", b=3, h=2)
        S0B = OTF[:, 2304:2560].rearrange("p (h v) -> p h v", h=2)

        G1 = GR[:, :].rearrange("p (g d) -> p g d", g=2)
        R3, R4, R5 = [z(2048 * i, 2048).rearrange("p (g d) -> p g d", g=2) for i in range(3)]
        ROWS = {2: G1, 3: R3, 4: R4, 5: R5}
        ZT = z(6144, 2048).rearrange("p (b d) -> p b d", b=2)
        HB = z(8192, 2048).rearrange("p (b d) -> p b d", b=2)
        SG = z(8192, 256).rearrange("p (b f) -> p b f", b=2)
        HID = z(8448, 256).rearrange("p (b f) -> p b f", b=2)
        HIDT = z(8704, 256).rearrange("p (b f) -> p b f", b=2)
        XG = z(10240, 2048).rearrange("p (b d) -> p b d", b=2)
        XGT = z(12288, 2048).rearrange("p (b d) -> p b d", b=2)
        SHOT = z(14336, 640).bitcast(bf16).rearrange("p (b t s) -> p b t s", b=2, t=NT)
        IOT = z(14976, 128)
        CM = z(15104, 160).rearrange("p (t e) -> p t e", t=NT)
        TIF = z(15264, 64).rearrange("p (b e) -> p b e", b=2)
        LG = OTF[:, 0:180].rearrange("p (t c) -> p t c", t=NT)
        RT = OTF[:, 4096:5056].rearrange("p (a c) -> p a c", a=6)
        YB = OTF[:, 0:4096].rearrange("p (b k d) -> p b k d", b=2, k=2)

        BG = z(0, 2560).rearrange("p (j t) -> p j t", j=4)
        CXP = z(2560, 4 * CXW).rearrange("p (j t) -> p j t", j=4)
        UP = z(5300, 4 * CXW).rearrange("p (j t) -> p j t", j=4)
        CO = z(8040, 4 * COW).rearrange("p (j t) -> p j t", j=4)
        SQ = z(10664, 4 * COW).rearrange("p (j t) -> p j t", j=4)
        RST = z(13288, COW)

        def state_before(i, n, step, hh):
            if step:
                return ST[:, i % 2, hh, step - 1, :]
            if n == 0:
                return S0B[:, hh, :]
            return ZERO[:, :] if n == 4 else CAR[:, (i - 1) % 3, hh, :]

        def slot3(s):
            return W[:, 4096 * s:4096 * (s + 1)]

        def col_chunk(w, a, b):
            return w.rearrange("(k p) n -> p k n", p=128)[:, :, a:b]

        WITEM = {}
        items = []

        def item(name, last, parts):
            s = len(items) % 3
            before = WITEM[items[-3]]["value"] if len(items) >= 3 else 0
            WITEM[name] = {"slot": s, "value": before + 16 * len(parts), "parts": parts, "last": last}
            items.append(name)

        def mod_item(l, c):
            s = len(items) % 3
            item(("mod", l, c), ("mod", l, c),
                 [(slot3(s).rearrange("p (k n) -> p k n", k=8), col_chunk(A["mod_w"][l], c * 512, c * 512 + 512)),
                  (MB[s], A["mod_b"][l, c * 512:c * 512 + 512].partition_broadcast(2))])

        def proj_item(name, last, w, a, b):
            s = len(items) % 3
            n = b - a
            item(name, last, [(slot3(s)[:, 0:8 * n].rearrange("p (k n) -> p k n", k=8), col_chunk(w, a, b))])

        for c in range(4):
            mod_item(0, c)
        w_in = A["ab_w_in"][0]
        proj_item(("cqa",), ("cq", 4), w_in, 2560, 3072)
        proj_item(("cqb",), ("cq", 4), w_in, 3072, AB_IN)
        s_ = len(items) % 3
        item(("uq",), ("q", 7), [(slot3(s_)[:, 0:2304].rearrange("p (k n) -> p k n", k=3),
                                 A["mla_w_uq"][0].rearrange("(k p) n -> p k n", p=128))])
        s_ = len(items) % 3
        item(("ukv",), ("k", 7), [(slot3(s_)[:, 0:2048].rearrange("p (k n) -> p k n", k=2),
                                  A["mla_w_ukv"][0].rearrange("(k p) n -> p k n", p=128))])
        for c in range(3):
            proj_item(("hq", c), ("hq", c, 3), w_in, c * 512, c * 512 + 512)
        for c in range(2):
            proj_item(("hv", c), ("hv", c, 4), w_in, 1536 + c * 512, 2048 + c * 512)
        for c in range(4, 12):
            mod_item(0, c)
        for c in range(2):
            proj_item(("wo", 0, c), ("y", 0, 4), A["ab_w_out"][0], c * 512, c * 512 + 512)
        N_ITEMS0 = len(items)
        for c in range(4):
            mod_item(1, c)
        for c in range(5):
            proj_item(("cd", c), ("cd", c, 3), A["cd_w_in"][0], c * 512, c * 512 + 512)
        for c in range(4, 12):
            mod_item(1, c)
        for c in range(2):
            proj_item(("wo", 1, c), ("y", 1, 4), A["cd_w_out"][0], c * 512, c * 512 + 512)

        def weights(pe, *name):
            it = WITEM[name]
            pe.wait_ge(w_full[it["slot"]], it["value"])
            return slot3(it["slot"])

        U = 8
        NI = NE // U
        EW = 3072

        def expert_gu(s):
            return W[:, EW * s:EW * s + 2048].rearrange("p (k f) -> p k f", k=8)

        def expert_down(s):
            return W[:, EW * s + 2048:EW * (s + 1)]

        block = ctx.enter_context(nc.Block())

        @block.sync
        def _(sp):
            sp.dma_start(C[:, :], A["consts"]).then_inc(d_const, 16)
            xs = A["x_sample"][0].rearrange("(t p) d -> p t d", p=128)

            def load_item(n):
                it = WITEM[items[n]]
                if n >= 3 and n not in (N_ITEMS0, N_ITEMS0 + 1, N_ITEMS0 + 2):
                    last = WITEM[items[n - 3]]["last"]
                    (emptied if last[0] == "mod" else filled)(sp, *last)
                for p, (dst, src) in enumerate(it["parts"]):
                    if n < 2 and p == 1:
                        sp.wait_ge(d_const, 16)
                    sp.dma_start(dst, src).then_inc(w_full[it["slot"]], 16)

            def load_expert(l, e, s):
                m = MS[l]
                wg = A["moe_w_gate"][l].rearrange("e (k p) f -> e p k f", p=128)
                wu = A["moe_w_up"][l].rearrange("e (k p) f -> e p k f", p=128)
                if isinstance(e, int):
                    g, u, dn = wg[e], wu[e], A["moe_w_down"][l, e]
                else:
                    g = wg[bass.ds(e, 1)].rearrange("e p k f -> (e p) k f")
                    u = wu[bass.ds(e, 1)].rearrange("e p k f -> (e p) k f")
                    dn = A["moe_w_down"][l][bass.ds(e, 1)].rearrange("e f d -> (e f) d")
                sp.dma_start(expert_gu(s)[:, :, 0:FF], g).then_inc(m[f"w{s}"], 16)
                sp.dma_start(expert_gu(s)[:, :, FF:2 * FF], u).then_inc(m[f"w{s}"], 16)
                sp.dma_start(expert_down(s), dn).then_inc(m[f"w{s}"], 16)

            for l in range(2):
                m = MS[l]
                lo, hi = (0, N_ITEMS0) if l == 0 else (N_ITEMS0, len(items))
                if l == 1:
                    sp.wait_ge(moe_done, 1)
                for n in range(lo, hi):
                    load_item(n)
                    if n == 2:
                        sp.dma_start(X[:, 0:4, :], xs).then_inc(d_x, 16)
                        sp.dma_start(X[:, 4, :], A["x_prompt"][0]).then_inc(d_x, 16)
                for n in range(hi - 3, hi):
                    filled(sp, *WITEM[items[n]]["last"])
                for e in range(4):
                    load_expert(l, e, e)
                sp.wait_ge(rt_ready, l + 1)
                R = sp.value_load(RI[0:1, 0:1], min_val=1, max_val=5)
                for u in range(4, U):
                    sp.wait_ge(m["down"], u - 3)
                    load_expert(l, u, u % 4)
                with sp.Fori(1, NI) as i:
                    for u in range(U):
                        sp.wait_ge(m["down"], i * U + (u - 3))
                        load_expert(l, i * U + u, u % 4)
                with sp.If(R > 1):
                    with sp.Fori(1, R) as r:
                        with sp.Fori(0, NI) as i:
                            for u in range(U):
                                sp.wait_ge(m["down"], r * NE + i * U + (u - 3))
                                load_expert(l, i * U + u, u % 4)
            for t in range(NT):
                sp.wait_ge(x_ready, 15 + t + 1)
                dst = O["y_sample"][0, t * 128:(t + 1) * 128, :] if t < 4 else O["y_prompt"][0]
                sp.dma_start(dst, X[:, t, :]).then_inc(d_out, 16)
            sp.wait_ge(d_out, 16 * NT)

        @block.gpsimd
        def _(pool):
            steps = [0]

            def chain(ins):
                steps[0] += 1
                ins.then_inc(pool_step, 1)
                pool.wait_ge(pool_step, steps[0])

            pool.dma_start(V1[0:8, :], A["c"][0].rearrange("(k p) -> k p", p=128)).then_inc(d_vec, 16)
            pool.dma_start(V1[8:16, :], A["c_ctx"].rearrange("(k p) -> k p", p=128)).then_inc(d_vec, 16)
            pool.dma_start(V2[0:16, :], A["hgrn_lb_logits"].rearrange("r d (h p) -> (r d h) p", p=128)).then_inc(d_vec, 16)
            pool.dma_start(V2[16:19, :], A["mla_q_norm_g"][0].rearrange("(k p) -> k p", p=128)).then_inc(d_vec, 16)
            pool.dma_start(V2[19:23, :], A["cf_conv_b"][0].rearrange("(k p) -> k p", p=128)).then_inc(d_vec, 16)
            pool.dma_start(V2[23:27, :], A["cf_ln_g"][0].rearrange("(k p) -> k p", p=128)).then_inc(d_vec, 16)
            pool.dma_start(V2[27:31, :], A["cf_ln_b"][0].rearrange("(k p) -> k p", p=128)).then_inc(d_vec, 16)
            pool.dma_start(V2[31:43, :], A["sc_conv_w"][0].rearrange("t (k p) -> (t k) p", p=128)).then_inc(d_vec, 16)
            pool.dma_start(V3[:, :], A["cf_conv_w"][0].rearrange("t (k p) -> (t k) p", p=128)).then_inc(d_vec, 16)
            pool.dma_start(CKG[:, :], A["mla_kv_norm_g"][0].partition_broadcast(128)).then_inc(d_rows, 16)
            pool.dma_start(HNG[:, :], A["hgrn_norm_g"][0].partition_broadcast(128)).then_inc(d_rows, 16)
            pool.dma_start(CC[:, 0:KVR], A["cache_mla_ckv"][0, 0]).then_inc(d_cache, 16)
            pool.dma_start(CC[:, KVR:288], A["cache_mla_krope"][0, 0]).then_inc(d_cache, 16)

            pool.wait_ge(norm_ready, 1)
            pool.dma_start(O["new_ckv"][0, 0], CQ[:, 4, QR:QR + KVR]).then_inc(d_kv_out, 16)
            pool.dma_start(O["new_kr"][0, 0], CQ[:, 4, QR + KVR:672]).then_inc(d_kv_out, 16)

            filled(pool, "obT", 3)
            nc.gpsimd.memset(VM[:, :, :, :, :], 0.0).then_inc(h_zero, 1)
            nc.gpsimd.memset(SC[:, :, :, :, :], 0.0).then_inc(h_zero, 1)
            nc.gpsimd.memset(ZERO[:, :], 0.0).then_inc(h_zero, 1)
            pool.wait_ge(h_zero, 3)
            state_in = [A["state_hgrn_fwd"][0, 0], A["state_hgrn_bwd"][0, 0]]
            state_out = [O["new_sf"][0, 0], O["new_sb"][0, 0]]
            emptied(pool, "hv", 0, 4)
            for u in range(4):
                d, hp = u // 2, u % 2
                if u:
                    filled(pool, "ho", u - 1, 1)
                pool.dma_start(S0B[:, :, :], state_in[d][2 * hp:2 * hp + 2].rearrange("h k v -> k h v")).then_inc(h_s0, 16)
                for n in range(NT):
                    i = 5 * u + n
                    t = (n if d == 0 else 3 - n) if n < 4 else 4
                    if i >= 2:
                        filled(pool, "hd", *divmod(i - 2, 5))
                    for j in range(4):
                        r = slice(32 * j, 32 * j + 32)
                        src = HV[r, t, 256 * hp:256 * hp + 256].rearrange("p (h v) -> p h v", h=2)
                        nc.gpsimd.tensor_copy(VM[r, i % 2, :, j, :], src).then_inc(h_vm, 1)
                emptied(pool, "hd", u, 4)
                pool.dma_start(state_out[d][2 * hp:2 * hp + 2].rearrange("h k v -> k h v"),
                               CAR[:, (5 * u + 4) % 3, :, :]).then_inc(d_state, 16)
            filled(pool, "ho", 3, 4)
            pool.dma_start(X[:, 0:4, :], A["x_sample"][0].rearrange("(t p) d -> p t d", p=128)).then_inc(d_xr, 16)
            pool.dma_start(X[:, 4, :], A["x_prompt"][0]).then_inc(d_xr, 16)

            hst = 0
            for l in range(2):
                m = MS[l]
                for k in range(2):
                    if k == 0:
                        if l == 0:
                            filled(pool, "oaT", 3)
                        else:
                            pool.wait_ge(x_ready, 10)
                        pool.dma_start(LNR[:, 0, :], A["ln_g"][l, 0].partition_broadcast(128)).then_inc(d_ln, 16)
                        pool.dma_start(LNR[:, 1, :], A["ln_b"][l, 0].partition_broadcast(128)).then_inc(d_ln, 16)
                        pool.dma_start(WR[:, :, 0:4], A["moe_w_group"][l].rearrange("(k p) n -> p k n", p=128)).then_inc(d_wr, 16)
                        pool.dma_start(WR[:, :, 4:36], A["moe_w_expert"][l].rearrange("(k p) n -> p k n", p=128)).then_inc(d_wr, 16)
                        for t in range(NT):
                            pool.wait_ge(h_ready, 5 * l + t + 1)
                            pool.dma_start(HD[t * 128:(t + 1) * 128, :], HB[:, t % 2, :]).then_inc(d_hst[t % 2], 16)
                        pool.wait_ge(x_ready, 10 * l + 5)
                        pool.dma_start(LNR[:, 0, :], A["ln_g"][l, 1].partition_broadcast(128)).then_inc(m["s0"], 16)
                        pool.dma_start(LNR[:, 1, :], A["ln_b"][l, 1].partition_broadcast(128)).then_inc(m["s1"], 16)
                pool.wait_ge(d_hst[0], 16 * 3 * (l + 1))
                pool.wait_ge(d_hst[1], 16 * 2 * (l + 1))
                pool.wait_ge(rt_ready, l + 1)
                R = pool.value_load(RI[0:1, 0:1], min_val=1, max_val=5)

                def gather(e, par, cnt, landed=None):
                    if landed is not None:
                        pool.wait_ge(m[f"g{par}"], landed)
                        pool.sem_inc(m["pool_passed"], 1)
                    nc.gpsimd.tensor_copy(IXG[:, par:par + 1], TI[:, bass.ds(e, 1)]).then_inc(m["s_ix"], 1)
                    pool.wait_ge(m["s_ix"], 1 + cnt)
                    pool.sem_inc(m["pool_passed"], 1)
                    nc.gpsimd.indirect_dma_start(
                        out=XG[:, par, :], out_offset=None, in_=HD[:, :],
                        in_offset=bass.IndirectOffsetOnAxis(ap=IXG[:, par:par + 1], axis=0),
                        bounds_check=NTOK - 1, oob_is_err=False).then_inc(m[f"g{par}"], 16)

                pool.sem_inc(m["s_ix"], 1)
                with pool.Fori(0, R) as r:
                    pool.wait_ge(m["table"], r * 7 + 7)
                    pool.sem_inc(m["pool_passed"], 1)
                    for e in range(2):
                        gather(e, e, r * 66 + (e + 1))
                    with pool.Fori(0, NI) as i:
                        for u in range(U):
                            n = u
                            par = u % 2
                            pool.wait_ge(m["t"], r * NE + i * U + (u + 1))
                            base = r * 66 + i * (2 * U)
                            gather(i * U + (u + 2), par, base + (2 + 2 * u + 1), r * 272 + i * 64 + 16 * ((u + 2) // 2))
                            pool.wait_ge(m["ya"], 1 + r * NE + i * U + (u + 1))
                            pool.wait_ge(m["yv"], 1 + r * NE + i * U + (u + 1))
                            pool.wait_ge(m[f"s{par}"], 16 + r * 256 + i * 64 + 16 * (u // 2))
                            pool.sem_inc(m["pool_passed"], 1)
                            nc.gpsimd.tensor_copy(IXY[:, par:par + 1], TY[:, bass.ds(i * U + u, 1)]).then_inc(m["s_ix"], 1)
                            pool.wait_ge(m["s_ix"], 1 + base + (2 + 2 * u + 2))
                            pool.sem_inc(m["pool_passed"], 1)
                            nc.gpsimd.indirect_dma_start(
                                out=YD[:, :], out_offset=bass.IndirectOffsetOnAxis(ap=IXY[:, par:par + 1], axis=0),
                                in_=ZT[:, par, :], in_offset=None,
                                bounds_check=2 * NTOK - 1, oob_is_err=False).then_inc(m[f"s{par}"], 16)
                    for par in range(2):
                        pool.wait_ge(m[f"g{par}"], r * 272 + 272)
                        pool.sem_inc(m["pool_passed"], 1)
                pool.wait_ge(m["s0"], 16 + R * (16 * NE // 2))
                pool.wait_ge(m["s1"], 16 + R * (16 * NE // 2))
                pool.sem_inc(moe_done, 1)
                for t in range(NT):
                    if t >= 2:
                        pool.wait_ge(y_used, 5 * l + t - 1)
                    for k in range(2):
                        pool.dma_start(YB[:, t % 2, k, :],
                                       YD[k * NTOK + t * 128:k * NTOK + (t + 1) * 128, :]).then_inc(d_yl[t % 2], 16)
            pool.wait_ge(d_kv_out, 32)
            pool.wait_ge(d_state, 64)

        @block.scalar
        def _(act):
            steps = [0]

            def chain(ins):
                steps[0] += 1
                ins.then_inc(act_step, 1)
                act.wait_ge(act_step, steps[0])

            A_ = nc.scalar.activation

            def mod_evac(l, c):
                if c < 4:
                    return
                filled(act, "modb", l, c)
                idx, half = c // 2, c % 2
                dst = ROWS[idx][:, :, half * 512:half * 512 + 512]
                src = ps("modb", l, c).rearrange("p (g n) -> p g n", g=2)
                if idx == 4:
                    release(nc.scalar.add(dst, src, 1.0), "modb", l, c)
                else:
                    release(A_(dst, src, ACT.Copy), "modb", l, c)

            def h_evac(l):
                for c in range(4):
                    emptied(act, "modb", l, c)
                for k in range(0, KD, 2):
                    filled(act, "xT", l, k)
                    A_(HT[:, k, 0:512], ps("xT", l, k)[:, 0:512], ACT.Identity,
                       bias=MC[:, 0, k, 0:1], scale=MC[:, 1, k, 0:1])
                    release(A_(HT[:, k, 512:640], ps("xT", l, k)[:, 512:640], ACT.Identity,
                               bias=MC[:, 0, k, 1:2], scale=MC[:, 1, k, 1:2]), "xT", l, k)

            act.wait_ge(d_vec, 16 * 9)
            A_(V1[:, :], V1[:, :], ACT.Silu).then_inc(c_silu, 1)
            act.wait_ge(lb_exp_in, 1)
            A_(LBS[:, 0:2, :], LBS[:, 0:2, :], ACT.Exp).then_inc(lb_exp, 1)

            h_evac(0)
            for t in range(NT):
                filled(act, "cq", t)
                release(A_(CQ[:, t, :], ps("cq", t)[:, 0:672], ACT.Copy), "cq", t)
            for t in range(NT):
                emptied(act, "cq", t)
                A_(z(6816 + 640 * t, QR), CQ[:, t, 0:QR], ACT.Square, accum_out=SS[:, t, 0:1])
                A_(z(6816 + 640 * t + QR, KVR), CQ[:, t, QR:QR + KVR], ACT.Square, accum_out=SS[:, t, 1:2]).then_inc(sq_ready, 1)
            act.wait_ge(rms_in, 1)
            A_(RR[:, :, :], RR[:, :, :], ACT.Sqrt).then_inc(rms_sd, 1)
            for r in range(2):
                filled(act, "ckvT", r)
                release(A_(CKVT[:, r, :], ps("ckvT", r)[:, 0:768], ACT.Copy), "ckvT", r)
            for t in range(6):
                filled(act, "v", t)
                release(A_(VT[:, t, :], ps("v", t)[:, 0:512], ACT.Copy), "v", t)

            def kq_evac(h):
                b = h % 2
                filled(act, "k", h)
                release(A_(KT[0:64, b, :], ps("k", h)[0:64, 0:768], ACT.Copy), "k", h)
                filled(act, "q", h)
                ins = A_(QT[0:96, b, :], ps("q", h)[0:96, 0:640], ACT.Copy)
                release(ins, "q", h)

            kq_evac(0)
            n = 0
            for h in range(MH):
                for t in range(NT):
                    nk = 640 if t < 4 else 128
                    b = n % 2
                    if h + 1 < MH and t == 1:
                        kq_evac(h + 1)
                    act.wait_ge(max_ready, n + 1)
                    if n >= 2:
                        filled(act, "pt", *divmod(n - 2, NT))
                        emptied(act, "o", *divmod(n - 2, NT))
                    release(A_(PB[:, b, 0:nk], ps("s", h, t)[:, 0:nk], ACT.Exp, bias=MXS[:, b, 1:2], scale=SCALE,
                               accum_out=SUM[:, b, 0:1]), "s", h, t)
                    filled(act, "pt", h, t)
                    release(A_(PTS[:, b, 0:nk], ps("pt", h, t)[:, 0:nk], ACT.Copy), "pt", h, t)
                    n += 1
            for j in range(4):
                filled(act, "obT", j)
                release(A_(OT[:, 4 + j, :], ps("obT", j)[:, 0:640], ACT.Copy), "obT", j)

            act.wait_ge(d_kv_out, 32)
            for c in range(3):
                for j in range(4):
                    filled(act, "hq", c, j)
                    dst = [HQ, HF[0], HF[1]][c]
                    release(A_(dst[:, j, :], ps("hq", c, j)[:, 0:640], ACT.Silu if c == 0 else ACT.Sigmoid), "hq", c, j)
            for t in range(NT):
                filled(act, "hv", 1, t)
                ins = A_(HG[:, t, :], ps("hv", 1, t)[:, 0:512], ACT.Silu)
                release(ins, "hv", 1, t)
            for u in range(4):
                d, hp = u // 2, u % 2
                act.wait_ge(h_f, u + 1)
                A_(BUFL[:, :, :], HF[d][:, 2 * hp:2 * hp + 2, :], ACT.Ln).then_inc(h_l, 1)
                act.wait_ge(h_arg, u + 1)
                if u:
                    filled(act, "ho", u - 1, 4)
                mid, full = (BUFA, BUFB) if d == 0 else (BUFB, BUFA)
                A_(QHAT[:, :, :], mid[:, :, :], ACT.Exp).then_inc(h_exp, 1)
                A_(KHAT[:, :, :], mid[:, :, :], ACT.Exp, scale=-1.0).then_inc(h_exp, 1)
                A_(KTIL[:, :, :], BUFL[:, :, :], ACT.Exp).then_inc(h_exp, 1)
                A_(QTIL[:, :, :], full[:, :, :], ACT.Exp).then_inc(h_exp, 1)
                e = CH - 1 if d == 0 else 0
                A_(DEC[:, :, :], full[:, :, :].rearrange("p h (c s) -> p h c s", s=CH)[:, :, :, e], ACT.Exp).then_inc(h_exp, 1)
                for n in range(NT):
                    i = 5 * u + n
                    t = (n if d == 0 else 3 - n) if n < 4 else 4
                    filled(act, "hk", u, n)
                    if i >= 2:
                        filled(act, "hd", *divmod(i - 2, 5))
                    release(A_(KTT[:, i % 2, :], ps("hk", u, n)[:, 0:256], ACT.Copy), "hk", u, n)
                    if d == 0 and n >= 1:
                        tt = n - 1
                        filled(act, "ho", u, tt)
                        release(A_(HO[:, tt, 256 * hp:256 * hp + 256], ps("ho", u, tt)[:, 0:256], ACT.Copy), "ho", u, tt)
                if d == 0:
                    filled(act, "ho", u, 4)
                    release(A_(HO[:, 4, 256 * hp:256 * hp + 256], ps("ho", u, 4)[:, 0:256], ACT.Copy), "ho", u, 4)
            act.wait_ge(o_var, 1)
            A_(HSS[:, :], HSS[:, :], ACT.Sqrt).then_inc(o_sd, 1)
            act.wait_ge(d_state, 64)
            for j in range(4):
                filled(act, "oaT", j)
                release(A_(OT[:, j, :], ps("oaT", j)[:, 0:640], ACT.Copy), "oaT", j)

            def ln_sqrt(q):
                act.wait_ge(ln_var, q + 1)
                A_(RSD[:, q % 2, 0:1], RSD[:, q % 2, 0:1], ACT.Sqrt).then_inc(ln_sd, 1)

            for l in range(2):
                m = MS[l]
                if l == 1:
                    h_evac(1)
                    for c, f in ((0, ACT.Copy), (1, ACT.Copy), (3, ACT.Copy), (4, ACT.Sigmoid)):
                        if c == 1:
                            act.wait_ge(cd_pad, 2)
                        for j in range(4):
                            filled(act, "cd", c, j)
                            src = ps("cd", c, j)
                            if c == 0:
                                release(A_(BG[:, j, :], src[:, 0:640], f), "cd", c, j)
                            elif c == 4:
                                ins = A_(CO[:, j, 0:640], src[:, 0:640], f)
                                release(ins, "cd", c, j)
                            else:
                                dst = CXP if c == 1 else UP
                                A_(dst[:, j, 15:527], src[:, 0:512], f)
                                release(A_(dst[:, j, 542:670], src[:, 512:640], f), "cd", c, j)
                    emptied(act, "mean")
                    A_(SQ[:, :, :], CO[:, :, :], ACT.Square).then_inc(cd_sq, 1)
                    emptied(act, "var")
                    A_(RST[:, :], RST[:, :], ACT.Sqrt).then_inc(cd_sd, 1)
                    for j in range(4):
                        act.wait_ge(cd_u, j + 1)
                        A_(OT[:, 4 + j, 0:512], CO[:, j, 0:512], ACT.Silu, bias=VC[:, 27 + j:28 + j], scale=VC[:, 23 + j:24 + j])
                        A_(OT[:, 4 + j, 512:640], CO[:, j, 527:655], ACT.Silu, bias=VC[:, 27 + j:28 + j],
                           scale=VC[:, 23 + j:24 + j]).then_inc(cd_out, 1)
                for c in range(4, 12):
                    mod_evac(l, c)
                for t in range(NT + 2):
                    if t < NT:
                        ln_sqrt(10 * l + t)
                    if t < 2:
                        continue
                    t -= 2
                    filled(act, "hT", l, t)
                    release(A_(HT[:, :, t * 128:(t + 1) * 128],
                               ps("hT", l, t).rearrange("p (k c) -> p k c", k=8), ACT.Copy), "hT", l, t)
                act.wait_ge(rt_exp_in, 2 * l + 1)
                A_(RT[:, 0, 0:20], RT[:, 0, 0:20], ACT.Exp).then_inc(rt_exp, 1)
                act.wait_ge(rt_exp_in, 2 * l + 2)
                A_(RS[:, 5, 0:5], RS[:, 5, 0:5], ACT.Exp).then_inc(rt_exp, 1)
                act.wait_ge(rt_ready, l + 1)
                R = act.value_load(RI[0:1, 0:1], min_val=1, max_val=5)
                for name in ('xa', 'ya'):
                    act.sem_inc(m[name], 1)
                with act.Fori(0, R) as r:
                    with act.Fori(0, NI) as i:
                        n0 = r * NE + i * U

                        def out_half(u):
                            act.wait_ge(m["down"], n0 + (u + 1))
                            act.wait_ge(m[f"s{u % 2}"], 16 + r * 256 + i * 64 + 16 * (u // 2))
                            A_(ZT[:, u % 2, 0:512], bank(6), ACT.Copy).then_inc(m["ya"], 1)

                        for u in range(U):
                            act.wait_ge(m["t"], n0 + (u + 1))
                            if u >= 2:
                                act.wait_ge(m["gu"], n0 + (u - 1))
                            A_(XGT[:, u % 2, 0:512], bank(0), ACT.Copy).then_inc(m["xa"], 1)
                            if u >= 1:
                                out_half(u - 1)
                            act.wait_ge(m["gu"], n0 + (u + 1))
                            A_(SG[:, u % 2, :], bank(2 + u % 2)[:, 0:FF], ACT.Silu).then_inc(m["sg"], 1)
                        out_half(U - 1)
                for t in range(NT):
                    ln_sqrt(10 * l + 5 + t)

        @block.vector
        def _(dve):
            steps = [0]
            V = nc.vector

            def chain(ins):
                steps[0] += 1
                ins.then_inc(vec_step, 1)
                dve.wait_ge(vec_step, steps[0])

            def mod_row(l, c):
                filled(dve, "mod", l, c)
                s = WITEM[("mod", l, c)]["slot"]
                dve.wait_ge(w_full[s], WITEM[("mod", l, c)]["value"])
                k = 12 * l + c
                if c >= 2:
                    filled(dve, "modb", l, c - 2)
                release(V.tensor_tensor(MR[:, c % 2, :], ps("mod", l, c)[0:2, 0:512], MB[s], ALU.add), "mod", l, c)

            def h_evac(l):
                for k in range(1, KD, 2):
                    filled(dve, "xT", l, k)
                    for g, (a, b) in enumerate(((0, 512), (512, 640))):
                        ins = V.tensor_scalar(HT[:, k, a:b], ps("xT", l, k)[:, a:b], MC[:, 1, k, g:g + 1],
                                              MC[:, 0, k, g:g + 1], ALU.mult, ALU.add)
                    release(ins, "xT", l, k)

            def mods_cols(l):
                for c in range(4):
                    mod_row(l, c)
                    filled(dve, "modb", l, c)
                    i, half = c // 2, c % 2
                    src = ps("modb", l, c)[:, 0:8].rearrange("p (k g) -> p k g", g=2)
                    release(V.tensor_scalar(MC[:, i, 4 * half:4 * half + 4, :], src, float(i), None, ALU.add), "modb", l, c)
                    emptied(dve, "modb", l, c)

            filled(dve, "vec")
            chain(V.tensor_copy(CT[:, :], ps("vec")[:, 0:16]))
            chain(V.tensor_copy(VC[:, :], ps("vec")[:, 16:59]))
            ins = V.tensor_copy(CW[:, :], ps("vec")[:, 64:188])
            release(ins, "vec")
            chain(V.tensor_tensor(LBS[:, 2, :], VC[:, 0:8], VC[:, 8:16], ALU.max))
            chain(V.tensor_tensor(LBS[:, 0, :], VC[:, 0:8], LBS[:, 2, :], ALU.subtract))
            V.tensor_tensor(LBS[:, 1, :], VC[:, 8:16], LBS[:, 2, :], ALU.subtract).then_inc(lb_exp_in, 1)
            dve.wait_ge(lb_exp, 1)
            chain(V.tensor_tensor(LBS[:, 2, :], LBS[:, 0, :], LBS[:, 1, :], ALU.add))
            chain(V.reciprocal(LBS[:, 2, :], LBS[:, 2, :]))
            chain(V.tensor_tensor(LBT[:, 0, :], LBS[:, 0, :], LBS[:, 2, :], ALU.mult))
            chain(V.tensor_tensor(LBT[:, 1, :], LBS[:, 1, :], LBS[:, 2, :], ALU.mult))
            dve.wait_ge(d_const, 16)
            chain(V.tensor_copy(VAL[:, :, 0, :], const("pidx").unsqueeze(2).to_broadcast([128, NT, NE])))
            for t in range(NT):
                chain(V.memset(VAL[:, t, 1, :], 128.0 * t))
            chain(V.memset(VAL[:, :, 3, :], 1.0))
            chain(V.memset(TI[:, 32:34], int(NOROW)))
            mods_cols(0)
            h_evac(0)

            dve.wait_ge(sq_ready, NT)
            chain(V.tensor_scalar(RR[:, :, 0:1], SS[:, :, 0:1], 1.0 / QR, RMS_EPS, ALU.mult, ALU.add))
            V.tensor_scalar(RR[:, :, 1:2], SS[:, :, 1:2], 1.0 / KVR, RMS_EPS, ALU.mult, ALU.add).then_inc(rms_in, 1)
            dve.wait_ge(rms_sd, 1)
            chain(V.reciprocal(RR[:, :, :], RR[:, :, :]))
            dve.wait_ge(d_rows, 32)
            for t in (4, 0, 1, 2, 3):
                V.tensor_scalar(CQ[:, t, 0:QR], CQ[:, t, 0:QR], RR[:, t, 0:1], None, ALU.mult)
                V.scalar_tensor_tensor(out=CQ[:, t, QR:QR + KVR], in0=CQ[:, t, QR:QR + KVR], scalar=RR[:, t, 1:2],
                                       in1=CKG[:, :], op0=ALU.mult, op1=ALU.mult).then_inc(norm_ready, 1)
            for r in range(3):
                filled(dve, "cqT", r)
                release(V.tensor_scalar(CQT[:, r, :], ps("cqT", r)[:, 0:640], VC[:, 16 + r:17 + r], None, ALU.mult), "cqT", r)
            filled(dve, "krT")
            rp = slice(64, 96)
            chain(V.tensor_copy(KT[rp, 0, 512:768], ps("krT")[rp, 512:768]))
            chain(V.tensor_copy(KT[rp, 1, 512:768], ps("krT")[rp, 512:768]))
            release(V.tensor_copy(KRS[rp, :], ps("krT")[rp, 0:512]), "krT")
            emptied(dve, "krT")
            cosr, sinr = const("cos", rp), const("sin", rp)
            filled(dve, "krP")
            release(V.tensor_tensor(ROT1[rp, :], ps("krP")[rp, 0:512], sinr, ALU.mult), "krP")
            chain(V.tensor_tensor(ROT2[rp, :], KRS[rp, :], cosr, ALU.mult))
            emptied(dve, "krP")
            V.tensor_tensor(KT[rp, 0, 0:512], ROT1[rp, :], ROT2[rp, :], ALU.add).then_inc(kr_ready, 1)
            V.tensor_tensor(KT[rp, 1, 0:512], ROT1[rp, :], ROT2[rp, :], ALU.add).then_inc(kr_ready, 1)
            dve.wait_ge(kr_ready, 2)

            def rotate_q(h):
                b = h % 2
                filled(dve, "qP", h)
                release(V.tensor_tensor(ROT1[rp, :], ps("qP", h)[rp, 0:512], sinr, ALU.mult), "qP", h)
                emptied(dve, "q", h)
                chain(V.tensor_tensor(ROT2[rp, :], QT[rp, b, 0:512], cosr, ALU.mult))
                emptied(dve, "qP", h)
                V.tensor_tensor(QT[rp, b, 0:512], ROT1[rp, :], ROT2[rp, :], ALU.add).then_inc(q_rot, 1)
                dve.wait_ge(q_rot, h + 1)

            def attend_out(n):
                h, t = divmod(n, NT)
                b = n % 2
                filled(dve, "o", h, t)
                emptied(dve, "s", h, t)
                chain(V.reciprocal(SUM[:, b, 1:2], SUM[:, b, 0:1]))
                release(V.tensor_scalar(OB[:, t, h * 64:h * 64 + 64], ps("o", h, t)[:, 0:64], SUM[:, b, 1:2], None,
                                        ALU.mult), "o", h, t)

            rotate_q(0)
            n = 0
            for h in range(MH):
                for t in range(NT):
                    nk = 640 if t < 4 else 128
                    b = n % 2
                    filled(dve, "s", h, t)
                    if n >= 2:
                        emptied(dve, "s", *divmod(n - 2, NT))
                    chain(V.tensor_reduce(MXS[:, b, 0:1], ps("s", h, t)[:, 0:nk], AX.X, ALU.max, negate=True))
                    V.tensor_scalar(MXS[:, b, 1:2], MXS[:, b, 0:1], SCALE, None, ALU.mult).then_inc(max_ready, 1)
                    if n >= 1:
                        attend_out(n - 1)
                    if h + 1 < MH and t == 3:
                        rotate_q(h + 1)
                    n += 1
            attend_out(n - 1)

            for t in range(NT):
                filled(dve, "hv", 0, t)
                release(V.tensor_copy(HV[:, t, :], ps("hv", 0, t)[:, 0:512]), "hv", 0, t)
            dve.wait_ge(h_zero, 3)
            scan_mask = const("scan")
            for u in range(4):
                d, hp = u // 2, u % 2
                F = HF[d][:, 2 * hp:2 * hp + 2, :]
                emptied(dve, "hq", 1 + d, 2 * hp + 1)
                for hh in range(2):
                    hd = d * 4 + 2 * hp + hh
                    ins = V.tensor_scalar(F[:, hh, :], F[:, hh, :], LBT[:, 1, hd:hd + 1], LBT[:, 0, hd:hd + 1], ALU.mult, ALU.add)
                    if hh == 0:
                        chain(ins)
                ins.then_inc(h_f, 1)
                dve.wait_ge(h_l, u + 1)
                if u >= 2:
                    emptied(dve, "ho", u - 2, 4)
                chain(V.tensor_scalar(F, F, -1.0, 1.0, ALU.mult, ALU.add))
                for hh in range(2):
                    ins = V.tensor_tensor_scan(BUFB[:, hh, :], scan_mask, BUFL[:, hh, :], 0.0, ALU.mult, ALU.add)
                    chain(ins)
                B4 = BUFB[:, :, :].rearrange("p h (c s) -> p (h c) s", s=CH)
                A4 = BUFA[:, :, :].rearrange("p h (c s) -> p (h c) s", s=CH)
                L4 = BUFL[:, :, :].rearrange("p h (c s) -> p (h c) s", s=CH)
                if d == 0:
                    chain(V.tensor_tensor(A4, B4, B4[:, :, 15:16].to_broadcast([128, 40, CH]), ALU.subtract))
                    V.tensor_tensor(L4, B4[:, :, 31:32].to_broadcast([128, 40, CH]), B4, ALU.subtract).then_inc(h_arg, 1)
                else:
                    chain(V.tensor_tensor(L4, B4, L4, ALU.subtract))
                    chain(V.tensor_tensor(A4, B4[:, :, 31:32].to_broadcast([128, 40, CH]), L4, ALU.subtract))
                    V.tensor_tensor(B4, A4, A4[:, :, 16:17].to_broadcast([128, 40, CH]), ALU.subtract).then_inc(h_arg, 1)
                Q = HQ[:, 2 * hp:2 * hp + 2, :]
                for k, (dst, src) in enumerate(((QHAT, Q), (KHAT, F), (KTIL, F), (QTIL, Q))):
                    dve.wait_ge(h_exp, 5 * u + k + 1)
                    V.tensor_tensor(dst[:, :, :], dst[:, :, :], src, ALU.mult).then_inc(h_mul, 1)
                dve.wait_ge(h_exp, 5 * u + 5)
                dve.wait_ge(h_s0, 16 * (u + 1))

                def out_add(n):
                    t = (3 - n) if n < 4 else 4
                    filled(dve, "ho", u, n)
                    dst = HO[:, t, 256 * hp:256 * hp + 256]
                    release(V.tensor_tensor(dst, ps("ho", u, n)[:, 0:256], dst, ALU.add), "ho", u, n)
                mask = const("mask_f" if d == 0 else "mask_b").bitcast(i32).unsqueeze(1).to_broadcast([128, 2, 128])
                for n in range(NT):
                    i = 5 * u + n
                    t = (n if d == 0 else 3 - n) if n < 4 else 4
                    if i >= 2:
                        filled(dve, "ho", *divmod(i - 2, 5))
                    filled(dve, "hs", u, n)
                    release(V.copy_predicated(SC[:, d, i % 2, :, :], mask,
                                              ps("hs", u, n)[:, 0:256].rearrange("p (h t) -> p h t", h=2)), "hs", u, n)
                    filled(dve, "hd", u, n)
                    if i >= 3:
                        if n == 2 and u >= 1:
                            dve.wait_ge(d_state, 16 * u)
                    for step in range(4):
                        j = step if d == 0 else 3 - step
                        for hh in range(2):
                            prev = state_before(i, n, step, hh)
                            nxt = ST[:, i % 2, hh, step, :] if step < 3 else CAR[:, i % 3, hh, :]
                            ins = V.scalar_tensor_tensor(out=nxt, in0=prev, scalar=DEC[:, hh, t * 4 + j:t * 4 + j + 1],
                                                         in1=ps("hd", u, n)[:, hh * 512 + j * 128:hh * 512 + (j + 1) * 128],
                                                         op0=ALU.mult, op1=ALU.add)
                            if step == 3 and hh == 1:
                                release(ins, "hd", u, n)
                            elif hh == 1 or step == 3:
                                chain(ins)
                            else:
                                steps[0] += 1
                                ins.then_inc(vec_step, 1)
                    emptied(dve, "hd", u, n)
                    if d == 1 and n >= 1:
                        out_add(n - 1)
                if d == 1:
                    out_add(4)
            emptied(dve, "ho", 3, 4)
            for t in range(NT):
                emptied(dve, "hv", 1, t)
            SQB = HTF[:, 0:2560]
            HOF, HGF = z(12800, 2560), z(10240, 2560)
            chain(V.tensor_tensor(SQB, HOF, HOF, ALU.mult))
            chain(V.tensor_reduce(HSS[:, :], SQB.rearrange("p (g v) -> p g v", v=128), AX.X, ALU.add))
            V.tensor_scalar(HSS[:, :], HSS[:, :], 1.0 / DK, RMS_EPS, ALU.mult, ALU.add).then_inc(o_var, 1)
            HG3 = HGF.rearrange("p (g v) -> p g v", v=128)
            HO3 = HOF.rearrange("p (g v) -> p g v", v=128)
            chain(V.tensor_tensor(HG3, HG3, HNG[:, :].unsqueeze(1).to_broadcast([128, 20, 128]), ALU.mult))
            dve.wait_ge(o_sd, 1)
            chain(V.reciprocal(HSS[:, :], HSS[:, :]))
            chain(V.tensor_tensor(HO3, HO3, HSS[:, :].unsqueeze(2).to_broadcast([128, 20, 128]), ALU.mult))
            V.tensor_tensor(HOF, HOF, HGF, ALU.mult).then_inc(o_ready, 1)

            def ln_first(q):
                b = q % 2
                for s in range(2):
                    V.bn_stats(ST6[:, b, s, :], ZT[:, b, s * 512:s * 512 + 512]).then_inc(vec_step, 1)
                    steps[0] += 1
                dve.wait_ge(vec_step, steps[0])
                chain(V.bn_aggr(MV[:, b, :], ST6[:, b, :, :]))
                V.tensor_scalar(RSD[:, b, 0:1], MV[:, b, 1:2], LN_EPS, None, ALU.add).then_inc(ln_var, 1)

            def ln_second(q, t, k):
                b = q % 2
                dve.wait_ge(ln_sd, q + 1)
                chain(V.reciprocal(RSD[:, b, 1:2], RSD[:, b, 0:1]))
                chain(V.tensor_scalar(ZT[:, b, :], ZT[:, b, :], MV[:, b, 0:1], RSD[:, b, 1:2], ALU.subtract, ALU.mult))
                if k % 2 == 0:
                    dve.wait_ge(d_ln, 16 * (k + 2))
                chain(V.tensor_tensor(ZT[:, b, :], ZT[:, b, :], LNR[:, 0, :], ALU.mult))
                V.tensor_tensor(X[:, t, :], ZT[:, b, :], LNR[:, 1, :], ALU.add).then_inc(x_ready, 1)
                dve.wait_ge(x_ready, q + 1)

            def first_max(src, n, prio, out, tmp, mx):
                chain(V.tensor_reduce(mx, src, AX.X, ALU.max))
                mb = mx.unsqueeze(2).to_broadcast([128, NT, n])
                chain(V.tensor_tensor(out, src, mb, ALU.is_equal))
                chain(V.tensor_tensor(out, out, prio.unsqueeze(1).to_broadcast([128, NT, n]), ALU.mult))
                chain(V.tensor_reduce(tmp, out, AX.X, ALU.max))
                chain(V.tensor_tensor(out, out, tmp.unsqueeze(2).to_broadcast([128, NT, n]), ALU.is_equal))

            def gated_convolutions():
                segs = ((0, 15, 512), (512, 542, 128))
                for j in range(4):
                    emptied(dve, "cd", 1, j)
                    filled(dve, "cd", 2, j)
                    for t0, p0, w in segs:
                        ins = V.tensor_tensor(CXP[:, j, p0:p0 + w], ps("cd", 2, j)[:, t0:t0 + w], CXP[:, j, p0:p0 + w], ALU.mult)
                    release(ins, "cd", 2, j)
                emptied(dve, "cd", 2, 3)
                for k in range(SCK):
                    for j in range(4):
                        for t0, p0, w in segs:
                            src = CXP[:, j, p0 + k - 1:p0 + k - 1 + w]
                            tap = VC[:, 31 + 4 * k + j:32 + 4 * k + j]
                            dst = OT[:, j, t0:t0 + w]
                            if k == 0:
                                ins = V.tensor_scalar(dst, src, tap, None, ALU.mult)
                            else:
                                ins = V.scalar_tensor_tensor(out=dst, in0=src, scalar=tap, in1=dst, op0=ALU.mult, op1=ALU.add)
                    chain(ins)
                for j in range(4):
                    emptied(dve, "cd", 0, j)
                V.tensor_tensor(OT[:, 0:4, :], OT[:, 0:4, :], BG[:, :, :], ALU.mult).then_inc(cd_out_v, 1)
                for j in range(4):
                    emptied(dve, "cd", 4, j)
                    for t0, p0, w in segs:
                        ins = V.tensor_tensor(UP[:, j, p0:p0 + w], UP[:, j, p0:p0 + w], CO[:, j, t0:t0 + w], ALU.mult)
                chain(ins)
                V.memset(CO[:, :, 655:656], 0.0)
                for k in range(CFK):
                    for j in range(4):
                        src = UP[:, j, k:k + 655]
                        tap = CW[:, 4 * k + j:4 * k + j + 1]
                        dst = CO[:, j, 0:655]
                        if k == 0:
                            ins = V.tensor_scalar(dst, src, tap, VC[:, 19 + j:20 + j], ALU.mult, ALU.add)
                        else:
                            ins = V.scalar_tensor_tensor(out=dst, in0=src, scalar=tap, in1=dst, op0=ALU.mult, op1=ALU.add)
                    if k == CFK - 1:
                        ins.then_inc(cd_conv, 1)
                    else:
                        chain(ins)

                def two(ap):
                    return ap.rearrange("p (b c) -> p b c", b=2)
                filled(dve, "mean")
                mean = two(ps("mean"))[:, :, 0:328]
                dve.wait_ge(cd_conv, 1)
                for j in range(4):
                    ins = V.scalar_tensor_tensor(out=two(CO[:, j, :]), in0=mean, scalar=-1.0 / 512, in1=two(CO[:, j, :]),
                                                 op0=ALU.mult, op1=ALU.add)
                release(ins, "mean")
                emptied(dve, "mean")
                filled(dve, "var")
                release(V.tensor_scalar(two(RST), two(ps("var"))[:, :, 0:328], 1.0 / 512, LN_EPS, ALU.mult, ALU.add), "var")
                dve.wait_ge(cd_sd, 1)
                chain(V.reciprocal(RST, RST))
                for j in range(4):
                    V.tensor_tensor(CO[:, j, :], CO[:, j, :], RST, ALU.mult).then_inc(cd_u, 1)

            for l in range(2):
                m = MS[l]
                if l == 1:
                    V.memset(CXP[:, :, :], 0.0).then_inc(cd_pad, 1)
                    V.memset(UP[:, :, :], 0.0).then_inc(cd_pad, 1)
                    mods_cols(1)
                    h_evac(1)
                    gated_convolutions()
                for c in range(4, 12):
                    mod_row(l, c)
                if l == 0:
                    dve.wait_ge(d_xr, 32)
                for c in range(4, 12):
                    emptied(dve, "modb", l, c)

                def mod_for_experts(t):
                    b, g = t % 2, (0 if t < 4 else 1)
                    if t >= 2:
                        filled(dve, "hT", l, t - 2)
                        dve.wait_ge(d_hst[b], 16 * ((3 if b == 0 else 2) * l + (t - 2) // 2 + 1))
                    chain(V.tensor_tensor(HB[:, b, :], X[:, t, :], R4[:, g, :], ALU.mult))
                    V.tensor_tensor(HB[:, b, :], HB[:, b, :], R3[:, g, :], ALU.add).then_inc(h_ready, 1)

                for t in range(NT):
                    q, g = 10 * l + t, (0 if t < 4 else 1)
                    b = q % 2
                    filled(dve, "y", l, t)
                    release(V.tensor_tensor(ZT[:, b, :], ps("y", l, t), G1[:, g, :], ALU.mult), "y", l, t)
                    emptied(dve, "y", l, t)
                    chain(V.scalar_tensor_tensor(out=ZT[:, b, :], in0=X[:, t, :], scalar=ALPHA, in1=ZT[:, b, :],
                                                 op0=ALU.mult, op1=ALU.add))
                    ln_first(q)
                    if t >= 1:
                        ln_second(q - 1, t - 1, 2 * l)
                        mod_for_experts(t - 1)
                ln_second(10 * l + 4, 4, 2 * l)
                mod_for_experts(4)

                filled(dve, "lg", l)
                release(V.tensor_copy(LG[:, :, :], ps("lg", l)[:, 0:180].rearrange("p (t c) -> p t c", t=NT)), "lg", l)
                emptied(dve, "lg", l)
                gl, el = LG[:, :, 0:4], LG[:, :, 4:36]
                gm, tmp, m1, m2, sume, ex, pg = [RS[:, i, 0:5] for i in range(7)]
                first_max(gl, 4, const("prio4"), O4[:, :, :], tmp, gm)
                D4 = RT[:, 0, 0:20].rearrange("p (t g) -> p t g", t=NT)
                V.tensor_tensor(D4, gl, gm.unsqueeze(2).to_broadcast([128, NT, 4]), ALU.subtract).then_inc(rt_exp_in, 1)
                E4 = RT[:, 1, :].rearrange("p (t g e) -> p t g e", t=NT, g=4)
                o4b = O4[:, :, :].unsqueeze(3).to_broadcast([128, NT, 4, 8])
                chain(V.tensor_tensor(E4, el.rearrange("p t (g e) -> p t g e", g=4), o4b, ALU.mult))
                EI = RT[:, 2, 0:40].rearrange("p (t e) -> p t e", t=NT)
                chain(V.tensor_reduce(EI, RT[:, 1, :].rearrange("p (t g e) -> p t e g", t=NT, g=4), AX.X, ALU.add))
                O1 = RT[:, 2, 40:80].rearrange("p (t e) -> p t e", t=NT)
                O2 = RT[:, 2, 80:120].rearrange("p (t e) -> p t e", t=NT)
                first_max(EI, 8, const("prio8"), O1, tmp, m1)
                chain(V.scalar_tensor_tensor(out=RT[:, 2, 0:40], in0=RT[:, 2, 40:80], scalar=-3.0e38, in1=RT[:, 2, 0:40],
                                             op0=ALU.mult, op1=ALU.add))
                first_max(EI, 8, const("prio8"), O2, tmp, m2)
                V.tensor_tensor(ex, m2, m1, ALU.subtract).then_inc(rt_exp_in, 1)
                dve.wait_ge(rt_exp, 2 * l + 2)
                chain(V.tensor_reduce(sume, D4, AX.X, ALU.add))
                chain(V.tensor_scalar(pg, ex, 1.0, None, ALU.add))
                chain(V.tensor_tensor(pg, pg, sume, ALU.mult))
                chain(V.reciprocal(W12[:, 0, :], pg))
                chain(V.tensor_tensor(W12[:, 1, :], W12[:, 0, :], ex, ALU.mult))
                M1 = RT[:, 3, :].rearrange("p (t g e) -> p t g e", t=NT, g=4)
                M2 = RT[:, 4, :].rearrange("p (t g e) -> p t g e", t=NT, g=4)
                chain(V.tensor_tensor(M1, o4b, O1.unsqueeze(2).to_broadcast([128, NT, 4, 8]), ALU.mult))
                chain(V.tensor_tensor(M2, o4b, O2.unsqueeze(2).to_broadcast([128, NT, 4, 8]), ALU.mult))
                V.tensor_tensor(RT[:, 5, :], RT[:, 3, :], RT[:, 4, :], ALU.add).then_inc(rt_mask, 1)
                chain(V.tensor_scalar(VAL[:, :, 2, :], RT[:, 4, :].rearrange("p (t e) -> p t e", t=NT), float(NTOK), None, ALU.mult))
                filled(dve, "ct", l)
                chain(V.memset(RUN[:, :], 0.0))
                for t in range(NT):
                    chain(V.tensor_tensor(CM[:, t, :], ps("ct", l)[:, t * 32:t * 32 + 32], RUN[:, :], ALU.add))
                    ins = V.tensor_tensor(RUN[:, :], ps("ct", l)[:, 512 + t * 32:512 + t * 32 + 32], RUN[:, :], ALU.add)
                    if t == NT - 1:
                        release(ins, "ct", l)
                        emptied(dve, "ct", l)
                    else:
                        chain(ins)
                CMF = CM[:, :, :].rearrange("p t e -> p (t e)")
                chain(V.scalar_tensor_tensor(out=CMF, in0=CMF, scalar=1.0, in1=RT[:, 5, :], op0=ALU.add, op1=ALU.mult))
                chain(V.tensor_scalar(CMF, CMF, -1.0, None, ALU.add))
                chain(V.tensor_reduce(RS[:, 7, 0:1], RUN[:, :], AX.X, ALU.max))
                for k in range(1, NT):
                    chain(V.tensor_scalar(RS[:, 8, k - 1:k], RS[:, 7, 0:1], 128.0 * k, None, ALU.is_gt))
                chain(V.tensor_reduce(RS[:, 7, 1:2], RS[:, 8, 0:4], AX.X, ALU.add))
                V.tensor_scalar(RI[:, :], RS[:, 7, 1:2], 1.0, None, ALU.add).then_inc(rt_ready, 1)
                chain(V.tensor_copy(IOT[:, :], const("iota")))
                dve.wait_ge(rt_ready, l + 1)
                R = dve.value_load(RI[0:1, 0:1], min_val=1, max_val=5)

                for name in ('xv', 'yv'):
                    dve.sem_inc(m[name], 1)
                with dve.Fori(0, R) as r:
                    with dve.Fori(0, NE // 2) as i:
                        for u in range(2):
                            dve.wait_ge(m["mtab"], 1 + r * NE + i * 2)
                            V.tensor_tensor(SHOT[:, u, :, :], IOT[:, :].unsqueeze(1).to_broadcast([128, NT, 128]),
                                            CM[:, :, bass.ds(i * 2 + u, 1)].to_broadcast([128, NT, 128]),
                                            ALU.is_equal).then_inc(m["mask"], 1)
                    dve.wait_ge(m["mtab"], 1 + r * NE + NE)
                    T4 = bank(7)[:, 0:128].rearrange("p (e c) -> p e c", c=4)
                    dve.wait_ge(m["s_ix"], 1 + r * 66)
                    V.tensor_copy(TIF[:, 0, :], T4[:, :, 0]).then_inc(m["table"], 1)
                    dve.wait_ge(m["table"], r * 7 + 1)
                    V.tensor_tensor(TIF[:, 0, :], T4[:, :, 1], TIF[:, 0, :], ALU.add).then_inc(m["table"], 1)
                    V.tensor_scalar(TIF[:, 1, :], T4[:, :, 3], -NOROW, NOROW, ALU.mult, ALU.add).then_inc(m["table"], 1)
                    dve.wait_ge(m["table"], r * 7 + 3)
                    V.tensor_tensor(TIF[:, 0, :], TIF[:, 0, :], TIF[:, 1, :], ALU.add).then_inc(m["table"], 1)
                    dve.wait_ge(m["table"], r * 7 + 4)
                    V.tensor_copy(TI[:, 0:32], TIF[:, 0, :]).then_inc(m["table"], 1)
                    V.tensor_tensor(TY[:, 0:32], T4[:, :, 2], TIF[:, 0, :], ALU.add).then_inc(m["table"], 1)
                    V.tensor_scalar(IOT[:, :], IOT[:, :], 128.0, None, ALU.add).then_inc(m["table"], 1)
                    with dve.Fori(0, NI) as i:
                        n0 = r * NE + i * U

                        def down_in(u):
                            dve.wait_ge(m["ht"], n0 + (u + 1))
                            V.tensor_copy(HIDT[:, u % 2, :], bank(4 + u % 2)[:, 0:128]).then_inc(m["hidt"], 1)

                        def out_half(u):
                            dve.wait_ge(m["down"], n0 + (u + 1))
                            dve.wait_ge(m[f"s{u % 2}"], 16 + r * 256 + i * 64 + 16 * (u // 2))
                            V.tensor_copy(ZT[:, u % 2, 512:1024], bank(7)).then_inc(m["yv"], 1)

                        for u in range(U):
                            dve.wait_ge(m["t"], n0 + (u + 1))
                            if u >= 2:
                                dve.wait_ge(m["gu"], n0 + (u - 1))
                            V.tensor_copy(XGT[:, u % 2, 512:1024], bank(1)).then_inc(m["xv"], 1)
                            if u >= 1:
                                down_in(u - 1)
                                out_half(u - 1)
                            dve.wait_ge(m["sg"], n0 + (u + 1))
                            V.tensor_tensor(HID[:, u % 2, :], bank(2 + u % 2)[:, FF:2 * FF], SG[:, u % 2, :],
                                            ALU.mult).then_inc(m["hid"], 1)
                        down_in(U - 1)
                        out_half(U - 1)
                dve.wait_ge(moe_done, l + 1)
                for t in range(NT):
                    q, g = 10 * l + 5 + t, (0 if t < 4 else 1)
                    b, yb = q % 2, t % 2
                    cnt = ((3 if yb == 0 else 2) * l + t // 2 + 1) * 32
                    dve.wait_ge(d_yl[yb], cnt)
                    chain(V.tensor_scalar(YB[:, yb, 0, :], YB[:, yb, 0, :], W12[:, 0, t:t + 1], None, ALU.mult))
                    chain(V.scalar_tensor_tensor(out=YB[:, yb, 0, :], in0=YB[:, yb, 1, :], scalar=W12[:, 1, t:t + 1],
                                                 in1=YB[:, yb, 0, :], op0=ALU.mult, op1=ALU.add))
                    V.tensor_tensor(ZT[:, b, :], YB[:, yb, 0, :], R5[:, g, :], ALU.mult).then_inc(y_used, 1)
                    dve.wait_ge(y_used, 5 * l + t + 1)
                    chain(V.scalar_tensor_tensor(out=ZT[:, b, :], in0=X[:, t, :], scalar=ALPHA, in1=ZT[:, b, :],
                                                 op0=ALU.mult, op1=ALU.add))
                    ln_first(q)
                    if t >= 1:
                        ln_second(q - 1, t - 1, 2 * l + 1)
                ln_second(10 * l + 9, 4, 2 * l + 1)

        @block.tensor
        def _(pe):
            T = nc.tensor

            def mod(l, c):
                w = weights(pe, "mod", l, c).rearrange("p (k n) -> p k n", k=8)
                open_group(pe, "mod", l, c)
                for k in range(KD):
                    ins = T.matmul(ps("mod", l, c)[0:2, 0:512], CT[:, :].rearrange("p (g k) -> p k g", g=2)[:, k, :],
                                   w[:, k, :], start=(k == 0), stop=(k == KD - 1))
                close_group(ins, "mod", l, c)
                emptied(pe, "mod", l, c)
                open_group(pe, "modb", l, c)
                row = MR[:, c % 2, :]
                if c < 4:
                    for b in range(4):
                        ins = T.matmul(ps("modb", l, c)[:, 2 * b:2 * b + 2], row[:, b * 128:b * 128 + 128],
                                       C[0:2, 0:2], start=True, stop=True)
                else:
                    for g in range(2):
                        ins = T.matmul(ps("modb", l, c)[:, g * 512:g * 512 + 512], const(f"sel{g}", slice(0, 2)),
                                       row, start=True, stop=True)
                close_group(ins, "modb", l, c)

            def x_transposes(l):
                for k in range(KD):
                    open_group(pe, "xT", l, k)
                    for t in range(NT):
                        ins = T.transpose(ps("xT", l, k)[:, t * 128:t * 128 + 128], X[:, t, k * 128:k * 128 + 128], ident)
                    close_group(ins, "xT", l, k)
                for k in range(KD):
                    emptied(pe, "xT", l, k)

            def project_cm(name, w, col):
                open_group(pe, *name)
                for a, b in ((0, 512), (512, 640)):
                    for k in range(KD):
                        ins = T.matmul(ps(*name)[:, a:b], w[:, k, col:col + 128], HT[:, k, a:b],
                                       start=(k == 0), stop=(k == KD - 1))
                close_group(ins, *name)

            def project_tm(name, src, t, parts):
                open_group(pe, *name)
                for at, w in parts:
                    for k in range(KD):
                        ins = T.matmul(ps(*name)[:, at:at + w.shape[2]], src[:, k, t * 128:t * 128 + 128], w[:, k, :],
                                       start=(k == 0), stop=(k == KD - 1))
                close_group(ins, *name)

            def w8(words, n=512):
                return words[:, 0:8 * n].rearrange("p (k n) -> p k n", k=8)

            pe.wait_ge(d_const, 16)
            pe.wait_ge(d_vec, 16 * 9)
            pe.wait_ge(c_silu, 1)
            v = ps("vec")
            T.matmul(v[:, 0:16], V1[:, :], C[0:16, 0:16], start=True, stop=True)
            T.matmul(v[:, 16:59], V2[:, :], C[0:43, 0:43], start=True, stop=True)
            close_group(T.matmul(v[:, 64:188], V3[:, :], C[0:124, 0:124], start=True, stop=True), "vec")
            emptied(pe, "vec")
            for c in range(4):
                mod(0, c)
            pe.wait_ge(d_x, 32)
            x_transposes(0)

            wa, wb = w8(weights(pe, "cqa")), w8(weights(pe, "cqb"), AB_IN - 3072)
            for t in range(NT):
                project_tm(("cq", t), HT, t, [(0, wa), (512, wb)])
            pe.wait_ge(norm_ready, NT)
            pe.wait_ge(d_cache, 32)
            for r in range(3):
                open_group(pe, "cqT", r)
                for t in range(NT):
                    ins = T.transpose(ps("cqT", r)[:, t * 128:t * 128 + 128], CQ[:, t, r * 128:r * 128 + 128], ident)
                close_group(ins, "cqT", r)
            for r in range(2):
                open_group(pe, "ckvT", r)
                srcs = [CQ[:, t, QR + r * 128:QR + r * 128 + 128] for t in range(4)]
                srcs += [CC[:, r * 128:r * 128 + 128], CQ[:, 4, QR + r * 128:QR + r * 128 + 128]]
                for t, src in enumerate(srcs):
                    ins = T.transpose(ps("ckvT", r)[:, t * 128:t * 128 + 128], src, ident)
                close_group(ins, "ckvT", r)
            open_group(pe, "krT")
            srcs = [CQ[:, t, 640:672] for t in range(4)] + [CC[:, KVR:288], CQ[:, 4, 640:672]]
            for t, src in enumerate(srcs):
                ins = T.matmul(ps("krT")[64:96, t * 128:t * 128 + 128], src, ident, start=True, stop=True)
            close_group(ins, "krT")
            perm = const("perm", slice(64, 96))
            emptied(pe, "krT")
            open_group(pe, "krP")
            close_group(T.matmul(ps("krP")[64:96, 0:512], perm, KRS[64:96, :], start=True, stop=True), "krP")
            uq = weights(pe, "uq")[:, 0:2304].rearrange("p (k n) -> p k n", k=3)
            ukv = weights(pe, "ukv")[:, 0:2048].rearrange("p (k n) -> p k n", k=2)
            for r in range(2):
                emptied(pe, "ckvT", r)
            wv = ukv.rearrange("p k (h c) -> p k h c", h=8)[:, :, :, 64:128]
            for t in range(6):
                open_group(pe, "v", t)
                for r in range(2):
                    ins = T.matmul(ps("v", t)[:, 0:512].rearrange("p (h c) -> p h c", h=8),
                                   CKVT[:, r, t * 128:t * 128 + 128], wv[:, r], start=(r == 0), stop=(r == 1))
                close_group(ins, "v", t)
            for r in range(3):
                emptied(pe, "cqT", r)

            def keys_queries(h):
                open_group(pe, "k", h)
                for a, b in ((0, 512), (512, 768)):
                    for r in range(2):
                        ins = T.matmul(ps("k", h)[0:64, a:b], ukv[:, r, h * 128:h * 128 + 64], CKVT[:, r, a:b],
                                       start=(r == 0), stop=(r == 1))
                close_group(ins, "k", h)
                open_group(pe, "q", h)
                for a, b in ((0, 512), (512, 640)):
                    for r in range(3):
                        ins = T.matmul(ps("q", h)[0:96, a:b], uq[:, r, h * 96:h * 96 + 96], CQT[:, r, a:b],
                                       start=(r == 0), stop=(r == 2))
                close_group(ins, "q", h)

            def swap_pairs(h):
                emptied(pe, "q", h)
                open_group(pe, "qP", h)
                close_group(T.matmul(ps("qP", h)[64:96, 0:512], perm, QT[64:96, h % 2, 0:512], start=True, stop=True), "qP", h)

            def scores(h, t):
                if t == 0:
                    emptied(pe, "k", h)
                    pe.wait_ge(q_rot, h + 1)
                    pe.wait_ge(kr_ready, 2)
                open_group(pe, "s", h, t)
                q = QT[0:96, h % 2, t * 128:t * 128 + 128]
                for a, b in (((0, 512), (512, 640)) if t < 4 else ((0, 128),)):
                    ka = a if t < 4 else 640
                    ins = T.matmul(ps("s", h, t)[:, a:b], q, KT[0:96, h % 2, ka:ka + b - a], start=True, stop=True)
                close_group(ins, "s", h, t)

            for t in range(6):
                emptied(pe, "v", t)
            keys_queries(0)
            swap_pairs(0)
            steps = [(h, t) for h in range(MH) for t in range(NT)]
            scores(0, 0)
            for n, (h, t) in enumerate(steps):
                if h + 1 < MH and t == 0:
                    keys_queries(h + 1)
                if h + 1 < MH and t == 2:
                    swap_pairs(h + 1)
                if n + 1 < len(steps):
                    scores(*steps[n + 1])
                blocks = [0, 1, 2, 3, 4] if t < 4 else [5]
                emptied(pe, "s", h, t)
                open_group(pe, "pt", h, t)
                for j, kb in enumerate(blocks):
                    ins = T.transpose(ps("pt", h, t)[:, j * 128:j * 128 + 128], PB[:, n % 2, j * 128:j * 128 + 128], ident)
                close_group(ins, "pt", h, t)
                emptied(pe, "pt", h, t)
                open_group(pe, "o", h, t)
                for j, kb in enumerate(blocks):
                    ins = T.matmul(ps("o", h, t)[:, 0:64], PTS[:, n % 2, j * 128:j * 128 + 128], VT[:, kb, h * 64:h * 64 + 64],
                                   start=(j == 0), stop=(j == len(blocks) - 1))
                close_group(ins, "o", h, t)
            emptied(pe, "o", MH - 1, NT - 1)
            for j in range(4):
                open_group(pe, "obT", j)
                for t in range(NT):
                    ins = T.transpose(ps("obT", j)[:, t * 128:t * 128 + 128], OB[:, t, j * 128:j * 128 + 128], ident)
                close_group(ins, "obT", j)

            for c in range(3):
                w = w8(weights(pe, "hq", c))
                for j in range(4):
                    project_cm(("hq", c, j), w, j * 128)
            for c in range(2):
                w = w8(weights(pe, "hv", c))
                for t in range(NT):
                    project_tm(("hv", c, t), HT, t, [(0, w)])
            emptied(pe, "hv", 0, 4)
            for u in range(4):
                d, hp = u // 2, u % 2

                def tile_at(n):
                    return (n if d == 0 else 3 - n) if n < 4 else 4

                def intra(n):
                    i, t = 5 * u + n, tile_at(n)
                    tc = slice(t * 128, t * 128 + 128)
                    open_group(pe, "hs", u, n)
                    for hh in range(2):
                        ins = T.matmul(ps("hs", u, n)[:, hh * 128:hh * 128 + 128], KHAT[:, hh, tc], QHAT[:, hh, tc],
                                       start=True, stop=True)
                    close_group(ins, "hs", u, n)
                    open_group(pe, "hk", u, n)
                    for hh in range(2):
                        ins = T.transpose(ps("hk", u, n)[:, hh * 128:hh * 128 + 128], KTIL[:, hh, tc], ident)
                    close_group(ins, "hk", u, n)
                    emptied(pe, "hk", u, n)
                    pe.wait_ge(h_vm, 4 * (i + 1))
                    open_group(pe, "hd", u, n)
                    for hh in range(2):
                        ins = T.matmul(ps("hd", u, n)[:, hh * 512:hh * 512 + 512], KTT[:, i % 2, hh * 128:hh * 128 + 128],
                                       VM[:, i % 2, hh, :, :].rearrange("p j v -> p (j v)"), start=True, stop=True)
                    close_group(ins, "hd", u, n)

                pe.wait_ge(h_mul, 4 * (u + 1))
                intra(0)
                for n in range(NT):
                    if n + 1 < NT:
                        intra(n + 1)
                    i, t = 5 * u + n, tile_at(n)
                    emptied(pe, "hs", u, n)
                    emptied(pe, "hd", u, n)
                    open_group(pe, "ho", u, n)
                    for hh in range(2):
                        h = 2 * hp + hh
                        T.matmul(ps("ho", u, n)[:, hh * 128:hh * 128 + 128], SC[:, d, i % 2, hh, :],
                                 HV[:, t, h * 128:h * 128 + 128], start=True, stop=False, skip_group_check=True)
                        for step in range(4):
                            j = step if d == 0 else 3 - step
                            ins = T.matmul(ps("ho", u, n)[32 * j:32 * j + 32, hh * 128:hh * 128 + 128],
                                           QTIL[:, hh, t * 128 + 32 * j:t * 128 + 32 * j + 32], state_before(i, n, step, hh),
                                           start=False, stop=(step == 3), skip_group_check=True)
                    close_group(ins, "ho", u, n)
            pe.wait_ge(o_ready, 1)
            for j in range(4):
                open_group(pe, "oaT", j)
                for t in range(NT):
                    ins = T.transpose(ps("oaT", j)[:, t * 128:t * 128 + 128], HO[:, t, j * 128:j * 128 + 128], ident)
                close_group(ins, "oaT", j)

            for l in range(2):
                m = MS[l]
                if l == 1:
                    for c in range(4):
                        mod(1, c)
                    pe.wait_ge(x_ready, 10)
                    x_transposes(1)
                    for c in range(5):
                        w = w8(weights(pe, "cd", c))
                        for j in range(4):
                            project_cm(("cd", c, j), w, j * 128)
                    for name, src in (("mean", CO), ("var", SQ)):
                        pe.wait_ge(cd_conv if name == "mean" else cd_sq, 1)
                        open_group(pe, name)
                        for b in range(2):
                            for j in range(4):
                                ins = T.matmul(ps(name)[:, b * 512:b * 512 + 328], const("ones"), src[:, j, b * 328:b * 328 + 328],
                                               start=(j == 0), stop=(j == 3))
                        close_group(ins, name)
                for c in range(4, 12):
                    mod(l, c)
                if l == 0:
                    for j in range(4):
                        emptied(pe, "oaT", j)
                else:
                    pe.wait_ge(cd_out_v, 1)
                    pe.wait_ge(cd_out, 4)
                w0, w1 = w8(weights(pe, "wo", l, 0)), w8(weights(pe, "wo", l, 1))
                for t in range(NT):
                    project_tm(("y", l, t), OT, t, [(0, w0), (512, w1)])
                for t in range(NT):
                    pe.wait_ge(h_ready, 5 * l + t + 1)
                    open_group(pe, "hT", l, t)
                    for k in range(KD):
                        ins = T.transpose(ps("hT", l, t)[:, k * 128:k * 128 + 128], HB[:, t % 2, k * 128:k * 128 + 128], ident)
                    close_group(ins, "hT", l, t)
                pe.wait_ge(d_wr, 32 * (l + 1))
                open_group(pe, "lg", l)
                for t in range(NT):
                    emptied(pe, "hT", l, t)
                    for k in range(KD):
                        ins = T.matmul(ps("lg", l)[:, t * 36:t * 36 + 36], HT[:, k, t * 128:t * 128 + 128], WR[:, k, :],
                                       start=(k == 0), stop=(k == KD - 1))
                close_group(ins, "lg", l)
                pe.wait_ge(rt_mask, l + 1)
                open_group(pe, "ct", l)
                T.matmul(ps("ct", l)[:, 0:160], const("tri"), RT[:, 5, :], start=True, stop=True)
                close_group(T.matmul(ps("ct", l)[:, 512:672], const("ones"), RT[:, 5, :], start=True, stop=True), "ct", l)
                emptied(pe, "lg", l)
                emptied(pe, "ct", l)

                pe.wait_ge(rt_ready, l + 1)
                R = pe.value_load(RI[0:1, 0:1], min_val=1, max_val=5)
                for name in ('mtab',):
                    pe.sem_inc(m[name], 1)
                with pe.Fori(0, R) as r:
                    pe.wait_ge(m["yv"], 1 + r * NE)
                    pe.sem_inc(m["pe_passed"], 1)
                    with pe.Fori(0, NE // 2) as i:
                        for u in range(2):
                            pe.wait_ge(m["mask"], r * NE + i * 2 + (u + 1))
                            for t in range(NT):
                                ins = T.matmul(bank(7)[:, bass.ds((i * 2 + u) * 4, 4)], SHOT[:, u, t, :],
                                               VAL[:, t, :, bass.ds(i * 2 + u, 1)].rearrange("p c e -> p (c e)"),
                                               start=(t == 0), stop=(t == NT - 1))
                            ins.then_inc(m["mtab"], 1)
                    with pe.Fori(0, NI) as i:
                        n0 = r * NE + i * U

                        def transposes(u):
                            pe.wait_ge(m[f"g{u % 2}"], r * 272 + i * 64 + 16 * (u // 2 + 1))
                            pe.wait_ge(m["xa"], 1 + n0 + u)
                            pe.wait_ge(m["xv"], 1 + n0 + u)
                            for k in range(KD):
                                ins = T.transpose(bank(k // 4)[:, (k % 4) * 128:(k % 4) * 128 + 128],
                                                  XG[:, u % 2, k * 128:k * 128 + 128], ident)
                            ins.then_inc(m["t"], 1)

                        def gate_up(u):
                            pe.wait_ge(m[f"w{u % 4}"], r * 384 + i * 96 + 48 * (u // 4 + 1))
                            pe.wait_ge(m["xa"], 1 + n0 + (u + 1))
                            pe.wait_ge(m["xv"], 1 + n0 + (u + 1))
                            if u >= 2:
                                pe.wait_ge(m["hid"], n0 + (u - 1))
                            w = expert_gu(u % 4)
                            for k in range(KD):
                                ins = T.matmul(bank(2 + u % 2)[:, 0:256], XGT[:, u % 2, k * 128:k * 128 + 128], w[:, k, :],
                                               start=(k == 0), stop=(k == KD - 1))
                            ins.then_inc(m["gu"], 1)

                        def down(u):
                            pe.wait_ge(m["hid"], n0 + (u + 1))
                            T.transpose(bank(4 + u % 2)[:, 0:128], HID[:, u % 2, :], ident).then_inc(m["ht"], 1)
                            pe.wait_ge(m["hidt"], n0 + (u + 1))
                            pe.wait_ge(m["ya"], 1 + n0 + u)
                            pe.wait_ge(m["yv"], 1 + n0 + u)
                            w = expert_down(u % 4)
                            for b in range(2):
                                ins = T.matmul(bank(6 + b), HIDT[:, u % 2, :], w[:, b * 512:b * 512 + 512], start=True, stop=True)
                            ins.then_inc(m["down"], 1)

                        transposes(0)
                        gate_up(0)
                        for u in range(1, U):
                            transposes(u)
                            down(u - 1)
                            gate_up(u)
                        down(U - 1)
                pe.wait_ge(moe_done, l + 1)

    return nc


_INS = ['x_prompt', 'x_sample', 'state_hgrn_fwd', 'state_hgrn_bwd', 'cache_mla_ckv', 'cache_mla_krope', 'c', 'c_ctx',
        'mod_w', 'mod_b', 'ln_g', 'ln_b', 'ab_w_in', 'ab_w_out', 'hgrn_lb_logits', 'hgrn_norm_g', 'mla_q_norm_g',
        'mla_w_uq', 'mla_kv_norm_g', 'mla_w_ukv', 'cd_w_in', 'cd_w_out', 'sc_conv_w', 'cf_conv_w', 'cf_conv_b',
        'cf_ln_g', 'cf_ln_b', 'moe_w_group', 'moe_w_expert', 'moe_w_gate', 'moe_w_up', 'moe_w_down']
_OUTS = [("y_prompt", (1, 128, D)), ("y_sample", (1, 512, D)), ("new_sf", (1, 1, HA, DK, DK)), ("new_sb", (1, 1, HA, DK, DK)),
         ("new_ckv", (1, 1, 128, KVR)), ("new_kr", (1, 1, 128, DR))]


def kernel(**inputs):
    import concourse.bacc as bacc
    from concourse.bass_utils import run_bass_kernel_spmd

    nc = bacc.Bacc("TRN2", target_bir_lowering=False, num_devices=1)
    arrays, A, O = {}, {}, {}
    for name in _INS:
        arrays["in_" + name] = np.ascontiguousarray(inputs[name])
    arrays["in_consts"] = constants()
    for name, a in arrays.items():
        A[name[3:]] = nc.dram_tensor(name, a.shape, mybir.dt.from_np(a.dtype), kind="ExternalInput").ap()
    for name, shape in _OUTS:
        O[name] = nc.dram_tensor("out_" + name, shape, mybir.dt.float32, kind="ExternalOutput").ap()
    build(nc, A, O)
    r = run_bass_kernel_spmd(nc, [arrays], core_ids=[0])
    return tuple(r.results[0]["out_" + name] for name, _ in _OUTS)
```

```python
import concourse.bass as bass
from concourse import mybir
from contextlib import ExitStack
import numpy as np

D = 1024
KD = D // 128
NT = 5
NLAT = 512
NTOK = 640
CH = 32
HA, DK = 4, 128
MH, DN, DR, DV = 8, 64, 32, 64
QR, KVR = 384, 256
AB_IN = 5 * 512 + QR + KVR + DR
NE, NG, EG, FF = 32, 4, 8, 128
ALPHA = 4.0 ** 0.25
LN_EPS, RMS_EPS = 1e-5, 1e-6
SCALE = float(DN + DR) ** -0.5
CFK, SCK = 31, 3
PADW = 15
CXW = 15 + 512 + 15 + 128 + 15
COW = 656
NOROW = 8192.0
NEXTRA = 10
NTILE = 32 + NEXTRA + 2

CONST_COLS = [("ident", 128), ("mask_f", 128), ("mask_b", 128), ("tri", 128), ("ones", 128), ("iota", 128),
              ("scan", 640), ("perm", 32), ("cos", 512), ("sin", 512),
              ("pidx", 1), ("prio4", 4), ("prio8", 8), ("e128", 32), ("evens", 5)]
COFF = {}
_at = 0
for _n, _w in CONST_COLS:
    COFF[_n] = (_at, _at + _w)
    _at += _w
NCONST = _at


def constants():
    c = np.zeros((128, NCONST), np.float32)

    def put(name, rows, value):
        a, b = COFF[name]
        c[rows, a:b] = value
    p = np.arange(128)
    same = (p[:, None] // CH) == (p[None, :] // CH)
    put("ident", slice(None), np.eye(128))
    put("mask_f", slice(None), same & (p[:, None] <= p[None, :]))
    put("mask_b", slice(None), same & (p[:, None] >= p[None, :]))
    put("tri", slice(None), p[:, None] < p[None, :])
    put("ones", slice(None), 1.0)
    put("iota", slice(None), p[None, :])
    put("scan", slice(None), (np.arange(NTOK) % CH != 0)[None, :])
    perm = np.zeros((32, 32))
    for a in range(2):
        for f in range(8):
            perm[a * 16 + 8 + f, a * 16 + f] = -1.0
            perm[a * 16 + f, a * 16 + 8 + f] = 1.0
    put("perm", slice(64, 96), perm)
    inv = np.float32(10000.0) ** (-np.arange(8, dtype=np.float32) / np.float32(8))
    tok = np.arange(NLAT)
    pos = np.stack([tok // 64, tok % 64]).astype(np.float32)
    ang = (pos[:, None, :] * inv[None, :, None]).astype(np.float32)
    ang = np.stack([ang, ang], axis=1).reshape(32, NLAT)
    put("cos", slice(64, 96), np.cos(ang))
    put("sin", slice(64, 96), np.sin(ang))
    put("pidx", slice(None), p[:, None])
    put("prio4", slice(None), np.arange(4, 0, -1)[None, :])
    put("prio8", slice(None), np.arange(8, 0, -1)[None, :])
    put("e128", slice(None), 128 * np.arange(32)[None, :])
    put("evens", slice(None), 2 * np.arange(5)[None, :])
    return c


FIRST_MODS = [("mod", 0), ("mod", 1), ("modb", 0), ("mod", 2), ("modb", 1), ("mod", 3), ("modb", 2), ("modb", 3)]
ATTN_MOD_TILE = 3
UNIT_MODS = [[("mod", 1, 3 * u), ("mod", 1, 3 * u + 1)] for u in range(4)]
STEP_MODS = {(u, 2): [("mod", 1, 3 * u + 2)] for u in range(4)}
STEP_MODS[0, 0] = [("modb", 1, 0), ("modb", 1, 1)]
STEP_MODS[0, 3] = [("modb", 1, 2)]
STEP_MODS[1, 0] = [("modb", 1, 3)]
CD_ORDER = (3, 4, 0, 1, 2)
PE_TAPS = 7


def psum_groups():
    g = [("vec",)]
    for l in range(2):
        if l == 0:
            g += [(kind, 0, c) for kind, c in FIRST_MODS]
        g += [("xT", l, k) for k in range(KD)]
        if l == 0:
            g += [("cq", t) for t in range(NT)]
            g += [("cqT", r) for r in range(3)] + [("ckvT", r) for r in range(2)] + [("krT",), ("krP",)]
            g += [("v", t) for t in range(6)]
            g += [("k", 0), ("q", 0), ("qP", 0)]
            steps = [(h, t) for h in range(MH) for t in range(NT)]
            g.append(("s",) + steps[0])
            for n, (h, t) in enumerate(steps):
                if h + 1 < MH and t == 0:
                    g += [("k", h + 1), ("q", h + 1)]
                if h + 1 < MH and t == 2:
                    g.append(("qP", h + 1))
                if n + 1 < len(steps):
                    g.append(("s",) + steps[n + 1])
                if t == ATTN_MOD_TILE:
                    g.append(("mod", 0, 4 + h))
                g += [("pt", h, t), ("o", h, t)]
            g += [("obT", j) for j in range(4)]
            g += [("hq", c, j) for c in range(3) for j in range(4)]
            g += [("hv", c, t) for c in range(2) for t in range(NT)]
            for u in range(4):
                g += UNIT_MODS[u]
                g += [("hs", u, 0), ("hk", u, 0), ("hd", u, 0)]
                for n in range(NT):
                    if n + 1 < NT:
                        g += [("hs", u, n + 1), ("hk", u, n + 1), ("hd", u, n + 1)]
                    g.append(("ho", u, n))
                    g += STEP_MODS.get((u, n), [])
            g += [("oaT", j) for j in range(4)]
        else:
            g += [("cd", c, j) for c in CD_ORDER for j in range(4)]
            g += [("cv", j) for j in range(4)]
            g += [("mean",), ("var",)]
        g += [("y", l, t) for t in range(NT)]
        g += [("hT", l, t) for t in range(NT)]
        g += [("lg", l), ("ct", l), ("tb", l)]
    return {name: n for n, name in enumerate(g)}


def build(nc, A, O):
    f32, i32, bf16 = mybir.dt.float32, mybir.dt.int32, mybir.dt.bfloat16
    ALU = mybir.AluOpType
    ACT = mybir.ActivationFunctionType
    AX = mybir.AxisListType
    GROUP = psum_groups()
    ctx = ExitStack()
    with ctx:
        def sb(name, shape, dt=f32):
            return ctx.enter_context(nc.sbuf_tensor(name, shape, dt))

        def sem(name):
            return ctx.enter_context(nc.semaphore(name))

        C = sb("consts", [128, NCONST])
        X = sb("x_tm", [128, NT, D])
        HT = sb("h_cm", [128, KD, NTOK])
        OT = sb("mix_cm", [128, KD, NTOK])
        W = sb("weights", [128, 3 * 4096])
        GR = sb("gate_rows", [128, 2048])
        LNR = sb("ln_rows", [128, 2, 1024])
        Z = sb("scratch", [128, 15360])
        MB2 = sb("mod_bias2", [2, 512])
        MR = sb("mod_row", [2, 2, 512])
        MC = sb("mod_cols", [128, 2, 2, KD, 2])
        CT = sb("c_cm", [128, 16])
        VC = sb("vectors_cm", [128, 43])
        CW = sb("taps_cm", [128, 124])
        LBT = sb("lower_bound", [128, 2, 8])
        LBS = sb("lower_bound_work", [128, 3, 8])
        HNG = sb("hgrn_norm_row", [128, DK])
        SS = sb("square_sums", [128, NT, 2])
        GF = sb("slots_of_tokens_f", [128, 2, NT])
        RR = sb("rms_scale", [128, NT, 2])
        MXS = sb("softmax_max", [128, 2, 2])
        SUM = sb("softmax_sum", [128, 2, 2])
        DEC = sb("chunk_decay", [128, 2, 20])
        ZERO = sb("zero_state", [128, 128])
        HSS = sb("head_square_sums", [128, 20])
        ST6 = sb("ln_stats", [128, 2, 2, 6])
        MV = sb("ln_mean_var", [128, 2, 2])
        RSD = sb("ln_rstd", [128, 2, 2])
        WR = sb("router_w", [128, KD, 36])
        RS = sb("router_small", [128, 10, 8])
        O4 = sb("group_onehot", [128, NT, 4])
        W12 = sb("pair_weights", [128, 2, NT])
        RUN = sb("running_count", [128, NE])
        TI = sb("gather_rows", [128, NTILE], i32)
        TY = sb("scatter_rows", [128, NTILE], i32)
        NOR = sb("no_rows", [128, 2 * NTILE])
        PAY = sb("slot_payload", [128, 2, NT, 2])
        GI = sb("slots_of_tokens", [128, 2, NT], i32)
        EXI = sb("extra_experts", [128, NEXTRA], i32)
        RI = sb("extra_pairs", [128, 1], i32)
        IXG = sb("gather_now", [128, 2], i32)
        IXY = sb("scatter_now", [128, 2], i32)
        PS = ctx.enter_context(nc.psum_tensor("ps", [128, 4, 1024], f32))

        def const(name, rows=slice(0, 128)):
            a, b = COFF[name]
            return C[rows, a:b]

        ident = const("ident")

        TBL = nc.dram_tensor("slot_table", [NTILE * 128, 2], f32).ap()
        HD = nc.dram_tensor("h_rows", [NTOK, D], f32).ap()
        MODD = nc.dram_tensor("mod_rows", [2, 2, 6 * D], f32).ap()
        YD = nc.dram_tensor("expert_rows", [2 * NTOK, D], f32).ap()

        slot_full = [sem(f"slot_full{i}") for i in range(4)]
        slot_free = [sem(f"slot_free{i}") for i in range(4)]
        w_full = [sem(f"w_full{i}") for i in range(3)]
        vec_step, act_step, pool_step = sem("vec_step"), sem("act_step"), sem("pool_step")
        d_const, d_vec, d_x, d_rows = sem("d_const"), sem("d_vec"), sem("d_x"), sem("d_rows")
        d_cache, d_kv_out, d_xr = sem("d_cache"), sem("d_kv_out"), sem("d_xr")
        c_silu, lb_exp_in, lb_exp = sem("c_silu"), sem("lb_exp_in"), sem("lb_exp")
        sq_ready, rms_in, rms_sd, norm_ready = sem("sq_ready"), sem("rms_in"), sem("rms_sd"), sem("norm_ready")
        kr_ready, q_raw, q_rot = sem("kr_ready"), sem("q_raw"), sem("q_rot")
        max_ready, exp_ready = sem("max_ready"), sem("exp_ready")
        h_zero, h_f, h_l, h_arg, h_exp, h_mul = (sem("h_zero"), sem("h_f"), sem("h_l"), sem("h_arg"),
                                                 sem("h_exp"), sem("h_mul"))
        h_vm, h_s0, d_state = sem("h_vm"), sem("h_s0"), sem("d_state")
        o_var, o_sd, o_ready = sem("o_var"), sem("o_sd"), sem("o_ready")
        ln_var, ln_sd, x_ready, h_ready = sem("ln_var"), sem("ln_sd"), sem("x_ready"), sem("h_ready")
        d_ln = sem("d_ln")
        d_mr, d_g1, d_r = [sem(f"d_mr{i}") for i in range(2)], sem("d_g1"), sem("d_r")
        tap_diag = sem("tap_diag")
        const_ready = sem("const_ready")
        d_hst = [sem(f"d_hst{i}") for i in range(2)]
        d_wr = sem("d_wr")
        rt_slots, d_init, d_scat, d_tb = sem("rt_slots"), sem("d_init"), sem("d_scat"), sem("d_tb")
        rt_exp_in, rt_exp, rt_mask, rt_ready = sem("rt_exp_in"), sem("rt_exp"), sem("rt_mask"), sem("rt_ready")
        d_yl = [sem(f"d_yl{i}") for i in range(2)]
        y_used = sem("y_used")
        moe_done = sem("moe_done")
        cd_pad, cd_conv, cd_sq, cd_sd, cd_u = (sem("cd_pad"), sem("cd_conv"), sem("cd_sq"), sem("cd_sd"), sem("cd_u"))
        cd_out, cd_up = sem("cd_out_a"), sem("cd_up")
        cd_out_v = sem("cd_out_v")
        d_out = sem("d_out")

        def moe_sems(l):
            names = ["w0", "w1", "w2", "w3", "xw0", "xw1", "g0", "g1", "t", "xa", "xv", "gu", "sg", "hid", "ht", "hidt",
                     "down", "ya", "yv", "s0", "s1", "s_ix", "pool_passed"]
            return {n: sem(f"moe{l}_{n}") for n in names}
        MS = [moe_sems(l) for l in range(2)]

        def ps(*name):
            return PS[:, GROUP[name] % 4, :]

        def open_group(pe, *name):
            n = GROUP[name]
            if n >= 4:
                pe.wait_ge(slot_free[n % 4], n // 4)

        def close_group(ins, *name):
            ins.then_inc(slot_full[GROUP[name] % 4], 1)

        def filled(eng, *name):
            eng.wait_ge(slot_full[GROUP[name] % 4], GROUP[name] // 4 + 1)

        def release(ins, *name):
            ins.then_inc(slot_free[GROUP[name] % 4], 1)

        def emptied(eng, *name):
            eng.wait_ge(slot_free[GROUP[name] % 4], GROUP[name] // 4 + 1)

        def bank(b):
            return PS[:, b // 2, (b % 2) * 512:(b % 2) * 512 + 512]

        MB = [C[0:2, COFF["cos"][0]:COFF["cos"][1]], C[0:2, COFF["sin"][0]:COFF["sin"][1]], MB2[:, :]]
        V1, V2, V3 = GR[0:16, 0:128], GR[0:43, 128:256], GR[0:124, 256:384]
        def z(a, n):
            return Z[:, a:a + n]

        CQ = z(0, 3360).rearrange("p (t c) -> p t c", t=NT)
        CQT = z(3360, 1920).rearrange("p (r t) -> p r t", r=3)
        CKVT = z(5280, 1536).rearrange("p (r t) -> p r t", r=2)
        VT = z(6816, 3072).rearrange("p (t c) -> p t c", t=6)
        KT = z(9888, 1536).rearrange("p (b t) -> p b t", b=2)
        QT = z(11424, 1280).rearrange("p (b t) -> p b t", b=2)
        KRS, ROT1, ROT2 = z(12704, 512), z(13216, 512), z(13728, 512)
        CC = z(14240, 288)
        CKG = z(14528, KVR)
        LNF = LNR[:, :, :].rearrange("p a b -> p (a b)")
        PB = LNF[:, 0:1280].rearrange("p (b t) -> p b t", b=2)
        PTS = GR[:, 0:1280].rearrange("p (b t) -> p b t", b=2)
        OTF = OT[:, :, :].rearrange("p a b -> p (a b)")
        OB = OTF[:, 0:2560].rearrange("p (t c) -> p t c", t=NT)

        HQ = z(0, 2560).rearrange("p (h t) -> p h t", h=4)
        HF = [z(2560 + 2560 * d, 2560).rearrange("p (h t) -> p h t", h=4) for d in range(2)]
        HV = z(7680, 2560).rearrange("p (t c) -> p t c", t=NT)
        HG = z(10240, 2560).rearrange("p (t c) -> p t c", t=NT)
        HO = z(12800, 2560).rearrange("p (t c) -> p t c", t=NT)
        HTF = HT[:, :, :].rearrange("p a b -> p (a b)")
        QHAT, KHAT, QTIL, KTIL = [HTF[:, 1280 * i:1280 * (i + 1)].rearrange("p (h t) -> p h t", h=2)
                                  for i in range(4)]
        XF = X[:, :, :].rearrange("p a b -> p (a b)")
        BUFB = XF[:, 0:1280].rearrange("p (h t) -> p h t", h=2)
        BUFA = XF[:, 1280:2560].rearrange("p (h t) -> p h t", h=2)
        VM = XF[:, 2560:4608].rearrange("p (b h j v) -> p b h j v", b=2, h=2, j=4)
        BUFL = LNF[:, 0:1280].rearrange("p (h t) -> p h t", h=2)
        SC = GR[:, 0:1024].rearrange("p (d b h t) -> p d b h t", d=2, b=2, h=2)
        KTT = GR[:, 1024:1536].rearrange("p (b c) -> p b c", b=2)
        ST = OTF[:, 0:1536].rearrange("p (b h n v) -> p b h n v", b=2, h=2, n=3)
        CAR = OTF[:, 1536:2304].rearrange("p (b h v) -> p b h v", b=3, h=2)
        S0B = OTF[:, 2304:2560].rearrange("p (h v) -> p h v", h=2)

        G1 = GR[:, :].rearrange("p (g d) -> p g d", g=2)
        R3, R4, R5 = [z(2048 * i, 2048).rearrange("p (g d) -> p g d", g=2) for i in range(3)]
        ZT = z(6144, 2048).rearrange("p (b d) -> p b d", b=2)
        HB = z(8192, 2048).rearrange("p (b d) -> p b d", b=2)
        SG = z(8192, 256).rearrange("p (b f) -> p b f", b=2)
        HID = z(8448, 256).rearrange("p (b f) -> p b f", b=2)
        HIDT = z(8704, 256).rearrange("p (b f) -> p b f", b=2)
        XG = z(10240, 2048).rearrange("p (b d) -> p b d", b=2)
        XGT = z(12288, 2048).rearrange("p (b d) -> p b d", b=2)
        CM = z(14336, 160).rearrange("p (t e) -> p t e", t=NT)
        IND, INC, DELTA = z(14496, 128), z(14624, 128), z(14912, 128)
        BASE = z(14752, 160)
        GG, GT = z(15040, 160), z(15200, 160)
        TBR = OTF[0:NTILE, 256:512]
        EXW = OTF[:, 512:512 + NEXTRA * 128].rearrange("p (n c) -> p n c", n=NEXTRA)
        EXF = OTF[:, 1800:1800 + NEXTRA]
        LG = OTF[:, 0:180].rearrange("p (t c) -> p t c", t=NT)
        RT = OTF[:, 4096:5056].rearrange("p (a c) -> p a c", a=6)
        YB = OTF[:, 0:4096].rearrange("p (b k d) -> p b k d", b=2, k=2)

        BG = z(0, 2560).rearrange("p (j t) -> p j t", j=4)
        CXP = z(2560, 4 * CXW).rearrange("p (j t) -> p j t", j=4)
        UP = z(5300, 4 * CXW).rearrange("p (j t) -> p j t", j=4)
        CO = z(8040, 4 * COW).rearrange("p (j t) -> p j t", j=4)
        SQ = z(10664, 4 * COW).rearrange("p (j t) -> p j t", j=4)
        RST = z(13288, COW)
        DG = [OTF[:, 2560 + 128 * i:2688 + 128 * i] for i in range(20)]
        DG += [z(13952 + 128 * i, 128) for i in range(4 * PE_TAPS - 20)]

        def state_before(i, n, step, hh):
            if step:
                return ST[:, i % 2, hh, step - 1, :]
            if n == 0:
                return S0B[:, hh, :]
            return ZERO[:, :] if n == 4 else CAR[:, (i - 1) % 3, hh, :]

        def slot3(s):
            return W[:, 4096 * s:4096 * (s + 1)]

        def col_chunk(w, a, b):
            return w.rearrange("(k p) n -> p k n", p=128)[:, :, a:b]

        WITEM = {}
        items = []
        in_slot = [None, None, None]
        words_in = [0, 0, 0]

        def item(name, s, last, parts):
            words_in[s] += 16 * len(parts)
            WITEM[name] = {"slot": s, "value": words_in[s], "parts": parts, "last": last, "before": in_slot[s]}
            in_slot[s] = name
            items.append(name)

        def mod_item(l, c, s):
            item(("mod", l, c), s, ("mod", l, c),
                 [(slot3(s).rearrange("p (k n) -> p k n", k=8), col_chunk(A["mod_w"][l], c * 512, c * 512 + 512)),
                  (MB[s], A["mod_b"][l, c * 512:c * 512 + 512].partition_broadcast(2))])

        def proj_item(name, s, last, w, a, b):
            n = b - a
            item(name, s, last, [(slot3(s)[:, 0:8 * n].rearrange("p (k n) -> p k n", k=8), col_chunk(w, a, b))])

        for c in range(4):
            mod_item(0, c, c % 3)
        w_in = A["ab_w_in"][0]
        proj_item(("cqa",), 1, ("cq", 4), w_in, 2560, 3072)
        proj_item(("cqb",), 2, ("cq", 4), w_in, 3072, AB_IN)
        item(("uq",), 0, ("q", 7), [(slot3(0)[:, 0:2304].rearrange("p (k n) -> p k n", k=3),
                                     A["mla_w_uq"][0].rearrange("(k p) n -> p k n", p=128))])
        item(("ukv",), 1, ("k", 7), [(slot3(1)[:, 0:2048].rearrange("p (k n) -> p k n", k=2),
                                      A["mla_w_ukv"][0].rearrange("(k p) n -> p k n", p=128))])

        def hq_item(c, s):
            proj_item(("hq", c), s, ("hq", c, 3), w_in, c * 512, c * 512 + 512)
        for c in range(4, 11):
            mod_item(0, c, 2)
        hq_item(0, 0)
        hq_item(1, 1)
        mod_item(0, 11, 2)
        hq_item(2, 2)
        for c in range(2):
            proj_item(("hv", c), c, ("hv", c, 4), w_in, 1536 + c * 512, 2048 + c * 512)
        for c in range(12):
            mod_item(1, c, (c + 2) % 3)
        for c in range(2):
            proj_item(("wo", 0, c), (c + 2) % 3, ("y", 0, 4), A["ab_w_out"][0], c * 512, c * 512 + 512)
        N_ITEMS0 = len(items)
        LAST_IN_SLOT0 = list(in_slot)
        in_slot[:] = [None, None, None]
        for n, c in enumerate(CD_ORDER):
            proj_item(("cd", c), n % 3, ("cd", c, 3), A["cd_w_in"][0], c * 512, c * 512 + 512)
        for c in range(2):
            proj_item(("wo", 1, c), (c + 2) % 3, ("y", 1, 4), A["cd_w_out"][0], c * 512, c * 512 + 512)
        LAST_IN_SLOT1 = list(in_slot)

        def rows_stored(l, c):
            return sum(1 for k in range(12 * l + c + 1) if k % 2 == c % 2 and k % 12 >= 4)

        def weights(pe, *name):
            it = WITEM[name]
            pe.wait_ge(w_full[it["slot"]], it["value"])
            return slot3(it["slot"])

        U = 8
        NI = NE // U
        EW = 3072

        def expert_gu(s):
            return W[:, EW * s:EW * s + 2048].rearrange("p (k f) -> p k f", k=8)

        def expert_down(s):
            return W[:, EW * s + 2048:EW * (s + 1)]

        block = ctx.enter_context(nc.Block())

        @block.sync
        def _(sp):
            sp.dma_start(C[:, :], A["consts"]).then_inc(d_const, 16)
            xs = A["x_sample"][0].rearrange("(t p) d -> p t d", p=128)

            def retire(name):
                last = WITEM[name]["last"]
                if last[0] != "mod":
                    filled(sp, *last)
                    return
                emptied(sp, *last)
                l, c = last[1:]
                if c >= 4:
                    sp.dma_start(MODD[l, :, c * 512:c * 512 + 512], MR[:, c % 2, :]).then_inc(d_mr[c % 2], 16)

            def load_rows(l, idx, dst, done):
                sp.dma_start(dst, MODD[l, :, idx * D:(idx + 1) * D].partition_broadcast(128)).then_inc(done, 16)

            def load_item(n):
                it = WITEM[items[n]]
                if it["before"] is not None:
                    retire(it["before"])
                for p, (dst, src) in enumerate(it["parts"]):
                    if n < 2 and p == 1:
                        sp.wait_ge(d_const, 16)
                    sp.dma_start(dst, src).then_inc(w_full[it["slot"]], 16)

            def load_expert(l, e, s, done=None):
                m = MS[l]
                done = m[f"w{s}"] if done is None else done
                wg = A["moe_w_gate"][l].rearrange("e (k p) f -> e p k f", p=128)
                wu = A["moe_w_up"][l].rearrange("e (k p) f -> e p k f", p=128)
                if isinstance(e, int):
                    g, u, dn = wg[e], wu[e], A["moe_w_down"][l, e]
                else:
                    g = wg[bass.ds(e, 1)].rearrange("e p k f -> (e p) k f")
                    u = wu[bass.ds(e, 1)].rearrange("e p k f -> (e p) k f")
                    dn = A["moe_w_down"][l][bass.ds(e, 1)].rearrange("e f d -> (e f) d")
                sp.dma_start(expert_gu(s)[:, :, 0:FF], g).then_inc(done, 16)
                sp.dma_start(expert_gu(s)[:, :, FF:2 * FF], u).then_inc(done, 16)
                sp.dma_start(expert_down(s), dn).then_inc(done, 16)

            for l in range(2):
                m = MS[l]
                lo, hi = (0, N_ITEMS0) if l == 0 else (N_ITEMS0, len(items))
                if l == 1:
                    sp.wait_ge(moe_done, 1)
                for n in range(lo, hi):
                    load_item(n)
                    if n == 2:
                        sp.dma_start(X[:, 0:4, :], xs).then_inc(d_x, 16)
                        sp.dma_start(X[:, 4, :], A["x_prompt"][0]).then_inc(d_x, 16)
                    if n == N_ITEMS0 + 2:
                        load_rows(1, 2, G1, d_g1)
                if l == 0:
                    retire(LAST_IN_SLOT0[1])
                    for i in range(2):
                        sp.wait_ge(d_mr[i], 16 * 8)
                    filled(sp, "ho", 3, 4)
                    load_rows(0, 2, G1, d_g1)
                else:
                    retire(LAST_IN_SLOT1[1])
                    sp.wait_ge(cd_out, 4)
                    sp.wait_ge(cd_out_v, 1)
                load_rows(l, 4, R4, d_r)
                load_rows(l, 3, R3, d_r)
                load_rows(l, 5, R5, d_r)
                retire(("wo", l, 1))
                for e in range(4):
                    load_expert(l, e, e)
                for u in range(4, U):
                    sp.wait_ge(m["down"], u - 3)
                    load_expert(l, u, u % 4)
                with sp.Fori(1, NI) as i:
                    for u in range(U):
                        sp.wait_ge(m["down"], i * U + (u - 3))
                        load_expert(l, i * U + u, u % 4)
                sp.wait_ge(rt_ready, l + 1)
                pairs = sp.value_load(RI[0:1, 0:1], min_val=0, max_val=NEXTRA // 2)
                with sp.If(pairs > 0):
                    with sp.Fori(0, pairs) as j:
                        for u in range(2):
                            e = sp.value_load(EXI[0:1, bass.ds(j * 2 + u, 1)], min_val=0, max_val=NE - 1)
                            sp.wait_ge(m["down"], NE + j * 2 + (u - 1))
                            load_expert(l, e, u, m[f"xw{u}"])
            for t in range(NT):
                sp.wait_ge(x_ready, 15 + t + 1)
                dst = O["y_sample"][0, t * 128:(t + 1) * 128, :] if t < 4 else O["y_prompt"][0]
                sp.dma_start(dst, X[:, t, :]).then_inc(d_out, 16)
            sp.wait_ge(d_out, 16 * NT)

        @block.gpsimd
        def _(pool):
            steps = [0]

            def chain(ins):
                steps[0] += 1
                ins.then_inc(pool_step, 1)
                pool.wait_ge(pool_step, steps[0])

            pool.dma_start(V1[0:8, :], A["c"][0].rearrange("(k p) -> k p", p=128)).then_inc(d_vec, 16)
            pool.dma_start(V1[8:16, :], A["c_ctx"].rearrange("(k p) -> k p", p=128)).then_inc(d_vec, 16)
            pool.dma_start(V2[0:16, :], A["hgrn_lb_logits"].rearrange("r d (h p) -> (r d h) p", p=128)).then_inc(d_vec, 16)
            pool.dma_start(V2[16:19, :], A["mla_q_norm_g"][0].rearrange("(k p) -> k p", p=128)).then_inc(d_vec, 16)
            pool.dma_start(V2[19:23, :], A["cf_conv_b"][0].rearrange("(k p) -> k p", p=128)).then_inc(d_vec, 16)
            pool.dma_start(V2[23:27, :], A["cf_ln_g"][0].rearrange("(k p) -> k p", p=128)).then_inc(d_vec, 16)
            pool.dma_start(V2[27:31, :], A["cf_ln_b"][0].rearrange("(k p) -> k p", p=128)).then_inc(d_vec, 16)
            pool.dma_start(V2[31:43, :], A["sc_conv_w"][0].rearrange("t (k p) -> (t k) p", p=128)).then_inc(d_vec, 16)
            pool.dma_start(V3[:, :], A["cf_conv_w"][0].rearrange("t (k p) -> (t k) p", p=128)).then_inc(d_vec, 16)
            pool.dma_start(CKG[:, :], A["mla_kv_norm_g"][0].partition_broadcast(128)).then_inc(d_rows, 16)
            pool.dma_start(HNG[:, :], A["hgrn_norm_g"][0].partition_broadcast(128)).then_inc(d_rows, 16)
            pool.dma_start(CC[:, 0:KVR], A["cache_mla_ckv"][0, 0]).then_inc(d_cache, 16)
            pool.dma_start(CC[:, KVR:288], A["cache_mla_krope"][0, 0]).then_inc(d_cache, 16)

            pool.wait_ge(norm_ready, 1)
            pool.dma_start(O["new_ckv"][0, 0], CQ[:, 4, QR:QR + KVR]).then_inc(d_kv_out, 16)
            pool.dma_start(O["new_kr"][0, 0], CQ[:, 4, QR + KVR:672]).then_inc(d_kv_out, 16)

            filled(pool, "obT", 3)
            nc.gpsimd.memset(VM[:, :, :, :, :], 0.0).then_inc(h_zero, 1)
            nc.gpsimd.memset(SC[:, :, :, :, :], 0.0).then_inc(h_zero, 1)
            nc.gpsimd.memset(ZERO[:, :], 0.0).then_inc(h_zero, 1)
            pool.wait_ge(h_zero, 3)
            state_in = [A["state_hgrn_fwd"][0, 0], A["state_hgrn_bwd"][0, 0]]
            state_out = [O["new_sf"][0, 0], O["new_sb"][0, 0]]
            emptied(pool, "hv", 0, 4)
            for u in range(4):
                d, hp = u // 2, u % 2
                if u:
                    filled(pool, "ho", u - 1, 1)
                pool.dma_start(S0B[:, :, :], state_in[d][2 * hp:2 * hp + 2].rearrange("h k v -> k h v")).then_inc(h_s0, 16)
                for n in range(NT):
                    i = 5 * u + n
                    t = (n if d == 0 else 3 - n) if n < 4 else 4
                    if i >= 2:
                        filled(pool, "hd", *divmod(i - 2, 5))
                    for j in range(4):
                        r = slice(32 * j, 32 * j + 32)
                        src = HV[r, t, 256 * hp:256 * hp + 256].rearrange("p (h v) -> p h v", h=2)
                        nc.gpsimd.tensor_copy(VM[r, i % 2, :, j, :], src).then_inc(h_vm, 1)
                emptied(pool, "hd", u, 4)
                pool.dma_start(state_out[d][2 * hp:2 * hp + 2].rearrange("h k v -> k h v"),
                               CAR[:, (5 * u + 4) % 3, :, :]).then_inc(d_state, 16)
            filled(pool, "ho", 3, 4)
            pool.dma_start(X[:, 0:4, :], A["x_sample"][0].rearrange("(t p) d -> p t d", p=128)).then_inc(d_xr, 16)
            pool.dma_start(X[:, 4, :], A["x_prompt"][0]).then_inc(d_xr, 16)

            for l in range(2):
                m = MS[l]
                if l == 1:
                    pool.wait_ge(x_ready, 10)
                    for i in range(4 * PE_TAPS):
                        j, k = i // PE_TAPS, CFK - PE_TAPS + i % PE_TAPS
                        nc.gpsimd.tensor_scalar(DG[i], ident, CW[:, 4 * k + j:4 * k + j + 1], None, ALU.mult).then_inc(tap_diag, 1)
                pool.wait_ge(const_ready, 1)
                pool.dma_start(TBL.rearrange("(p a) c -> p (a c)", p=128), NOR[:, :]).then_inc(d_init, 16)
                for k in range(2):
                    if k == 0:
                        if l == 0:
                            filled(pool, "oaT", 3)
                        else:
                            pool.wait_ge(x_ready, 10)
                        pool.dma_start(LNR[:, 0, :], A["ln_g"][l, 0].partition_broadcast(128)).then_inc(d_ln, 16)
                        pool.dma_start(LNR[:, 1, :], A["ln_b"][l, 0].partition_broadcast(128)).then_inc(d_ln, 16)
                        pool.dma_start(WR[:, :, 0:4], A["moe_w_group"][l].rearrange("(k p) n -> p k n", p=128)).then_inc(d_wr, 16)
                        pool.dma_start(WR[:, :, 4:36], A["moe_w_expert"][l].rearrange("(k p) n -> p k n", p=128)).then_inc(d_wr, 16)
                        for t in range(NT):
                            pool.wait_ge(h_ready, 5 * l + t + 1)
                            pool.dma_start(HD[t * 128:(t + 1) * 128, :], HB[:, t % 2, :]).then_inc(d_hst[t % 2], 16)
                        pool.wait_ge(x_ready, 10 * l + 5)
                        pool.dma_start(LNR[:, 0, :], A["ln_g"][l, 1].partition_broadcast(128)).then_inc(m["s0"], 16)
                        pool.dma_start(LNR[:, 1, :], A["ln_b"][l, 1].partition_broadcast(128)).then_inc(m["s1"], 16)
                pool.wait_ge(d_init, 16 * (l + 1))
                pool.wait_ge(rt_slots, l + 1)
                for k in range(2):
                    for t in range(NT):
                        nc.gpsimd.indirect_dma_start(
                            out=TBL[:, :], out_offset=bass.IndirectOffsetOnAxis(ap=GI[:, k, t:t + 1], axis=0),
                            in_=PAY[:, k, t, :], in_offset=None,
                            bounds_check=NTILE * 128 - 1, oob_is_err=False).then_inc(d_scat, 16)
                pool.wait_ge(d_scat, 160 * (l + 1))
                pool.dma_start(TBR, TBL.rearrange("(n s) c -> n (s c)", s=128)).then_inc(d_tb, 16)
                pool.wait_ge(d_hst[0], 16 * 3 * (l + 1))
                pool.wait_ge(d_hst[1], 16 * 2 * (l + 1))

                def gather(e, par, cnt, landed=None):
                    if landed is not None:
                        pool.wait_ge(m[f"g{par}"], landed)
                        pool.sem_inc(m["pool_passed"], 1)
                    nc.gpsimd.tensor_copy(IXG[:, par:par + 1], TI[:, bass.ds(e, 1)]).then_inc(m["s_ix"], 1)
                    pool.wait_ge(m["s_ix"], cnt)
                    pool.sem_inc(m["pool_passed"], 1)
                    nc.gpsimd.indirect_dma_start(
                        out=XG[:, par, :], out_offset=None, in_=HD[:, :],
                        in_offset=bass.IndirectOffsetOnAxis(ap=IXG[:, par:par + 1], axis=0),
                        bounds_check=NTOK - 1, oob_is_err=False).then_inc(m[f"g{par}"], 16)

                def tiles(n0, h0, count):
                    for u in range(count):
                        par = u % 2
                        pool.wait_ge(m["t"], n0 + (u + 1))
                        gather(n0 + (u + 2), par, n0 + n0 + (2 * u + 3), h0 + 16 * ((u + 2) // 2))
                        pool.wait_ge(m["ya"], 1 + n0 + (u + 1))
                        pool.wait_ge(m["yv"], 1 + n0 + (u + 1))
                        pool.wait_ge(m[f"s{par}"], 16 + h0 + 16 * (u // 2))
                        pool.sem_inc(m["pool_passed"], 1)
                        nc.gpsimd.tensor_copy(IXY[:, par:par + 1], TY[:, bass.ds(n0 + u, 1)]).then_inc(m["s_ix"], 1)
                        pool.wait_ge(m["s_ix"], n0 + n0 + (2 * u + 4))
                        pool.sem_inc(m["pool_passed"], 1)
                        nc.gpsimd.indirect_dma_start(
                            out=YD[:, :], out_offset=bass.IndirectOffsetOnAxis(ap=IXY[:, par:par + 1], axis=0),
                            in_=ZT[:, par, :], in_offset=None,
                            bounds_check=2 * NTOK - 1, oob_is_err=False).then_inc(m[f"s{par}"], 16)

                emptied(pool, "tb", l)
                for e in range(2):
                    gather(e, e, e + 1)
                with pool.Fori(0, NI) as i:
                    tiles(i * U, i * (8 * U), U)
                pool.wait_ge(rt_ready, l + 1)
                pairs = pool.value_load(RI[0:1, 0:1], min_val=0, max_val=NEXTRA // 2)
                with pool.If(pairs > 0):
                    with pool.Fori(0, pairs) as j:
                        tiles(j * 2 + NE, j * 16 + 8 * NE, 2)
                pool.wait_ge(m["s0"], pairs * 16 + (16 + 8 * NE))
                pool.wait_ge(m["s1"], pairs * 16 + (16 + 8 * NE))
                pool.wait_ge(m["g0"], pairs * 16 + (16 + 8 * NE))
                pool.wait_ge(m["g1"], pairs * 16 + (16 + 8 * NE))
                pool.sem_inc(moe_done, 1)
                for t in range(NT):
                    if t >= 2:
                        pool.wait_ge(y_used, 5 * l + t - 1)
                    for k in range(2):
                        pool.dma_start(YB[:, t % 2, k, :],
                                       YD[k * NTOK + t * 128:k * NTOK + (t + 1) * 128, :]).then_inc(d_yl[t % 2], 16)
            pool.wait_ge(d_kv_out, 32)
            pool.wait_ge(d_state, 64)

        @block.scalar
        def _(act):
            steps = [0]

            def chain(ins):
                steps[0] += 1
                ins.then_inc(act_step, 1)
                act.wait_ge(act_step, steps[0])

            A_ = nc.scalar.activation

            def h_evac(l):
                for c in range(4):
                    emptied(act, "modb", l, c)
                shift, scale = MC[:, l, 0], MC[:, l, 1]
                for k in range(0, KD, 2):
                    filled(act, "xT", l, k)
                    A_(HT[:, k, 0:512], ps("xT", l, k)[:, 0:512], ACT.Identity,
                       bias=shift[:, k, 0:1], scale=scale[:, k, 0:1])
                    release(A_(HT[:, k, 512:640], ps("xT", l, k)[:, 512:640], ACT.Identity,
                               bias=shift[:, k, 1:2], scale=scale[:, k, 1:2]), "xT", l, k)

            act.wait_ge(d_vec, 16 * 9)
            A_(V1[:, :], V1[:, :], ACT.Silu).then_inc(c_silu, 1)
            act.wait_ge(lb_exp_in, 1)
            A_(LBS[:, 0:2, :], LBS[:, 0:2, :], ACT.Exp).then_inc(lb_exp, 1)

            h_evac(0)
            for t in range(NT):
                filled(act, "cq", t)
                release(A_(CQ[:, t, :], ps("cq", t)[:, 0:672], ACT.Copy), "cq", t)
            for t in range(NT):
                emptied(act, "cq", t)
                A_(z(6816 + 640 * t, QR), CQ[:, t, 0:QR], ACT.Square, accum_out=SS[:, t, 0:1])
                A_(z(6816 + 640 * t + QR, KVR), CQ[:, t, QR:QR + KVR], ACT.Square, accum_out=SS[:, t, 1:2]).then_inc(sq_ready, 1)
            act.wait_ge(rms_in, 1)
            A_(RR[:, :, :], RR[:, :, :], ACT.Sqrt).then_inc(rms_sd, 1)
            for r in range(2):
                filled(act, "ckvT", r)
                release(A_(CKVT[:, r, :], ps("ckvT", r)[:, 0:768], ACT.Copy), "ckvT", r)
            for t in range(6):
                filled(act, "v", t)
                release(A_(VT[:, t, :], ps("v", t)[:, 0:512], ACT.Copy), "v", t)

            def kq_evac(h):
                b = h % 2
                filled(act, "k", h)
                release(A_(KT[0:64, b, :], ps("k", h)[0:64, 0:768], ACT.Copy), "k", h)
                filled(act, "q", h)
                ins = A_(QT[0:96, b, :], ps("q", h)[0:96, 0:640], ACT.Copy)
                release(ins, "q", h)

            kq_evac(0)
            n = 0
            for h in range(MH):
                for t in range(NT):
                    nk = 640 if t < 4 else 128
                    b = n % 2
                    if h + 1 < MH and t == 1:
                        kq_evac(h + 1)
                    act.wait_ge(max_ready, n + 1)
                    if n >= 2:
                        filled(act, "pt", *divmod(n - 2, NT))
                        emptied(act, "o", *divmod(n - 2, NT))
                    release(A_(PB[:, b, 0:nk], ps("s", h, t)[:, 0:nk], ACT.Exp, bias=MXS[:, b, 1:2], scale=SCALE,
                               accum_out=SUM[:, b, 0:1]), "s", h, t)
                    filled(act, "pt", h, t)
                    release(A_(PTS[:, b, 0:nk], ps("pt", h, t)[:, 0:nk], ACT.Copy), "pt", h, t)
                    n += 1
            for j in range(4):
                filled(act, "obT", j)
                release(A_(OT[:, 4 + j, :], ps("obT", j)[:, 0:640], ACT.Copy), "obT", j)

            act.wait_ge(d_kv_out, 32)
            for c in range(3):
                for j in range(4):
                    filled(act, "hq", c, j)
                    dst = [HQ, HF[0], HF[1]][c]
                    release(A_(dst[:, j, :], ps("hq", c, j)[:, 0:640], ACT.Silu if c == 0 else ACT.Sigmoid), "hq", c, j)
            for t in range(NT):
                filled(act, "hv", 1, t)
                ins = A_(HG[:, t, :], ps("hv", 1, t)[:, 0:512], ACT.Silu)
                release(ins, "hv", 1, t)
            for u in range(4):
                d, hp = u // 2, u % 2
                act.wait_ge(h_f, u + 1)
                A_(BUFL[:, :, :], HF[d][:, 2 * hp:2 * hp + 2, :], ACT.Ln).then_inc(h_l, 1)
                act.wait_ge(h_arg, u + 1)
                if u:
                    filled(act, "ho", u - 1, 4)
                mid, full = (BUFA, BUFB) if d == 0 else (BUFB, BUFA)
                A_(QHAT[:, :, :], mid[:, :, :], ACT.Exp).then_inc(h_exp, 1)
                A_(KHAT[:, :, :], mid[:, :, :], ACT.Exp, scale=-1.0).then_inc(h_exp, 1)
                A_(KTIL[:, :, :], BUFL[:, :, :], ACT.Exp).then_inc(h_exp, 1)
                A_(QTIL[:, :, :], full[:, :, :], ACT.Exp).then_inc(h_exp, 1)
                e = CH - 1 if d == 0 else 0
                A_(DEC[:, :, :], full[:, :, :].rearrange("p h (c s) -> p h c s", s=CH)[:, :, :, e], ACT.Exp).then_inc(h_exp, 1)
                for n in range(NT):
                    i = 5 * u + n
                    t = (n if d == 0 else 3 - n) if n < 4 else 4
                    filled(act, "hk", u, n)
                    if i >= 2:
                        filled(act, "hd", *divmod(i - 2, 5))
                    release(A_(KTT[:, i % 2, :], ps("hk", u, n)[:, 0:256], ACT.Copy), "hk", u, n)
                    if d == 0 and n >= 1:
                        tt = n - 1
                        filled(act, "ho", u, tt)
                        release(A_(HO[:, tt, 256 * hp:256 * hp + 256], ps("ho", u, tt)[:, 0:256], ACT.Copy), "ho", u, tt)
                if d == 0:
                    filled(act, "ho", u, 4)
                    release(A_(HO[:, 4, 256 * hp:256 * hp + 256], ps("ho", u, 4)[:, 0:256], ACT.Copy), "ho", u, 4)
            act.wait_ge(o_var, 1)
            A_(HSS[:, :], HSS[:, :], ACT.Sqrt).then_inc(o_sd, 1)
            act.wait_ge(d_state, 64)
            for j in range(4):
                filled(act, "oaT", j)
                release(A_(OT[:, j, :], ps("oaT", j)[:, 0:640], ACT.Copy), "oaT", j)

            def ln_sqrt(q):
                act.wait_ge(ln_var, q + 1)
                A_(RSD[:, q % 2, 0:1], RSD[:, q % 2, 0:1], ACT.Sqrt).then_inc(ln_sd, 1)

            for l in range(2):
                m = MS[l]
                if l == 1:
                    h_evac(1)
                    act.wait_ge(cd_pad, 2)
                    for c in CD_ORDER:
                        f = ACT.Sigmoid if c == 4 else ACT.Copy
                        for j in range(4):
                            filled(act, "cd", c, j)
                            src = ps("cd", c, j)
                            if c == 0:
                                release(A_(BG[:, j, :], src[:, 0:640], f), "cd", c, j)
                            elif c == 2:
                                release(A_(SQ[:, j, 0:640], src[:, 0:640], f), "cd", c, j)
                            elif c == 4:
                                ins = A_(CO[:, j, 0:640], src[:, 0:640], f)
                                release(ins, "cd", c, j)
                            else:
                                dst = CXP if c == 1 else UP
                                A_(dst[:, j, 15:527], src[:, 0:512], f)
                                release(A_(dst[:, j, 542:670], src[:, 512:640], f), "cd", c, j)
                    emptied(act, "mean")
                    A_(SQ[:, :, :], CO[:, :, :], ACT.Square).then_inc(cd_sq, 1)
                    emptied(act, "var")
                    A_(RST[:, :], RST[:, :], ACT.Sqrt).then_inc(cd_sd, 1)
                    for j in range(4):
                        act.wait_ge(cd_u, j + 1)
                        A_(OT[:, 4 + j, 0:512], CO[:, j, 0:512], ACT.Silu, bias=VC[:, 27 + j:28 + j], scale=VC[:, 23 + j:24 + j])
                        A_(OT[:, 4 + j, 512:640], CO[:, j, 527:655], ACT.Silu, bias=VC[:, 27 + j:28 + j],
                           scale=VC[:, 23 + j:24 + j]).then_inc(cd_out, 1)
                for t in range(NT + 2):
                    if t < NT:
                        ln_sqrt(10 * l + t)
                    if t < 2:
                        continue
                    t -= 2
                    filled(act, "hT", l, t)
                    release(A_(HT[:, :, t * 128:(t + 1) * 128],
                               ps("hT", l, t).rearrange("p (k c) -> p k c", k=8), ACT.Copy), "hT", l, t)
                act.wait_ge(rt_exp_in, 2 * l + 1)
                A_(RT[:, 0, 0:20], RT[:, 0, 0:20], ACT.Exp).then_inc(rt_exp, 1)
                act.wait_ge(rt_exp_in, 2 * l + 2)
                A_(RS[:, 5, 0:5], RS[:, 5, 0:5], ACT.Exp).then_inc(rt_exp, 1)
                def tiles(n0, h0, count):
                    def out_half(u):
                        act.wait_ge(m["down"], n0 + (u + 1))
                        act.wait_ge(m[f"s{u % 2}"], 16 + h0 + 16 * (u // 2))
                        A_(ZT[:, u % 2, 0:512], bank(6), ACT.Copy).then_inc(m["ya"], 1)

                    for u in range(count):
                        act.wait_ge(m["t"], n0 + (u + 1))
                        if u >= 2:
                            act.wait_ge(m["gu"], n0 + (u - 1))
                        A_(XGT[:, u % 2, 0:512], bank(0), ACT.Copy).then_inc(m["xa"], 1)
                        if u >= 1:
                            out_half(u - 1)
                        act.wait_ge(m["gu"], n0 + (u + 1))
                        A_(SG[:, u % 2, :], bank(2 + u % 2)[:, 0:FF], ACT.Silu).then_inc(m["sg"], 1)
                    out_half(count - 1)
                emptied(act, "tb", l)
                for name in ("xa", "ya"):
                    act.sem_inc(m[name], 1)
                with act.Fori(0, NI) as i:
                    tiles(i * U, i * (8 * U), U)
                act.wait_ge(rt_ready, l + 1)
                pairs = act.value_load(RI[0:1, 0:1], min_val=0, max_val=NEXTRA // 2)
                with act.If(pairs > 0):
                    with act.Fori(0, pairs) as j:
                        tiles(j * 2 + NE, j * 16 + 8 * NE, 2)
                for t in range(NT):
                    ln_sqrt(10 * l + 5 + t)

        @block.vector
        def _(dve):
            steps = [0]
            V = nc.vector

            def chain(ins):
                steps[0] += 1
                ins.then_inc(vec_step, 1)
                dve.wait_ge(vec_step, steps[0])

            def mod_row(l, c):
                filled(dve, "mod", l, c)
                s = WITEM[("mod", l, c)]["slot"]
                dve.wait_ge(w_full[s], WITEM[("mod", l, c)]["value"])
                if l or c >= 2:
                    pl, pc = divmod(12 * l + c - 2, 12)
                    if pc < 4:
                        filled(dve, "modb", pl, pc)
                    else:
                        dve.wait_ge(d_mr[c % 2], 16 * rows_stored(pl, pc))
                release(V.scalar_tensor_tensor(out=MR[:, c % 2, :], in0=ps("mod", l, c)[0:2, 0:512],
                                               scalar=float(c // 2 == 4), in1=MB[s], op0=ALU.add, op1=ALU.add), "mod", l, c)

            def mod_columns(l, c):
                filled(dve, "modb", l, c)
                i, half = c // 2, c % 2
                src = ps("modb", l, c)[:, 0:8].rearrange("p (k g) -> p k g", g=2)
                release(V.tensor_scalar(MC[:, l, i, 4 * half:4 * half + 4, :], src, float(i), None, ALU.add), "modb", l, c)

            def drain_mod(kind, l, c):
                (mod_row if kind == "mod" else mod_columns)(l, c)

            def h_evac(l):
                for c in range(4):
                    emptied(dve, "modb", l, c)
                for k in range(1, KD, 2):
                    filled(dve, "xT", l, k)
                    for g, (a, b) in enumerate(((0, 512), (512, 640))):
                        ins = V.tensor_scalar(HT[:, k, a:b], ps("xT", l, k)[:, a:b], MC[:, l, 1, k, g:g + 1],
                                              MC[:, l, 0, k, g:g + 1], ALU.mult, ALU.add)
                    release(ins, "xT", l, k)

            filled(dve, "vec")
            chain(V.tensor_copy(CT[:, :], ps("vec")[:, 0:16]))
            chain(V.tensor_copy(VC[:, :], ps("vec")[:, 16:59]))
            ins = V.tensor_copy(CW[:, :], ps("vec")[:, 64:188])
            release(ins, "vec")
            chain(V.tensor_tensor(LBS[:, 2, :], VC[:, 0:8], VC[:, 8:16], ALU.max))
            chain(V.tensor_tensor(LBS[:, 0, :], VC[:, 0:8], LBS[:, 2, :], ALU.subtract))
            V.tensor_tensor(LBS[:, 1, :], VC[:, 8:16], LBS[:, 2, :], ALU.subtract).then_inc(lb_exp_in, 1)
            dve.wait_ge(lb_exp, 1)
            chain(V.tensor_tensor(LBS[:, 2, :], LBS[:, 0, :], LBS[:, 1, :], ALU.add))
            chain(V.reciprocal(LBS[:, 2, :], LBS[:, 2, :]))
            chain(V.tensor_tensor(LBT[:, 0, :], LBS[:, 0, :], LBS[:, 2, :], ALU.mult))
            chain(V.tensor_tensor(LBT[:, 1, :], LBS[:, 1, :], LBS[:, 2, :], ALU.mult))
            dve.wait_ge(d_const, 16)
            for k in range(2):
                for t in range(NT):
                    for c in range(2):
                        ins = V.tensor_scalar(PAY[:, k, t, c:c + 1], const("pidx"), 128.0 * t + k * c * NTOK, None, ALU.add)
            chain(ins)
            V.memset(NOR[:, :], NOROW).then_inc(const_ready, 1)
            for kind, c in FIRST_MODS:
                drain_mod(kind, 0, c)
            h_evac(0)

            dve.wait_ge(sq_ready, NT)
            chain(V.tensor_scalar(RR[:, :, 0:1], SS[:, :, 0:1], 1.0 / QR, RMS_EPS, ALU.mult, ALU.add))
            V.tensor_scalar(RR[:, :, 1:2], SS[:, :, 1:2], 1.0 / KVR, RMS_EPS, ALU.mult, ALU.add).then_inc(rms_in, 1)
            dve.wait_ge(rms_sd, 1)
            chain(V.reciprocal(RR[:, :, :], RR[:, :, :]))
            dve.wait_ge(d_rows, 32)
            for t in (4, 0, 1, 2, 3):
                V.tensor_scalar(CQ[:, t, 0:QR], CQ[:, t, 0:QR], RR[:, t, 0:1], None, ALU.mult)
                V.scalar_tensor_tensor(out=CQ[:, t, QR:QR + KVR], in0=CQ[:, t, QR:QR + KVR], scalar=RR[:, t, 1:2],
                                       in1=CKG[:, :], op0=ALU.mult, op1=ALU.mult).then_inc(norm_ready, 1)
            for r in range(3):
                filled(dve, "cqT", r)
                release(V.tensor_scalar(CQT[:, r, :], ps("cqT", r)[:, 0:640], VC[:, 16 + r:17 + r], None, ALU.mult), "cqT", r)
            filled(dve, "krT")
            rp = slice(64, 96)
            chain(V.tensor_copy(KT[rp, 0, 512:768], ps("krT")[rp, 512:768]))
            chain(V.tensor_copy(KT[rp, 1, 512:768], ps("krT")[rp, 512:768]))
            release(V.tensor_copy(KRS[rp, :], ps("krT")[rp, 0:512]), "krT")
            emptied(dve, "krT")
            cosr, sinr = const("cos", rp), const("sin", rp)
            filled(dve, "krP")
            release(V.tensor_tensor(ROT1[rp, :], ps("krP")[rp, 0:512], sinr, ALU.mult), "krP")
            chain(V.tensor_tensor(ROT2[rp, :], KRS[rp, :], cosr, ALU.mult))
            emptied(dve, "krP")
            V.tensor_tensor(KT[rp, 0, 0:512], ROT1[rp, :], ROT2[rp, :], ALU.add).then_inc(kr_ready, 1)
            V.tensor_tensor(KT[rp, 1, 0:512], ROT1[rp, :], ROT2[rp, :], ALU.add).then_inc(kr_ready, 1)
            dve.wait_ge(kr_ready, 2)

            def rotate_q(h):
                b = h % 2
                filled(dve, "qP", h)
                release(V.tensor_tensor(ROT1[rp, :], ps("qP", h)[rp, 0:512], sinr, ALU.mult), "qP", h)
                emptied(dve, "q", h)
                chain(V.tensor_tensor(ROT2[rp, :], QT[rp, b, 0:512], cosr, ALU.mult))
                emptied(dve, "qP", h)
                V.tensor_tensor(QT[rp, b, 0:512], ROT1[rp, :], ROT2[rp, :], ALU.add).then_inc(q_rot, 1)
                dve.wait_ge(q_rot, h + 1)

            def attend_out(n):
                h, t = divmod(n, NT)
                b = n % 2
                filled(dve, "o", h, t)
                emptied(dve, "s", h, t)
                chain(V.reciprocal(SUM[:, b, 1:2], SUM[:, b, 0:1]))
                release(V.tensor_scalar(OB[:, t, h * 64:h * 64 + 64], ps("o", h, t)[:, 0:64], SUM[:, b, 1:2], None,
                                        ALU.mult), "o", h, t)

            rotate_q(0)
            n = 0
            for h in range(MH):
                for t in range(NT):
                    nk = 640 if t < 4 else 128
                    b = n % 2
                    filled(dve, "s", h, t)
                    if n >= 2:
                        emptied(dve, "s", *divmod(n - 2, NT))
                    chain(V.tensor_reduce(MXS[:, b, 0:1], ps("s", h, t)[:, 0:nk], AX.X, ALU.max, negate=True))
                    V.tensor_scalar(MXS[:, b, 1:2], MXS[:, b, 0:1], SCALE, None, ALU.mult).then_inc(max_ready, 1)
                    if n >= 1:
                        attend_out(n - 1)
                    if t == ATTN_MOD_TILE + 1:
                        mod_row(0, 4 + h)
                    if h + 1 < MH and t == 3:
                        rotate_q(h + 1)
                    n += 1
            attend_out(n - 1)

            for t in range(NT):
                filled(dve, "hv", 0, t)
                release(V.tensor_copy(HV[:, t, :], ps("hv", 0, t)[:, 0:512]), "hv", 0, t)
            dve.wait_ge(h_zero, 3)
            scan_mask = const("scan")
            for u in range(4):
                d, hp = u // 2, u % 2
                F = HF[d][:, 2 * hp:2 * hp + 2, :]
                emptied(dve, "hq", 1 + d, 2 * hp + 1)
                for hh in range(2):
                    hd = d * 4 + 2 * hp + hh
                    ins = V.tensor_scalar(F[:, hh, :], F[:, hh, :], LBT[:, 1, hd:hd + 1], LBT[:, 0, hd:hd + 1], ALU.mult, ALU.add)
                    if hh == 0:
                        chain(ins)
                ins.then_inc(h_f, 1)
                dve.wait_ge(h_l, u + 1)
                if u >= 2:
                    emptied(dve, "ho", u - 2, 4)
                chain(V.tensor_scalar(F, F, -1.0, 1.0, ALU.mult, ALU.add))
                for hh in range(2):
                    ins = V.tensor_tensor_scan(BUFB[:, hh, :], scan_mask, BUFL[:, hh, :], 0.0, ALU.mult, ALU.add)
                    chain(ins)
                B4 = BUFB[:, :, :].rearrange("p h (c s) -> p (h c) s", s=CH)
                A4 = BUFA[:, :, :].rearrange("p h (c s) -> p (h c) s", s=CH)
                L4 = BUFL[:, :, :].rearrange("p h (c s) -> p (h c) s", s=CH)
                if d == 0:
                    chain(V.tensor_tensor(A4, B4, B4[:, :, 15:16].to_broadcast([128, 40, CH]), ALU.subtract))
                    V.tensor_tensor(L4, B4[:, :, 31:32].to_broadcast([128, 40, CH]), B4, ALU.subtract).then_inc(h_arg, 1)
                else:
                    chain(V.tensor_tensor(L4, B4, L4, ALU.subtract))
                    chain(V.tensor_tensor(A4, B4[:, :, 31:32].to_broadcast([128, 40, CH]), L4, ALU.subtract))
                    V.tensor_tensor(B4, A4, A4[:, :, 16:17].to_broadcast([128, 40, CH]), ALU.subtract).then_inc(h_arg, 1)
                drain_mod(*UNIT_MODS[u][0])
                Q = HQ[:, 2 * hp:2 * hp + 2, :]
                for k, (dst, src) in enumerate(((QHAT, Q), (KHAT, F), (KTIL, F), (QTIL, Q))):
                    dve.wait_ge(h_exp, 5 * u + k + 1)
                    V.tensor_tensor(dst[:, :, :], dst[:, :, :], src, ALU.mult).then_inc(h_mul, 1)
                drain_mod(*UNIT_MODS[u][1])
                dve.wait_ge(h_exp, 5 * u + 5)
                dve.wait_ge(h_s0, 16 * (u + 1))

                def out_add(n):
                    t = (3 - n) if n < 4 else 4
                    filled(dve, "ho", u, n)
                    dst = HO[:, t, 256 * hp:256 * hp + 256]
                    release(V.tensor_tensor(dst, ps("ho", u, n)[:, 0:256], dst, ALU.add), "ho", u, n)
                mask = const("mask_f" if d == 0 else "mask_b").bitcast(i32).unsqueeze(1).to_broadcast([128, 2, 128])
                for n in range(NT):
                    i = 5 * u + n
                    t = (n if d == 0 else 3 - n) if n < 4 else 4
                    if i >= 2:
                        filled(dve, "ho", *divmod(i - 2, 5))
                    filled(dve, "hs", u, n)
                    release(V.copy_predicated(SC[:, d, i % 2, :, :], mask,
                                              ps("hs", u, n)[:, 0:256].rearrange("p (h t) -> p h t", h=2)), "hs", u, n)
                    filled(dve, "hd", u, n)
                    if i >= 3:
                        if n == 2 and u >= 1:
                            dve.wait_ge(d_state, 16 * u)
                    for step in range(4):
                        j = step if d == 0 else 3 - step
                        for hh in range(2):
                            prev = state_before(i, n, step, hh)
                            nxt = ST[:, i % 2, hh, step, :] if step < 3 else CAR[:, i % 3, hh, :]
                            ins = V.scalar_tensor_tensor(out=nxt, in0=prev, scalar=DEC[:, hh, t * 4 + j:t * 4 + j + 1],
                                                         in1=ps("hd", u, n)[:, hh * 512 + j * 128:hh * 512 + (j + 1) * 128],
                                                         op0=ALU.mult, op1=ALU.add)
                            if step == 3 and hh == 1:
                                release(ins, "hd", u, n)
                            elif hh == 1 or step == 3:
                                chain(ins)
                            else:
                                steps[0] += 1
                                ins.then_inc(vec_step, 1)
                    emptied(dve, "hd", u, n)
                    if d == 1 and n >= 1:
                        out_add(n - 1)
                    for piece in STEP_MODS.get((u, n - 1), []):
                        drain_mod(*piece)
                if d == 1:
                    out_add(4)
            emptied(dve, "ho", 3, 4)
            for t in range(NT):
                emptied(dve, "hv", 1, t)
            SQB = HTF[:, 0:2560]
            HOF, HGF = z(12800, 2560), z(10240, 2560)
            chain(V.tensor_tensor(SQB, HOF, HOF, ALU.mult))
            chain(V.tensor_reduce(HSS[:, :], SQB.rearrange("p (g v) -> p g v", v=128), AX.X, ALU.add))
            V.tensor_scalar(HSS[:, :], HSS[:, :], 1.0 / DK, RMS_EPS, ALU.mult, ALU.add).then_inc(o_var, 1)
            HG3 = HGF.rearrange("p (g v) -> p g v", v=128)
            HO3 = HOF.rearrange("p (g v) -> p g v", v=128)
            chain(V.tensor_tensor(HG3, HG3, HNG[:, :].unsqueeze(1).to_broadcast([128, 20, 128]), ALU.mult))
            dve.wait_ge(o_sd, 1)
            chain(V.reciprocal(HSS[:, :], HSS[:, :]))
            chain(V.tensor_tensor(HO3, HO3, HSS[:, :].unsqueeze(2).to_broadcast([128, 20, 128]), ALU.mult))
            V.tensor_tensor(HOF, HOF, HGF, ALU.mult).then_inc(o_ready, 1)

            def ln_first(q):
                b = q % 2
                for s in range(2):
                    V.bn_stats(ST6[:, b, s, :], ZT[:, b, s * 512:s * 512 + 512]).then_inc(vec_step, 1)
                    steps[0] += 1
                dve.wait_ge(vec_step, steps[0])
                chain(V.bn_aggr(MV[:, b, :], ST6[:, b, :, :]))
                V.tensor_scalar(RSD[:, b, 0:1], MV[:, b, 1:2], LN_EPS, None, ALU.add).then_inc(ln_var, 1)

            def ln_second(q, t, k):
                b = q % 2
                dve.wait_ge(ln_sd, q + 1)
                chain(V.reciprocal(RSD[:, b, 1:2], RSD[:, b, 0:1]))
                chain(V.tensor_scalar(ZT[:, b, :], ZT[:, b, :], MV[:, b, 0:1], RSD[:, b, 1:2], ALU.subtract, ALU.mult))
                if k % 2 == 0:
                    dve.wait_ge(d_ln, 16 * (k + 2))
                chain(V.tensor_tensor(ZT[:, b, :], ZT[:, b, :], LNR[:, 0, :], ALU.mult))
                V.tensor_tensor(X[:, t, :], ZT[:, b, :], LNR[:, 1, :], ALU.add).then_inc(x_ready, 1)
                dve.wait_ge(x_ready, q + 1)

            def first_max(src, n, prio, out, tmp, mx):
                chain(V.tensor_reduce(mx, src, AX.X, ALU.max))
                mb = mx.unsqueeze(2).to_broadcast([128, NT, n])
                chain(V.tensor_tensor(out, src, mb, ALU.is_equal))
                chain(V.tensor_tensor(out, out, prio.unsqueeze(1).to_broadcast([128, NT, n]), ALU.mult))
                chain(V.tensor_reduce(tmp, out, AX.X, ALU.max))
                chain(V.tensor_tensor(out, out, tmp.unsqueeze(2).to_broadcast([128, NT, n]), ALU.is_equal))

            def gated_convolutions():
                segs = ((0, 15, 512), (512, 542, 128))
                for j in range(4):
                    emptied(dve, "cd", 4, j)
                    for t0, p0, w in segs:
                        ins = V.tensor_tensor(UP[:, j, p0:p0 + w], UP[:, j, p0:p0 + w], CO[:, j, t0:t0 + w], ALU.mult)
                ins.then_inc(cd_up, 1)
                dve.wait_ge(cd_up, 1)
                V.memset(CO[:, :, 655:656], 0.0)
                for k in range(CFK - PE_TAPS):
                    for j in range(4):
                        src = UP[:, j, k:k + 655]
                        tap = CW[:, 4 * k + j:4 * k + j + 1]
                        dst = CO[:, j, 0:655]
                        if k == 0:
                            ins = V.tensor_scalar(dst, src, tap, VC[:, 19 + j:20 + j], ALU.mult, ALU.add)
                        else:
                            ins = V.scalar_tensor_tensor(out=dst, in0=src, scalar=tap, in1=dst, op0=ALU.mult, op1=ALU.add)
                    chain(ins)
                emptied(dve, "cd", 2, 3)
                for t0, p0, w in segs:
                    ins = V.tensor_tensor(CXP[:, :, p0:p0 + w], SQ[:, :, t0:t0 + w], CXP[:, :, p0:p0 + w], ALU.mult)
                chain(ins)
                for k in range(SCK):
                    for j in range(4):
                        for t0, p0, w in segs:
                            src = CXP[:, j, p0 + k - 1:p0 + k - 1 + w]
                            tap = VC[:, 31 + 4 * k + j:32 + 4 * k + j]
                            dst = OT[:, j, t0:t0 + w]
                            if k == 0:
                                ins = V.tensor_scalar(dst, src, tap, None, ALU.mult)
                            else:
                                ins = V.scalar_tensor_tensor(out=dst, in0=src, scalar=tap, in1=dst, op0=ALU.mult, op1=ALU.add)
                    chain(ins)
                V.tensor_tensor(OT[:, 0:4, :], OT[:, 0:4, :], BG[:, :, :], ALU.mult).then_inc(cd_out_v, 1)
                for j in range(4):
                    filled(dve, "cv", j)
                    V.tensor_tensor(CO[:, j, 0:512], ps("cv", j)[:, 0:512], CO[:, j, 0:512], ALU.add).then_inc(cd_conv, 1)
                    release(V.tensor_tensor(CO[:, j, 527:655], ps("cv", j)[:, 512:640], CO[:, j, 527:655], ALU.add), "cv", j)
                emptied(dve, "cv", 3)

                def two(ap):
                    return ap.rearrange("p (b c) -> p b c", b=2)
                filled(dve, "mean")
                mean = two(ps("mean"))[:, :, 0:328]
                dve.wait_ge(cd_conv, 4)
                for j in range(4):
                    ins = V.scalar_tensor_tensor(out=two(CO[:, j, :]), in0=mean, scalar=-1.0 / 512, in1=two(CO[:, j, :]),
                                                 op0=ALU.mult, op1=ALU.add)
                release(ins, "mean")
                emptied(dve, "mean")
                filled(dve, "var")
                release(V.tensor_scalar(two(RST), two(ps("var"))[:, :, 0:328], 1.0 / 512, LN_EPS, ALU.mult, ALU.add), "var")
                dve.wait_ge(cd_sd, 1)
                chain(V.reciprocal(RST, RST))
                for j in range(4):
                    V.tensor_tensor(CO[:, j, :], CO[:, j, :], RST, ALU.mult).then_inc(cd_u, 1)

            for l in range(2):
                m = MS[l]
                if l == 1:
                    V.memset(CXP[:, :, :], 0.0).then_inc(cd_pad, 1)
                    V.memset(UP[:, :, :], 0.0).then_inc(cd_pad, 1)
                    h_evac(1)
                    gated_convolutions()
                if l == 0:
                    dve.wait_ge(d_xr, 32)
                dve.wait_ge(d_g1, 16 * (l + 1))

                def mod_for_experts(t):
                    b, g = t % 2, (0 if t < 4 else 1)
                    if t == 0:
                        dve.wait_ge(d_r, 48 * (l + 1))
                    if t >= 2:
                        filled(dve, "hT", l, t - 2)
                        dve.wait_ge(d_hst[b], 16 * ((3 if b == 0 else 2) * l + (t - 2) // 2 + 1))
                    chain(V.tensor_tensor(HB[:, b, :], X[:, t, :], R4[:, g, :], ALU.mult))
                    V.tensor_tensor(HB[:, b, :], HB[:, b, :], R3[:, g, :], ALU.add).then_inc(h_ready, 1)

                for t in range(NT):
                    q, g = 10 * l + t, (0 if t < 4 else 1)
                    b = q % 2
                    filled(dve, "y", l, t)
                    release(V.tensor_tensor(ZT[:, b, :], ps("y", l, t), G1[:, g, :], ALU.mult), "y", l, t)
                    emptied(dve, "y", l, t)
                    chain(V.scalar_tensor_tensor(out=ZT[:, b, :], in0=X[:, t, :], scalar=ALPHA, in1=ZT[:, b, :],
                                                 op0=ALU.mult, op1=ALU.add))
                    ln_first(q)
                    if t >= 1:
                        ln_second(q - 1, t - 1, 2 * l)
                        mod_for_experts(t - 1)
                ln_second(10 * l + 4, 4, 2 * l)
                mod_for_experts(4)

                filled(dve, "lg", l)
                release(V.tensor_copy(LG[:, :, :], ps("lg", l)[:, 0:180].rearrange("p (t c) -> p t c", t=NT)), "lg", l)
                emptied(dve, "lg", l)
                gl, el = LG[:, :, 0:4], LG[:, :, 4:36]
                gm, tmp, m1, m2, sume, ex, pg = [RS[:, i, 0:5] for i in range(7)]
                first_max(gl, 4, const("prio4"), O4[:, :, :], tmp, gm)
                D4 = RT[:, 0, 0:20].rearrange("p (t g) -> p t g", t=NT)
                V.tensor_tensor(D4, gl, gm.unsqueeze(2).to_broadcast([128, NT, 4]), ALU.subtract).then_inc(rt_exp_in, 1)
                E4 = RT[:, 1, :].rearrange("p (t g e) -> p t g e", t=NT, g=4)
                o4b = O4[:, :, :].unsqueeze(3).to_broadcast([128, NT, 4, 8])
                chain(V.tensor_tensor(E4, el.rearrange("p t (g e) -> p t g e", g=4), o4b, ALU.mult))
                EI = RT[:, 2, 0:40].rearrange("p (t e) -> p t e", t=NT)
                chain(V.tensor_reduce(EI, RT[:, 1, :].rearrange("p (t g e) -> p t e g", t=NT, g=4), AX.X, ALU.add))
                O1 = RT[:, 2, 40:80].rearrange("p (t e) -> p t e", t=NT)
                O2 = RT[:, 2, 80:120].rearrange("p (t e) -> p t e", t=NT)
                first_max(EI, 8, const("prio8"), O1, tmp, m1)
                chain(V.scalar_tensor_tensor(out=RT[:, 2, 0:40], in0=RT[:, 2, 40:80], scalar=-3.0e38, in1=RT[:, 2, 0:40],
                                             op0=ALU.mult, op1=ALU.add))
                first_max(EI, 8, const("prio8"), O2, tmp, m2)
                V.tensor_tensor(ex, m2, m1, ALU.subtract).then_inc(rt_exp_in, 1)
                dve.wait_ge(rt_exp, 2 * l + 2)
                chain(V.tensor_reduce(sume, D4, AX.X, ALU.add))
                chain(V.tensor_scalar(pg, ex, 1.0, None, ALU.add))
                chain(V.tensor_tensor(pg, pg, sume, ALU.mult))
                chain(V.reciprocal(W12[:, 0, :], pg))
                chain(V.tensor_tensor(W12[:, 1, :], W12[:, 0, :], ex, ALU.mult))
                M1 = RT[:, 3, :].rearrange("p (t g e) -> p t g e", t=NT, g=4)
                M2 = RT[:, 4, :].rearrange("p (t g e) -> p t g e", t=NT, g=4)
                chain(V.tensor_tensor(M1, o4b, O1.unsqueeze(2).to_broadcast([128, NT, 4, 8]), ALU.mult))
                chain(V.tensor_tensor(M2, o4b, O2.unsqueeze(2).to_broadcast([128, NT, 4, 8]), ALU.mult))
                V.tensor_tensor(RT[:, 5, :], RT[:, 3, :], RT[:, 4, :], ALU.add).then_inc(rt_mask, 1)
                filled(dve, "ct", l)
                chain(V.memset(RUN[:, :], 0.0))
                for t in range(NT):
                    chain(V.tensor_tensor(CM[:, t, :], ps("ct", l)[:, t * 32:t * 32 + 32], RUN[:, :], ALU.add))
                    ins = V.tensor_tensor(RUN[:, :], ps("ct", l)[:, 512 + t * 32:512 + t * 32 + 32], RUN[:, :], ALU.add)
                    if t == NT - 1:
                        release(ins, "ct", l)
                        emptied(dve, "ct", l)
                    else:
                        chain(ins)
                for k in range(1, NT):
                    ins = V.tensor_scalar(IND[:, 32 * (k - 1):32 * k], RUN[:, :], 128.0 * k, None, ALU.is_gt)
                chain(ins)
                chain(V.tensor_tensor_scan(INC, const("ones"), IND, 0.0, ALU.mult, ALU.add))
                V.tensor_copy(BASE[:, 0:32], const("e128"))
                chain(V.tensor_tensor(BASE[:, 32:160], INC, IND, ALU.subtract))
                for k in range(1, NT):
                    blk = BASE[:, 32 * k:32 * k + 32]
                    ins = V.tensor_scalar(blk, blk, 128.0, 128.0 * (NE - k), ALU.mult, ALU.add)
                chain(ins)
                chain(V.tensor_tensor(DELTA, BASE[:, 32:160], BASE[:, 0:128], ALU.subtract))
                G3 = GG.rearrange("p (t e) -> p t e", t=NT)
                T3 = GT.rearrange("p (t e) -> p t e", t=NT)
                chain(V.tensor_tensor(G3, CM[:, :, :], const("e128").unsqueeze(1).to_broadcast([128, NT, NE]), ALU.add))
                for k in range(1, NT):
                    dk = DELTA[:, 32 * (k - 1):32 * k].unsqueeze(1).to_broadcast([128, NT, NE])
                    chain(V.scalar_tensor_tensor(out=T3, in0=CM[:, :, :], scalar=128.0 * k, in1=dk, op0=ALU.is_ge, op1=ALU.mult))
                    chain(V.tensor_tensor(GG, GG, GT, ALU.add))
                for k in range(2):
                    chain(V.tensor_tensor(GT, GG, RT[:, 3 + k, :], ALU.mult))
                    ins = V.tensor_reduce(GF[:, k, :], T3, AX.X, ALU.add)
                    chain(ins)
                V.tensor_copy(GI[:, :, :], GF[:, :, :]).then_inc(rt_slots, 1)
                ev = const("evens")
                chain(V.tensor_tensor(RS[:, 8, 0:5], INC[:, 127:128].to_broadcast([128, 5]), ev, ALU.is_gt))
                chain(V.tensor_reduce(RS[:, 7, 0:1], RS[:, 8, 0:5], AX.X, ALU.add))
                chain(V.tensor_copy(RI[:, :], RS[:, 7, 0:1]))
                chain(V.tensor_tensor(DELTA, INC, IND, ALU.subtract))
                chain(V.tensor_tensor(EXW, DELTA.unsqueeze(1).to_broadcast([128, NEXTRA, 128]),
                                      const("iota")[:, 0:NEXTRA].unsqueeze(2).to_broadcast([128, NEXTRA, 128]), ALU.is_equal))
                chain(V.tensor_tensor(IND.rearrange("p (k e) -> p k e", e=NE), IND.rearrange("p (k e) -> p k e", e=NE),
                                      const("iota")[:, 0:NE].unsqueeze(1).to_broadcast([128, 4, NE]), ALU.mult))
                chain(V.tensor_tensor(EXW, EXW, IND.unsqueeze(1).to_broadcast([128, NEXTRA, 128]), ALU.mult))
                chain(V.tensor_reduce(EXF, EXW, AX.X, ALU.add))
                V.tensor_copy(EXI[:, :], EXF).then_inc(rt_ready, 1)
                filled(dve, "tb", l)
                chain(V.tensor_copy(TI[:, :], ps("tb", l)[:, 0:NTILE]))
                release(V.tensor_copy(TY[:, :], ps("tb", l)[:, NTILE:2 * NTILE]), "tb", l)

                def tiles(n0, h0, count):
                    def down_in(u):
                        dve.wait_ge(m["ht"], n0 + (u + 1))
                        V.tensor_copy(HIDT[:, u % 2, :], bank(4 + u % 2)[:, 0:128]).then_inc(m["hidt"], 1)

                    def out_half(u):
                        dve.wait_ge(m["down"], n0 + (u + 1))
                        dve.wait_ge(m[f"s{u % 2}"], 16 + h0 + 16 * (u // 2))
                        V.tensor_copy(ZT[:, u % 2, 512:1024], bank(7)).then_inc(m["yv"], 1)

                    for u in range(count):
                        dve.wait_ge(m["t"], n0 + (u + 1))
                        if u >= 2:
                            dve.wait_ge(m["gu"], n0 + (u - 1))
                        V.tensor_copy(XGT[:, u % 2, 512:1024], bank(1)).then_inc(m["xv"], 1)
                        if u >= 1:
                            down_in(u - 1)
                            out_half(u - 1)
                        dve.wait_ge(m["sg"], n0 + (u + 1))
                        V.tensor_tensor(HID[:, u % 2, :], bank(2 + u % 2)[:, FF:2 * FF], SG[:, u % 2, :],
                                        ALU.mult).then_inc(m["hid"], 1)
                    down_in(count - 1)
                    out_half(count - 1)
                for name in ("xv", "yv"):
                    dve.sem_inc(m[name], 1)
                dve.wait_ge(rt_ready, l + 1)
                pairs = dve.value_load(RI[0:1, 0:1], min_val=0, max_val=NEXTRA // 2)
                with dve.Fori(0, NI) as i:
                    tiles(i * U, i * (8 * U), U)
                with dve.If(pairs > 0):
                    with dve.Fori(0, pairs) as j:
                        tiles(j * 2 + NE, j * 16 + 8 * NE, 2)
                dve.wait_ge(moe_done, l + 1)
                for t in range(NT):
                    q, g = 10 * l + 5 + t, (0 if t < 4 else 1)
                    b, yb = q % 2, t % 2
                    cnt = ((3 if yb == 0 else 2) * l + t // 2 + 1) * 32
                    dve.wait_ge(d_yl[yb], cnt)
                    chain(V.tensor_scalar(YB[:, yb, 0, :], YB[:, yb, 0, :], W12[:, 0, t:t + 1], None, ALU.mult))
                    chain(V.scalar_tensor_tensor(out=YB[:, yb, 0, :], in0=YB[:, yb, 1, :], scalar=W12[:, 1, t:t + 1],
                                                 in1=YB[:, yb, 0, :], op0=ALU.mult, op1=ALU.add))
                    V.tensor_tensor(ZT[:, b, :], YB[:, yb, 0, :], R5[:, g, :], ALU.mult).then_inc(y_used, 1)
                    dve.wait_ge(y_used, 5 * l + t + 1)
                    chain(V.scalar_tensor_tensor(out=ZT[:, b, :], in0=X[:, t, :], scalar=ALPHA, in1=ZT[:, b, :],
                                                 op0=ALU.mult, op1=ALU.add))
                    ln_first(q)
                    if t >= 1:
                        ln_second(q - 1, t - 1, 2 * l + 1)
                ln_second(10 * l + 9, 4, 2 * l + 1)

        @block.tensor
        def _(pe):
            T = nc.tensor

            def mod_product(l, c, lo=0, hi=KD):
                if lo == 0:
                    weights(pe, "mod", l, c)
                    open_group(pe, "mod", l, c)
                w = slot3(WITEM[("mod", l, c)]["slot"]).rearrange("p (k n) -> p k n", k=8)
                for k in range(lo, hi):
                    ins = T.matmul(ps("mod", l, c)[0:2, 0:512], CT[:, :].rearrange("p (g k) -> p k g", g=2)[:, k, :],
                                   w[:, k, :], start=(k == 0), stop=(k == KD - 1))
                if hi == KD:
                    close_group(ins, "mod", l, c)

            def mod_turn(l, c):
                emptied(pe, "mod", l, c)
                open_group(pe, "modb", l, c)
                for b in range(4):
                    ins = T.matmul(ps("modb", l, c)[:, 2 * b:2 * b + 2], MR[:, c % 2, b * 128:b * 128 + 128],
                                   C[0:2, 0:2], start=True, stop=True)
                close_group(ins, "modb", l, c)

            def side(kind, l, c):
                (mod_product if kind == "mod" else mod_turn)(l, c)

            def x_transposes(l):
                for k in range(KD):
                    open_group(pe, "xT", l, k)
                    for t in range(NT):
                        ins = T.transpose(ps("xT", l, k)[:, t * 128:t * 128 + 128], X[:, t, k * 128:k * 128 + 128], ident)
                    close_group(ins, "xT", l, k)
                for k in range(KD):
                    emptied(pe, "xT", l, k)

            def project_cm(name, w, col):
                open_group(pe, *name)
                for a, b in ((0, 512), (512, 640)):
                    for k in range(KD):
                        ins = T.matmul(ps(*name)[:, a:b], w[:, k, col:col + 128], HT[:, k, a:b],
                                       start=(k == 0), stop=(k == KD - 1))
                close_group(ins, *name)

            def project_tm(name, src, t, parts):
                open_group(pe, *name)
                for at, w in parts:
                    for k in range(KD):
                        ins = T.matmul(ps(*name)[:, at:at + w.shape[2]], src[:, k, t * 128:t * 128 + 128], w[:, k, :],
                                       start=(k == 0), stop=(k == KD - 1))
                close_group(ins, *name)

            def w8(words, n=512):
                return words[:, 0:8 * n].rearrange("p (k n) -> p k n", k=8)

            pe.wait_ge(d_const, 16)
            pe.wait_ge(d_vec, 16 * 9)
            pe.wait_ge(c_silu, 1)
            v = ps("vec")
            T.matmul(v[:, 0:16], V1[:, :], C[0:16, 0:16], start=True, stop=True)
            T.matmul(v[:, 16:59], V2[:, :], C[0:43, 0:43], start=True, stop=True)
            close_group(T.matmul(v[:, 64:188], V3[:, :], C[0:124, 0:124], start=True, stop=True), "vec")
            emptied(pe, "vec")
            for kind, c in FIRST_MODS:
                side(kind, 0, c)
            pe.wait_ge(d_x, 32)
            x_transposes(0)

            wa, wb = w8(weights(pe, "cqa")), w8(weights(pe, "cqb"), AB_IN - 3072)
            for t in range(NT):
                project_tm(("cq", t), HT, t, [(0, wa), (512, wb)])
            pe.wait_ge(norm_ready, NT)
            pe.wait_ge(d_cache, 32)
            for r in range(3):
                open_group(pe, "cqT", r)
                for t in range(NT):
                    ins = T.transpose(ps("cqT", r)[:, t * 128:t * 128 + 128], CQ[:, t, r * 128:r * 128 + 128], ident)
                close_group(ins, "cqT", r)
            for r in range(2):
                open_group(pe, "ckvT", r)
                srcs = [CQ[:, t, QR + r * 128:QR + r * 128 + 128] for t in range(4)]
                srcs += [CC[:, r * 128:r * 128 + 128], CQ[:, 4, QR + r * 128:QR + r * 128 + 128]]
                for t, src in enumerate(srcs):
                    ins = T.transpose(ps("ckvT", r)[:, t * 128:t * 128 + 128], src, ident)
                close_group(ins, "ckvT", r)
            open_group(pe, "krT")
            srcs = [CQ[:, t, 640:672] for t in range(4)] + [CC[:, KVR:288], CQ[:, 4, 640:672]]
            for t, src in enumerate(srcs):
                ins = T.matmul(ps("krT")[64:96, t * 128:t * 128 + 128], src, ident, start=True, stop=True)
            close_group(ins, "krT")
            perm = const("perm", slice(64, 96))
            emptied(pe, "krT")
            open_group(pe, "krP")
            close_group(T.matmul(ps("krP")[64:96, 0:512], perm, KRS[64:96, :], start=True, stop=True), "krP")
            uq = weights(pe, "uq")[:, 0:2304].rearrange("p (k n) -> p k n", k=3)
            ukv = weights(pe, "ukv")[:, 0:2048].rearrange("p (k n) -> p k n", k=2)
            for r in range(2):
                emptied(pe, "ckvT", r)
            wv = ukv.rearrange("p k (h c) -> p k h c", h=8)[:, :, :, 64:128]
            for t in range(6):
                open_group(pe, "v", t)
                for r in range(2):
                    ins = T.matmul(ps("v", t)[:, 0:512].rearrange("p (h c) -> p h c", h=8),
                                   CKVT[:, r, t * 128:t * 128 + 128], wv[:, r], start=(r == 0), stop=(r == 1))
                close_group(ins, "v", t)
            for r in range(3):
                emptied(pe, "cqT", r)

            def keys_queries(h):
                open_group(pe, "k", h)
                for a, b in ((0, 512), (512, 768)):
                    for r in range(2):
                        ins = T.matmul(ps("k", h)[0:64, a:b], ukv[:, r, h * 128:h * 128 + 64], CKVT[:, r, a:b],
                                       start=(r == 0), stop=(r == 1))
                close_group(ins, "k", h)
                open_group(pe, "q", h)
                for a, b in ((0, 512), (512, 640)):
                    for r in range(3):
                        ins = T.matmul(ps("q", h)[0:96, a:b], uq[:, r, h * 96:h * 96 + 96], CQT[:, r, a:b],
                                       start=(r == 0), stop=(r == 2))
                close_group(ins, "q", h)

            def swap_pairs(h):
                emptied(pe, "q", h)
                open_group(pe, "qP", h)
                close_group(T.matmul(ps("qP", h)[64:96, 0:512], perm, QT[64:96, h % 2, 0:512], start=True, stop=True), "qP", h)

            def scores(h, t):
                if t == 0:
                    emptied(pe, "k", h)
                    pe.wait_ge(q_rot, h + 1)
                    pe.wait_ge(kr_ready, 2)
                open_group(pe, "s", h, t)
                q = QT[0:96, h % 2, t * 128:t * 128 + 128]
                for a, b in (((0, 512), (512, 640)) if t < 4 else ((0, 128),)):
                    ka = a if t < 4 else 640
                    ins = T.matmul(ps("s", h, t)[:, a:b], q, KT[0:96, h % 2, ka:ka + b - a], start=True, stop=True)
                close_group(ins, "s", h, t)

            for t in range(6):
                emptied(pe, "v", t)
            keys_queries(0)
            swap_pairs(0)
            steps = [(h, t) for h in range(MH) for t in range(NT)]
            scores(0, 0)
            for n, (h, t) in enumerate(steps):
                if h + 1 < MH and t == 0:
                    keys_queries(h + 1)
                if h + 1 < MH and t == 2:
                    swap_pairs(h + 1)
                if n + 1 < len(steps):
                    scores(*steps[n + 1])
                if t == ATTN_MOD_TILE:
                    mod_product(0, 4 + h, 0, KD // 2)
                blocks = [0, 1, 2, 3, 4] if t < 4 else [5]
                emptied(pe, "s", h, t)
                open_group(pe, "pt", h, t)
                for j, kb in enumerate(blocks):
                    ins = T.transpose(ps("pt", h, t)[:, j * 128:j * 128 + 128], PB[:, n % 2, j * 128:j * 128 + 128], ident)
                close_group(ins, "pt", h, t)
                if t == ATTN_MOD_TILE:
                    mod_product(0, 4 + h, KD // 2, KD)
                emptied(pe, "pt", h, t)
                open_group(pe, "o", h, t)
                for j, kb in enumerate(blocks):
                    ins = T.matmul(ps("o", h, t)[:, 0:64], PTS[:, n % 2, j * 128:j * 128 + 128], VT[:, kb, h * 64:h * 64 + 64],
                                   start=(j == 0), stop=(j == len(blocks) - 1))
                close_group(ins, "o", h, t)
            emptied(pe, "o", MH - 1, NT - 1)
            for j in range(4):
                open_group(pe, "obT", j)
                for t in range(NT):
                    ins = T.transpose(ps("obT", j)[:, t * 128:t * 128 + 128], OB[:, t, j * 128:j * 128 + 128], ident)
                close_group(ins, "obT", j)

            for c in range(3):
                w = w8(weights(pe, "hq", c))
                for j in range(4):
                    project_cm(("hq", c, j), w, j * 128)
            for c in range(2):
                w = w8(weights(pe, "hv", c))
                for t in range(NT):
                    project_tm(("hv", c, t), HT, t, [(0, w)])
            emptied(pe, "hv", 0, 4)
            for u in range(4):
                d, hp = u // 2, u % 2

                def tile_at(n):
                    return (n if d == 0 else 3 - n) if n < 4 else 4

                def intra(n):
                    i, t = 5 * u + n, tile_at(n)
                    tc = slice(t * 128, t * 128 + 128)
                    open_group(pe, "hs", u, n)
                    for hh in range(2):
                        ins = T.matmul(ps("hs", u, n)[:, hh * 128:hh * 128 + 128], KHAT[:, hh, tc], QHAT[:, hh, tc],
                                       start=True, stop=True)
                    close_group(ins, "hs", u, n)
                    open_group(pe, "hk", u, n)
                    for hh in range(2):
                        ins = T.transpose(ps("hk", u, n)[:, hh * 128:hh * 128 + 128], KTIL[:, hh, tc], ident)
                    close_group(ins, "hk", u, n)
                    emptied(pe, "hk", u, n)
                    pe.wait_ge(h_vm, 4 * (i + 1))
                    open_group(pe, "hd", u, n)
                    for hh in range(2):
                        ins = T.matmul(ps("hd", u, n)[:, hh * 512:hh * 512 + 512], KTT[:, i % 2, hh * 128:hh * 128 + 128],
                                       VM[:, i % 2, hh, :, :].rearrange("p j v -> p (j v)"), start=True, stop=True)
                    close_group(ins, "hd", u, n)

                for piece in UNIT_MODS[u]:
                    side(*piece)
                pe.wait_ge(h_mul, 4 * (u + 1))
                intra(0)
                for n in range(NT):
                    if n + 1 < NT:
                        intra(n + 1)
                    i, t = 5 * u + n, tile_at(n)
                    emptied(pe, "hs", u, n)
                    emptied(pe, "hd", u, n)
                    open_group(pe, "ho", u, n)
                    for hh in range(2):
                        h = 2 * hp + hh
                        T.matmul(ps("ho", u, n)[:, hh * 128:hh * 128 + 128], SC[:, d, i % 2, hh, :],
                                 HV[:, t, h * 128:h * 128 + 128], start=True, stop=False, skip_group_check=True)
                        for step in range(4):
                            j = step if d == 0 else 3 - step
                            ins = T.matmul(ps("ho", u, n)[32 * j:32 * j + 32, hh * 128:hh * 128 + 128],
                                           QTIL[:, hh, t * 128 + 32 * j:t * 128 + 32 * j + 32], state_before(i, n, step, hh),
                                           start=False, stop=(step == 3), skip_group_check=True)
                    close_group(ins, "ho", u, n)
                    for piece in STEP_MODS.get((u, n), []):
                        side(*piece)
            pe.wait_ge(o_ready, 1)
            for j in range(4):
                open_group(pe, "oaT", j)
                for t in range(NT):
                    ins = T.transpose(ps("oaT", j)[:, t * 128:t * 128 + 128], HO[:, t, j * 128:j * 128 + 128], ident)
                close_group(ins, "oaT", j)

            for l in range(2):
                m = MS[l]
                if l == 1:
                    pe.wait_ge(x_ready, 10)
                    x_transposes(1)
                    for c in CD_ORDER:
                        w = w8(weights(pe, "cd", c))
                        for j in range(4):
                            project_cm(("cd", c, j), w, j * 128)
                    pe.wait_ge(cd_up, 1)
                    for j in range(4):
                        pe.wait_ge(tap_diag, PE_TAPS * (j + 1))
                        open_group(pe, "cv", j)
                        for i in range(PE_TAPS):
                            k = CFK - PE_TAPS + i
                            for at, a, n in ((0, 0, 512), (512, 527, 128)):
                                ins = T.matmul(ps("cv", j)[:, at:at + n], DG[PE_TAPS * j + i], UP[:, j, a + k:a + k + n],
                                               start=(i == 0), stop=(i == PE_TAPS - 1))
                        close_group(ins, "cv", j)
                    emptied(pe, "cv", 3)
                    for name, src in (("mean", CO), ("var", SQ)):
                        pe.wait_ge(cd_conv if name == "mean" else cd_sq, 4 if name == "mean" else 1)
                        open_group(pe, name)
                        for b in range(2):
                            for j in range(4):
                                ins = T.matmul(ps(name)[:, b * 512:b * 512 + 328], const("ones"), src[:, j, b * 328:b * 328 + 328],
                                               start=(j == 0), stop=(j == 3))
                        close_group(ins, name)
                if l == 0:
                    for j in range(4):
                        emptied(pe, "oaT", j)
                else:
                    pe.wait_ge(cd_out_v, 1)
                    pe.wait_ge(cd_out, 4)
                w0, w1 = w8(weights(pe, "wo", l, 0)), w8(weights(pe, "wo", l, 1))
                for t in range(NT):
                    project_tm(("y", l, t), OT, t, [(0, w0), (512, w1)])
                for t in range(NT):
                    pe.wait_ge(h_ready, 5 * l + t + 1)
                    open_group(pe, "hT", l, t)
                    for k in range(KD):
                        ins = T.transpose(ps("hT", l, t)[:, k * 128:k * 128 + 128], HB[:, t % 2, k * 128:k * 128 + 128], ident)
                    close_group(ins, "hT", l, t)
                pe.wait_ge(d_wr, 32 * (l + 1))
                open_group(pe, "lg", l)
                for t in range(NT):
                    emptied(pe, "hT", l, t)
                    for k in range(KD):
                        ins = T.matmul(ps("lg", l)[:, t * 36:t * 36 + 36], HT[:, k, t * 128:t * 128 + 128], WR[:, k, :],
                                       start=(k == 0), stop=(k == KD - 1))
                close_group(ins, "lg", l)
                pe.wait_ge(rt_mask, l + 1)
                open_group(pe, "ct", l)
                T.matmul(ps("ct", l)[:, 0:160], const("tri"), RT[:, 5, :], start=True, stop=True)
                close_group(T.matmul(ps("ct", l)[:, 512:672], const("ones"), RT[:, 5, :], start=True, stop=True), "ct", l)
                pe.wait_ge(d_tb, 16 * (l + 1))
                open_group(pe, "tb", l)
                for c in range(2):
                    ins = T.matmul(ps("tb", l)[:, NTILE * c:NTILE * (c + 1)], TBR.rearrange("n (s c) -> n c s", c=2)[:, c, :],
                                   C[0:NTILE, 0:NTILE], start=True, stop=True)
                close_group(ins, "tb", l)
                emptied(pe, "hT", l, 4)
                emptied(pe, "lg", l)
                emptied(pe, "ct", l)
                emptied(pe, "tb", l)

                def tiles(n0, h0, count, arrived):
                    def transposes(u):
                        pe.wait_ge(m[f"g{u % 2}"], h0 + 16 * (u // 2 + 1))
                        pe.wait_ge(m["xa"], 1 + n0 + u)
                        pe.wait_ge(m["xv"], 1 + n0 + u)
                        for k in range(KD):
                            ins = T.transpose(bank(k // 4)[:, (k % 4) * 128:(k % 4) * 128 + 128],
                                              XG[:, u % 2, k * 128:k * 128 + 128], ident)
                        ins.then_inc(m["t"], 1)

                    def gate_up(u):
                        arrived(u)
                        pe.wait_ge(m["xa"], 1 + n0 + (u + 1))
                        pe.wait_ge(m["xv"], 1 + n0 + (u + 1))
                        if u >= 2:
                            pe.wait_ge(m["hid"], n0 + (u - 1))
                        w = expert_gu(u % 4)
                        for k in range(KD):
                            ins = T.matmul(bank(2 + u % 2)[:, 0:256], XGT[:, u % 2, k * 128:k * 128 + 128], w[:, k, :],
                                           start=(k == 0), stop=(k == KD - 1))
                        ins.then_inc(m["gu"], 1)

                    def down(u):
                        pe.wait_ge(m["hid"], n0 + (u + 1))
                        T.transpose(bank(4 + u % 2)[:, 0:128], HID[:, u % 2, :], ident).then_inc(m["ht"], 1)
                        pe.wait_ge(m["hidt"], n0 + (u + 1))
                        pe.wait_ge(m["ya"], 1 + n0 + u)
                        pe.wait_ge(m["yv"], 1 + n0 + u)
                        w = expert_down(u % 4)
                        for b in range(2):
                            ins = T.matmul(bank(6 + b), HIDT[:, u % 2, :], w[:, b * 512:b * 512 + 512], start=True, stop=True)
                        ins.then_inc(m["down"], 1)

                    transposes(0)
                    gate_up(0)
                    for u in range(1, count):
                        transposes(u)
                        down(u - 1)
                        gate_up(u)
                    down(count - 1)

                pe.wait_ge(rt_ready, l + 1)
                pairs = pe.value_load(RI[0:1, 0:1], min_val=0, max_val=NEXTRA // 2)
                with pe.Fori(0, NI) as i:
                    tiles(i * U, i * (8 * U), U, lambda u: pe.wait_ge(m[f"w{u % 4}"], i * 96 + 48 * (u // 4 + 1)))
                with pe.If(pairs > 0):
                    with pe.Fori(0, pairs) as j:
                        tiles(j * 2 + NE, j * 16 + 8 * NE, 2, lambda u: pe.wait_ge(m[f"xw{u}"], j * 48 + 48))
                pe.wait_ge(moe_done, l + 1)

    return nc


_INS = ['x_prompt', 'x_sample', 'state_hgrn_fwd', 'state_hgrn_bwd', 'cache_mla_ckv', 'cache_mla_krope', 'c', 'c_ctx',
        'mod_w', 'mod_b', 'ln_g', 'ln_b', 'ab_w_in', 'ab_w_out', 'hgrn_lb_logits', 'hgrn_norm_g', 'mla_q_norm_g',
        'mla_w_uq', 'mla_kv_norm_g', 'mla_w_ukv', 'cd_w_in', 'cd_w_out', 'sc_conv_w', 'cf_conv_w', 'cf_conv_b',
        'cf_ln_g', 'cf_ln_b', 'moe_w_group', 'moe_w_expert', 'moe_w_gate', 'moe_w_up', 'moe_w_down']
_OUTS = [("y_prompt", (1, 128, D)), ("y_sample", (1, 512, D)), ("new_sf", (1, 1, HA, DK, DK)), ("new_sb", (1, 1, HA, DK, DK)),
         ("new_ckv", (1, 1, 128, KVR)), ("new_kr", (1, 1, 128, DR))]


def kernel(**inputs):
    import concourse.bacc as bacc
    from concourse.bass_utils import run_bass_kernel_spmd

    nc = bacc.Bacc("TRN2", target_bir_lowering=False, num_devices=1)
    arrays, A, O = {}, {}, {}
    for name in _INS:
        arrays["in_" + name] = np.ascontiguousarray(inputs[name])
    arrays["in_consts"] = constants()
    for name, a in arrays.items():
        A[name[3:]] = nc.dram_tensor(name, a.shape, mybir.dt.from_np(a.dtype), kind="ExternalInput").ap()
    for name, shape in _OUTS:
        O[name] = nc.dram_tensor("out_" + name, shape, mybir.dt.float32, kind="ExternalOutput").ap()
    build(nc, A, O)
    r = run_bass_kernel_spmd(nc, [arrays], core_ids=[0])
    return tuple(r.results[0]["out_" + name] for name, _ in _OUTS)
```

```python
import concourse.bass as bass
from concourse import mybir
from contextlib import ExitStack
import numpy as np

D = 1024
KD = D // 128
NT = 5
NLAT = 512
NTOK = 640
CH = 32
HA, DK = 4, 128
MH, DN, DR, DV = 8, 64, 32, 64
QR, KVR = 384, 256
AB_IN = 5 * 512 + QR + KVR + DR
NE, NG, EG, FF = 32, 4, 8, 128
ALPHA = 4.0 ** 0.25
LN_EPS, RMS_EPS = 1e-5, 1e-6
SCALE = float(DN + DR) ** -0.5
CFK, SCK = 31, 3
PADW = 15
CXW = 15 + 512 + 15 + 128 + 15
COW = 656
NOROW = 8192.0
SL = 96
NEXTRA = 2 * ((2 * NTOK // (SL + 1) + 1) // 2)
NTILE = 32 + NEXTRA + 2
NBLK = -(-NTOK // SL) - 1

CONST_COLS = [("ident", 128), ("mask_f", 128), ("mask_b", 128), ("tri", 128), ("ones", 192), ("iota", 128),
              ("scan", 640), ("perm", 32), ("cos", 512), ("sin", 512),
              ("pidx", 1), ("prio4", 4), ("prio8", 8), ("first_slot", 32), ("evens", 7)]
COFF = {}
_at = 0
for _n, _w in CONST_COLS:
    COFF[_n] = (_at, _at + _w)
    _at += _w
NCONST = _at


def constants():
    c = np.zeros((128, NCONST), np.float32)

    def put(name, rows, value):
        a, b = COFF[name]
        c[rows, a:b] = value
    p = np.arange(128)
    same = (p[:, None] // CH) == (p[None, :] // CH)
    put("ident", slice(None), np.eye(128))
    put("mask_f", slice(None), same & (p[:, None] <= p[None, :]))
    put("mask_b", slice(None), same & (p[:, None] >= p[None, :]))
    put("tri", slice(None), p[:, None] < p[None, :])
    put("ones", slice(None), 1.0)
    put("iota", slice(None), p[None, :])
    put("scan", slice(None), (np.arange(NTOK) % CH != 0)[None, :])
    perm = np.zeros((32, 32))
    for a in range(2):
        for f in range(8):
            perm[a * 16 + 8 + f, a * 16 + f] = -1.0
            perm[a * 16 + f, a * 16 + 8 + f] = 1.0
    put("perm", slice(64, 96), perm)
    inv = np.float32(10000.0) ** (-np.arange(8, dtype=np.float32) / np.float32(8))
    tok = np.arange(NLAT)
    pos = np.stack([tok // 64, tok % 64]).astype(np.float32)
    ang = (pos[:, None, :] * inv[None, :, None]).astype(np.float32)
    ang = np.stack([ang, ang], axis=1).reshape(32, NLAT)
    put("cos", slice(64, 96), np.cos(ang))
    put("sin", slice(64, 96), np.sin(ang))
    put("pidx", slice(None), p[:, None])
    put("prio4", slice(None), np.arange(4, 0, -1)[None, :])
    put("prio8", slice(None), np.arange(8, 0, -1)[None, :])
    put("first_slot", slice(None), SL * np.arange(32)[None, :])
    put("evens", slice(None), 2 * np.arange(7)[None, :])
    return c


FIRST_MODS = [("mod", 0), ("mod", 1), ("modb", 0), ("mod", 2), ("modb", 1), ("mod", 3), ("modb", 2), ("modb", 3)]
ATTN_MOD_TILE = 3
UNIT_MODS = [[("mod", 1, 3 * u), ("mod", 1, 3 * u + 1)] for u in range(4)]
STEP_MODS = {(u, 2): [("mod", 1, 3 * u + 2)] for u in range(4)}
STEP_MODS[0, 0] = [("modb", 1, 0), ("modb", 1, 1)]
STEP_MODS[0, 3] = [("modb", 1, 2)]
STEP_MODS[1, 0] = [("modb", 1, 3)]
CD_ORDER = (3, 4, 0, 1, 2)
PE_TAPS = 3
OUT_ORDER = [("y", 0), ("y", 1), ("y", 2), ("hT", 0), ("y", 3), ("hT", 1), ("lg", 0), ("y", 4), ("hT", 2), ("lg", 1),
             ("hT", 3), ("lg", 2), ("hT", 4), ("lg", 3), ("lg", 4)]


def psum_groups():
    g = [("vec",)]
    for l in range(2):
        if l == 0:
            g += [(kind, 0, c) for kind, c in FIRST_MODS]
        g += [("xT", l, k) for k in range(KD if l == 0 else NT)]
        if l == 0:
            g += [("cq", t) for t in range(NT)]
            g += [("cqT", r) for r in range(3)] + [("ckvT", r) for r in range(2)] + [("krT",), ("krP",)]
            g += [("v", t) for t in range(6)]
            g += [("k", 0), ("q", 0), ("qP", 0)]
            steps = [(h, t) for h in range(MH) for t in range(NT)]
            g.append(("s",) + steps[0])
            for n, (h, t) in enumerate(steps):
                if h + 1 < MH and t == 0:
                    g += [("k", h + 1), ("q", h + 1)]
                if h + 1 < MH and t == 2:
                    g.append(("qP", h + 1))
                if n + 1 < len(steps):
                    g.append(("s",) + steps[n + 1])
                if t == ATTN_MOD_TILE:
                    g.append(("mod", 0, 4 + h))
                g += [("pt", h, t), ("o", h, t)]
            g += [("obT", j) for j in range(4)]
            g += [("hq", c, j) for c in range(3) for j in range(4)]
            g += [("hv", c, t) for c in range(2) for t in range(NT)]
            for u in range(4):
                g += UNIT_MODS[u]
                g += [("hs", u, 0), ("hk", u, 0), ("hd", u, 0)]
                for n in range(NT):
                    if n + 1 < NT:
                        g += [("hs", u, n + 1), ("hk", u, n + 1), ("hd", u, n + 1)]
                    g.append(("ho", u, n))
                    g += STEP_MODS.get((u, n), [])
            g += [("oaT", j) for j in range(4)]
        else:
            g += [("cd", c, j) for c in CD_ORDER for j in range(4)]
            g += [("cv", j) for j in range(4)]
            g += [("mean",), ("var",)]
        g += [(kind, l, t) for kind, t in OUT_ORDER]
        g += [("ct", l), ("tb", l)]
    return {name: n for n, name in enumerate(g)}


def build(nc, A, O):
    f32, i32, bf16 = mybir.dt.float32, mybir.dt.int32, mybir.dt.bfloat16
    ALU = mybir.AluOpType
    ACT = mybir.ActivationFunctionType
    AX = mybir.AxisListType
    GROUP = psum_groups()
    ctx = ExitStack()
    with ctx:
        def sb(name, shape, dt=f32):
            return ctx.enter_context(nc.sbuf_tensor(name, shape, dt))

        def sem(name):
            return ctx.enter_context(nc.semaphore(name))

        C = sb("consts", [128, NCONST])
        X = sb("x_tm", [128, NT, D])
        HT = sb("h_cm", [128, KD, NTOK])
        OT = sb("mix_cm", [128, KD, NTOK])
        W = sb("weights", [128, 3 * 4096])
        GR = sb("gate_rows", [128, 2048])
        LNR = sb("ln_rows", [128, 2, 1024])
        Z = sb("scratch", [128, 15360])
        MB2 = sb("mod_bias2", [2, 512])
        MR = sb("mod_row", [2, 2, 512])
        MC = sb("mod_cols", [128, 2, 2, KD, 2])
        CT = sb("c_cm", [128, 16])
        VC = sb("vectors_cm", [128, 43])
        CW = sb("taps_cm", [128, 124])
        LBT = sb("lower_bound", [128, 2, 8])
        LBS = sb("lower_bound_work", [128, 3, 8])
        HNG = sb("hgrn_norm_row", [128, DK])
        SS = sb("square_sums", [128, NT, 2])
        GF = sb("slots_of_tokens_f", [128, 2, NT])
        RR = sb("rms_scale", [128, NT, 2])
        MXS = sb("softmax_max", [128, 2, 2])
        SUM = sb("softmax_sum", [128, 2, 2])
        DEC = sb("chunk_decay", [128, 2, 20])
        ZERO = sb("zero_state", [128, 128])
        HSS = sb("head_square_sums", [128, 2, 10])
        ST6 = sb("ln_stats", [128, 2, 2, 6])
        MV = sb("ln_mean_var", [128, 2, 2])
        RSD = sb("ln_rstd", [128, 2, 2])
        NB = sb("ln_shift", [128, 2])
        WR = sb("router_w", [128, KD, 36])
        RS = sb("router_small", [128, 10, 8])
        O4 = sb("group_onehot", [128, NT, 4])
        W12 = sb("pair_weights", [128, 2, NT])
        RUN = sb("running_count", [128, NE])
        TI = sb("gather_rows", [128, NTILE], i32)
        TY = sb("scatter_rows", [128, NTILE], i32)
        NOR = sb("no_rows", [128, 2 * NTILE * SL // 128])
        PAY = sb("slot_payload", [128, 2, NT, 2])
        GI = sb("slots_of_tokens", [128, 2, NT], i32)
        EXI = sb("extra_experts", [128, NEXTRA], i32)
        RI = sb("extra_pairs", [128, 1], i32)
        IXG = sb("gather_now", [128, 2], i32)
        IXY = sb("scatter_now", [128, 2], i32)
        PS = ctx.enter_context(nc.psum_tensor("ps", [128, 4, 1024], f32))

        def const(name, rows=slice(0, 128)):
            a, b = COFF[name]
            return C[rows, a:b]

        ident = const("ident")

        TBL = nc.dram_tensor("slot_table", [NTILE * SL, 2], f32).ap()
        HD = nc.dram_tensor("h_rows", [NTOK, D], f32).ap()
        MODD = nc.dram_tensor("mod_rows", [2, 2, 6 * D], f32).ap()
        YD = nc.dram_tensor("expert_rows", [2 * NTOK, D], f32).ap()

        slot_full = [sem(f"slot_full{i}") for i in range(4)]
        slot_free = [sem(f"slot_free{i}") for i in range(4)]
        w_full = [sem(f"w_full{i}") for i in range(3)]
        vec_step, act_step, pool_step = sem("vec_step"), sem("act_step"), sem("pool_step")
        d_vec_a = sem("d_vec_a")
        d_const, d_vec, d_x, d_rows = sem("d_const"), sem("d_vec"), sem("d_x"), sem("d_rows")
        d_cache, d_kv_out, d_xr = sem("d_cache"), sem("d_kv_out"), sem("d_xr")
        c_silu, lb_exp_in, lb_exp = sem("c_silu"), sem("lb_exp_in"), sem("lb_exp")
        sq_ready, rms_in, rms_sd, norm_ready = sem("sq_ready"), sem("rms_in"), sem("rms_sd"), sem("norm_ready")
        kr_ready, q_raw, q_rot = sem("kr_ready"), sem("q_raw"), sem("q_rot")
        max_ready, exp_ready = sem("max_ready"), sem("exp_ready")
        h_zero, h_f, h_l, h_arg, h_exp, h_mul = (sem("h_zero"), sem("h_f"), sem("h_l"), sem("h_arg"),
                                                 sem("h_exp"), sem("h_mul"))
        h_vm, h_s0, d_state = sem("h_vm"), sem("h_s0"), sem("d_state")
        o_gate = sem("o_gate")
        o_var, o_sd, o_ready = sem("o_var"), sem("o_sd"), sem("o_ready")
        ln_var, ln_sd, x_ready, h_ready = sem("ln_var"), sem("ln_sd"), sem("x_ready"), sem("h_ready")
        d_ln = sem("d_ln")
        d_mr, d_g1, d_r = [sem(f"d_mr{i}") for i in range(2)], sem("d_g1"), sem("d_r")
        tap_diag = sem("tap_diag")
        const_ready = sem("const_ready")
        d_hst = [sem(f"d_hst{i}") for i in range(2)]
        d_wr = sem("d_wr")
        rt_slots, d_init, d_scat, d_tb = sem("rt_slots"), sem("d_init"), sem("d_scat"), sem("d_tb")
        rt_exp_in, rt_exp, rt_mask, rt_ready = sem("rt_exp_in"), sem("rt_exp"), sem("rt_mask"), sem("rt_ready")
        d_yl = [sem(f"d_yl{i}") for i in range(2)]
        y_used, y_scaled = sem("y_used"), sem("y_scaled")
        ln_shift, ln_normed = sem("ln_shift_ready"), sem("ln_normed")
        moe_done = sem("moe_done")
        cd_pad, cd_conv, cd_sq, cd_sd, cd_u = (sem("cd_pad"), sem("cd_conv"), sem("cd_sq"), sem("cd_sd"), sem("cd_u"))
        cd_out, cd_up = sem("cd_out_a"), sem("cd_up")
        cd_out_v = sem("cd_out_v")
        d_out = sem("d_out")

        def moe_sems(l):
            names = ["w0", "w1", "w2", "w3", "xw0", "xw1", "g0", "g1", "t", "xa", "xv", "gu", "sg", "hid",
                     "down", "ya", "yv", "s0", "s1", "s_ix", "pool_passed"]
            return {n: sem(f"moe{l}_{n}") for n in names}
        MS = [moe_sems(l) for l in range(2)]

        def ps(*name):
            return PS[:, GROUP[name] % 4, :]

        def open_group(pe, *name):
            n = GROUP[name]
            if n >= 4:
                pe.wait_ge(slot_free[n % 4], n // 4)

        def close_group(ins, *name):
            ins.then_inc(slot_full[GROUP[name] % 4], 1)

        def filled(eng, *name):
            eng.wait_ge(slot_full[GROUP[name] % 4], GROUP[name] // 4 + 1)

        def release(ins, *name):
            ins.then_inc(slot_free[GROUP[name] % 4], 1)

        def emptied(eng, *name):
            eng.wait_ge(slot_free[GROUP[name] % 4], GROUP[name] // 4 + 1)

        def bank(b):
            return PS[:, b // 2, (b % 2) * 512:(b % 2) * 512 + 512]

        def turned_bank(b):
            return bank(b)[:, 0:4 * SL]

        def result_bank(u, half):
            return bank(4 + 2 * (u % 2) + half)[0:SL, :]

        MB = [C[0:2, COFF["cos"][0]:COFF["cos"][1]], C[0:2, COFF["sin"][0]:COFF["sin"][1]], MB2[:, :]]
        V1, V2, V3 = GR[0:16, 0:128], GR[0:43, 128:256], GR[0:124, 256:384]
        def z(a, n):
            return Z[:, a:a + n]

        CQ = z(0, 3360).rearrange("p (t c) -> p t c", t=NT)
        CQT = z(3360, 1920).rearrange("p (r t) -> p r t", r=3)
        CKVT = z(5280, 1536).rearrange("p (r t) -> p r t", r=2)
        VT = z(6816, 3072).rearrange("p (t c) -> p t c", t=6)
        KT = z(9888, 1536).rearrange("p (b t) -> p b t", b=2)
        QT = z(11424, 1280).rearrange("p (b t) -> p b t", b=2)
        KRS, ROT1, ROT2 = z(12704, 512), z(13216, 512), z(13728, 512)
        CC = z(14240, 288)
        CKG = z(14528, KVR)
        LNF = LNR[:, :, :].rearrange("p a b -> p (a b)")
        PB = LNF[:, 0:1280].rearrange("p (b t) -> p b t", b=2)
        PTS = GR[:, 0:1280].rearrange("p (b t) -> p b t", b=2)
        OTF = OT[:, :, :].rearrange("p a b -> p (a b)")
        OB = OTF[:, 0:2560].rearrange("p (t c) -> p t c", t=NT)

        HQ = z(0, 2560).rearrange("p (h t) -> p h t", h=4)
        HF = [z(2560 + 2560 * d, 2560).rearrange("p (h t) -> p h t", h=4) for d in range(2)]
        HV = z(7680, 2560).rearrange("p (t c) -> p t c", t=NT)
        HG = z(10240, 2560).rearrange("p (t c) -> p t c", t=NT)
        HO = z(12800, 2560).rearrange("p (t c) -> p t c", t=NT)
        HTF = HT[:, :, :].rearrange("p a b -> p (a b)")
        QHAT, KHAT, QTIL, KTIL = [HTF[:, 1280 * i:1280 * (i + 1)].rearrange("p (h t) -> p h t", h=2)
                                  for i in range(4)]
        XF = X[:, :, :].rearrange("p a b -> p (a b)")
        BUFB = XF[:, 0:1280].rearrange("p (h t) -> p h t", h=2)
        BUFA = XF[:, 1280:2560].rearrange("p (h t) -> p h t", h=2)
        VM = XF[:, 2560:4608].rearrange("p (b h j v) -> p b h j v", b=2, h=2, j=4)
        BUFL = LNF[:, 0:1280].rearrange("p (h t) -> p h t", h=2)
        SC = GR[:, 0:1024].rearrange("p (d b h t) -> p d b h t", d=2, b=2, h=2)
        KTT = GR[:, 1024:1536].rearrange("p (b c) -> p b c", b=2)
        ST = OTF[:, 0:1536].rearrange("p (b h n v) -> p b h n v", b=2, h=2, n=3)
        CAR = OTF[:, 1536:2304].rearrange("p (b h v) -> p b h v", b=3, h=2)
        S0B = OTF[:, 2304:2560].rearrange("p (h v) -> p h v", h=2)

        G1 = GR[:, :].rearrange("p (g d) -> p g d", g=2)
        R3, R4, R5 = [z(2048 * i, 2048).rearrange("p (g d) -> p g d", g=2) for i in range(3)]
        ZT = z(6144, 2048).rearrange("p (b d) -> p b d", b=2)
        HB = z(8192, 2048).rearrange("p (b d) -> p b d", b=2)
        SG = z(8192, 256).rearrange("p (b f) -> p b f", b=2)
        HID = z(8448, 256).rearrange("p (b f) -> p b f", b=2)
        XG = z(10240, 2048).rearrange("p (b d) -> p b d", b=2)
        XGT = z(12288, 2048).rearrange("p (b d) -> p b d", b=2)
        CM = z(14336, 160).rearrange("p (t e) -> p t e", t=NT)
        IND, INC, DELTA, BASE = z(12288, NBLK * 32), z(12480, NBLK * 32), z(12896, NBLK * 32), z(12672, NBLK * 32 + 32)
        GG, GT = z(15040, 160), z(15200, 160)
        TBR = OTF[0:NTILE, 256:256 + 2 * SL]
        EXW = OTF[:, 512:512 + NEXTRA * NBLK * 32].rearrange("p (n c) -> p n c", n=NEXTRA)
        EXF = OTF[:, 3584:3584 + NEXTRA]
        LG = OTF[:, 0:180].rearrange("p (t c) -> p t c", t=NT)
        RT = OTF[:, 4096:5056].rearrange("p (a c) -> p a c", a=6)
        YB = OTF[:, 0:4096].rearrange("p (b k d) -> p b k d", b=2, k=2)

        BG = z(0, 2560).rearrange("p (j t) -> p j t", j=4)
        CXP = z(2560, 4 * CXW).rearrange("p (j t) -> p j t", j=4)
        UP = z(5300, 4 * CXW).rearrange("p (j t) -> p j t", j=4)
        CO = z(8040, 4 * COW).rearrange("p (j t) -> p j t", j=4)
        SQ = z(10664, 4 * COW).rearrange("p (j t) -> p j t", j=4)
        RST = z(13288, COW)
        DG = [OTF[:, 2560 + 128 * i:2688 + 128 * i] for i in range(4 * PE_TAPS)]

        def state_before(i, n, step, hh):
            if step:
                return ST[:, i % 2, hh, step - 1, :]
            if n == 0:
                return S0B[:, hh, :]
            return ZERO[:, :] if n == 4 else CAR[:, (i - 1) % 3, hh, :]

        def slot3(s):
            return W[:, 4096 * s:4096 * (s + 1)]

        def col_chunk(w, a, b):
            return w.rearrange("(k p) n -> p k n", p=128)[:, :, a:b]

        WITEM = {}
        items = []
        in_slot = [None, None, None]
        words_in = [0, 0, 0]

        def item(name, s, last, parts):
            words_in[s] += 16 * len(parts)
            WITEM[name] = {"slot": s, "value": words_in[s], "parts": parts, "last": last, "before": in_slot[s]}
            in_slot[s] = name
            items.append(name)

        def mod_item(l, c, s):
            item(("mod", l, c), s, ("mod", l, c),
                 [(slot3(s).rearrange("p (k n) -> p k n", k=8), col_chunk(A["mod_w"][l], c * 512, c * 512 + 512)),
                  (MB[s], A["mod_b"][l, c * 512:c * 512 + 512].partition_broadcast(2))])

        def proj_item(name, s, last, w, a, b):
            n = b - a
            item(name, s, last, [(slot3(s)[:, 0:8 * n].rearrange("p (k n) -> p k n", k=8), col_chunk(w, a, b))])

        for c in range(4):
            mod_item(0, c, c % 3)
        w_in = A["ab_w_in"][0]
        proj_item(("cqa",), 1, ("cq", 4), w_in, 2560, 3072)
        proj_item(("cqb",), 2, ("cq", 4), w_in, 3072, AB_IN)
        item(("uq",), 0, ("q", 7), [(slot3(0)[:, 0:2304].rearrange("p (k n) -> p k n", k=3),
                                     A["mla_w_uq"][0].rearrange("(k p) n -> p k n", p=128))])
        item(("ukv",), 1, ("k", 7), [(slot3(1)[:, 0:2048].rearrange("p (k n) -> p k n", k=2),
                                      A["mla_w_ukv"][0].rearrange("(k p) n -> p k n", p=128))])

        def hq_item(c, s):
            proj_item(("hq", c), s, ("hq", c, 3), w_in, c * 512, c * 512 + 512)
        for c in range(4, 11):
            mod_item(0, c, 2)
        hq_item(0, 0)
        hq_item(1, 1)
        mod_item(0, 11, 2)
        hq_item(2, 2)
        for c in range(2):
            proj_item(("hv", c), c, ("hv", c, 4), w_in, 1536 + c * 512, 2048 + c * 512)
        for c in range(12):
            mod_item(1, c, (c + 2) % 3)
        for c in range(2):
            proj_item(("wo", 0, c), (c + 2) % 3, ("y", 0, 4), A["ab_w_out"][0], c * 512, c * 512 + 512)
        N_ITEMS0 = len(items)
        LAST_IN_SLOT0 = list(in_slot)
        in_slot[:] = [None, None, None]
        for n, c in enumerate(CD_ORDER):
            proj_item(("cd", c), n % 3, ("cd", c, 3), A["cd_w_in"][0], c * 512, c * 512 + 512)
        for c in range(2):
            proj_item(("wo", 1, c), (c + 2) % 3, ("y", 1, 4), A["cd_w_out"][0], c * 512, c * 512 + 512)
        LAST_IN_SLOT1 = list(in_slot)

        def rows_stored(l, c):
            return sum(1 for k in range(12 * l + c + 1) if k % 2 == c % 2 and k % 12 >= 4)

        def weights(pe, *name):
            it = WITEM[name]
            pe.wait_ge(w_full[it["slot"]], it["value"])
            return slot3(it["slot"])

        U = 8
        NI = NE // U
        EW = 3072

        def expert_gu(s, g):
            return W[:, EW * s + 1024 * g:EW * s + 1024 * g + 1024]

        def expert_down(s):
            return W[:, EW * s + 2048:EW * (s + 1)]

        block = ctx.enter_context(nc.Block())

        @block.sync
        def _(sp):
            sp.dma_start(C[:, :], A["consts"]).then_inc(d_const, 16)
            xs = A["x_sample"][0].rearrange("(t p) d -> p t d", p=128)

            def retire(name):
                last = WITEM[name]["last"]
                if last[0] != "mod":
                    filled(sp, *last)
                    return
                emptied(sp, *last)
                l, c = last[1:]
                if c >= 4:
                    sp.dma_start(MODD[l, :, c * 512:c * 512 + 512], MR[:, c % 2, :]).then_inc(d_mr[c % 2], 16)

            def load_rows(l, idx, dst, done):
                sp.dma_start(dst, MODD[l, :, idx * D:(idx + 1) * D].partition_broadcast(128)).then_inc(done, 16)

            def load_item(n):
                it = WITEM[items[n]]
                if it["before"] is not None:
                    retire(it["before"])
                for p, (dst, src) in enumerate(it["parts"]):
                    if n < 2 and p == 1:
                        sp.wait_ge(d_const, 16)
                    sp.dma_start(dst, src).then_inc(w_full[it["slot"]], 16)

            def load_expert(l, e, s, done=None):
                m = MS[l]
                done = m[f"w{s}"] if done is None else done
                wg = A["moe_w_gate"][l].rearrange("e (p k) f -> e p (k f)", k=KD)
                wu = A["moe_w_up"][l].rearrange("e (p k) f -> e p (k f)", k=KD)
                if isinstance(e, int):
                    g, u, dn = wg[e], wu[e], A["moe_w_down"][l, e]
                else:
                    g = wg[bass.ds(e, 1)].rearrange("e p c -> (e p) c")
                    u = wu[bass.ds(e, 1)].rearrange("e p c -> (e p) c")
                    dn = A["moe_w_down"][l][bass.ds(e, 1)].rearrange("e f d -> (e f) d")
                sp.dma_start(expert_gu(s, 0), g).then_inc(done, 16)
                sp.dma_start(expert_gu(s, 1), u).then_inc(done, 16)
                sp.dma_start(expert_down(s), dn).then_inc(done, 16)

            for l in range(2):
                m = MS[l]
                lo, hi = (0, N_ITEMS0) if l == 0 else (N_ITEMS0, len(items))
                for n in range(lo, hi):
                    if n == 1:
                        sp.wait_ge(d_vec, 16 * 5)
                        sp.wait_ge(d_vec_a, 16 * 4)
                    load_item(n)
                    if n == 2:
                        sp.dma_start(X[:, 0:4, :], xs).then_inc(d_x, 16)
                        sp.dma_start(X[:, 4, :], A["x_prompt"][0]).then_inc(d_x, 16)
                    if n == N_ITEMS0 + 2:
                        load_rows(1, 2, G1, d_g1)
                if l == 0:
                    retire(LAST_IN_SLOT0[1])
                    for i in range(2):
                        sp.wait_ge(d_mr[i], 16 * 8)
                    filled(sp, "ho", 3, 4)
                    load_rows(0, 2, G1, d_g1)
                else:
                    retire(LAST_IN_SLOT1[1])
                    sp.wait_ge(cd_out, 4)
                    sp.wait_ge(cd_out_v, 1)
                load_rows(l, 4, R4, d_r)
                load_rows(l, 3, R3, d_r)
                load_rows(l, 5, R5, d_r)
                retire(("wo", l, 1))
                for e in range(4):
                    load_expert(l, e, e)
                for u in range(4, U):
                    sp.wait_ge(m["down"], u - 3)
                    load_expert(l, u, u % 4)
                with sp.Fori(1, NI) as i:
                    for u in range(U):
                        sp.wait_ge(m["down"], i * U + (u - 3))
                        load_expert(l, i * U + u, u % 4)
                sp.wait_ge(rt_ready, l + 1)
                pairs = sp.value_load(RI[0:1, 0:1], min_val=0, max_val=NEXTRA // 2)
                with sp.If(pairs > 0):
                    with sp.Fori(0, pairs) as j:
                        for u in range(2):
                            e = sp.value_load(EXI[0:1, bass.ds(j * 2 + u, 1)], min_val=0, max_val=NE - 1)
                            sp.wait_ge(m["down"], NE + j * 2 + (u - 1))
                            load_expert(l, e, u, m[f"xw{u}"])
                sp.wait_ge(moe_done, l + 1)
                for t in range(NT):
                    if t >= 2:
                        sp.wait_ge(y_used, 5 * l + t - 1)
                    for k in range(2):
                        sp.dma_start(YB[:, t % 2, k, :],
                                     YD[k * NTOK + t * 128:k * NTOK + (t + 1) * 128, :]).then_inc(d_yl[t % 2], 16)
            for t in range(NT):
                sp.wait_ge(x_ready, 15 + t + 1)
                dst = O["y_sample"][0, t * 128:(t + 1) * 128, :] if t < 4 else O["y_prompt"][0]
                sp.dma_start(dst, X[:, t, :]).then_inc(d_out, 16)
            sp.wait_ge(d_out, 16 * NT)

        @block.gpsimd
        def _(pool):
            steps = [0]

            def chain(ins):
                steps[0] += 1
                ins.then_inc(pool_step, 1)
                pool.wait_ge(pool_step, steps[0])

            pool.dma_start(V2[16:19, :], A["mla_q_norm_g"][0].rearrange("(k p) -> k p", p=128)).then_inc(d_vec, 16)
            pool.dma_start(V2[19:23, :], A["cf_conv_b"][0].rearrange("(k p) -> k p", p=128)).then_inc(d_vec, 16)
            pool.dma_start(V2[23:27, :], A["cf_ln_g"][0].rearrange("(k p) -> k p", p=128)).then_inc(d_vec, 16)
            pool.dma_start(V2[27:31, :], A["cf_ln_b"][0].rearrange("(k p) -> k p", p=128)).then_inc(d_vec, 16)
            pool.dma_start(V2[31:43, :], A["sc_conv_w"][0].rearrange("t (k p) -> (t k) p", p=128)).then_inc(d_vec, 16)
            pool.dma_start(CKG[:, :], A["mla_kv_norm_g"][0].partition_broadcast(128)).then_inc(d_rows, 16)
            pool.dma_start(HNG[:, :], A["hgrn_norm_g"][0].partition_broadcast(128)).then_inc(d_rows, 16)
            pool.dma_start(CC[:, 0:KVR], A["cache_mla_ckv"][0, 0]).then_inc(d_cache, 16)
            pool.dma_start(CC[:, KVR:288], A["cache_mla_krope"][0, 0]).then_inc(d_cache, 16)

            pool.wait_ge(norm_ready, 1)
            pool.dma_start(O["new_ckv"][0, 0], CQ[:, 4, QR:QR + KVR]).then_inc(d_kv_out, 16)
            pool.dma_start(O["new_kr"][0, 0], CQ[:, 4, QR + KVR:672]).then_inc(d_kv_out, 16)

            filled(pool, "obT", 3)
            nc.gpsimd.memset(VM[:, :, :, :, :], 0.0).then_inc(h_zero, 1)
            nc.gpsimd.memset(SC[:, :, :, :, :], 0.0).then_inc(h_zero, 1)
            nc.gpsimd.memset(ZERO[:, :], 0.0).then_inc(h_zero, 1)
            pool.wait_ge(h_zero, 3)
            state_in = [A["state_hgrn_fwd"][0, 0], A["state_hgrn_bwd"][0, 0]]
            state_out = [O["new_sf"][0, 0], O["new_sb"][0, 0]]
            emptied(pool, "hv", 0, 4)
            for u in range(4):
                d, hp = u // 2, u % 2
                if u:
                    filled(pool, "ho", u - 1, 1)
                pool.dma_start(S0B[:, :, :], state_in[d][2 * hp:2 * hp + 2].rearrange("h k v -> k h v")).then_inc(h_s0, 16)
                for n in range(NT):
                    i = 5 * u + n
                    t = (n if d == 0 else 3 - n) if n < 4 else 4
                    if i >= 2:
                        filled(pool, "hd", *divmod(i - 2, 5))
                    for j in range(4):
                        r = slice(32 * j, 32 * j + 32)
                        src = HV[r, t, 256 * hp:256 * hp + 256].rearrange("p (h v) -> p h v", h=2)
                        nc.gpsimd.tensor_copy(VM[r, i % 2, :, j, :], src).then_inc(h_vm, 1)
                emptied(pool, "hd", u, 4)
                pool.dma_start(state_out[d][2 * hp:2 * hp + 2].rearrange("h k v -> k h v"),
                               CAR[:, (5 * u + 4) % 3, :, :]).then_inc(d_state, 16)
                if u == 0:
                    for t in range(NT):
                        emptied(pool, "hv", 1, t)
                    pool.wait_ge(d_rows, 32)
                    HG3 = z(10240, 2560).rearrange("p (g v) -> p g v", v=128)
                    nc.gpsimd.tensor_tensor(HG3, HG3, HNG[:, :].unsqueeze(1).to_broadcast([128, 20, 128]),
                                            ALU.mult).then_inc(o_gate, 1)
                    pool.wait_ge(o_gate, 1)
            filled(pool, "ho", 3, 4)
            pool.dma_start(X[:, 0:4, :], A["x_sample"][0].rearrange("(t p) d -> p t d", p=128)).then_inc(d_xr, 16)
            pool.dma_start(X[:, 4, :], A["x_prompt"][0]).then_inc(d_xr, 16)

            for l in range(2):
                m = MS[l]
                if l == 1:
                    pool.wait_ge(x_ready, 10)
                    for i in range(4 * PE_TAPS):
                        j, k = i // PE_TAPS, CFK - PE_TAPS + i % PE_TAPS
                        nc.gpsimd.tensor_scalar(DG[i], ident, CW[:, 4 * k + j:4 * k + j + 1], None, ALU.mult).then_inc(tap_diag, 1)
                pool.wait_ge(const_ready, 1)
                pool.dma_start(TBL.rearrange("(p a) c -> p (a c)", p=128), NOR[:, :]).then_inc(d_init, 16)
                if l == 0:
                    filled(pool, "oaT", 3)
                else:
                    pool.wait_ge(x_ready, 10)
                pool.dma_start(LNR[:, 0, :], A["ln_g"][l, 0].partition_broadcast(128)).then_inc(d_ln, 16)
                pool.dma_start(LNR[:, 1, :], A["ln_b"][l, 0].partition_broadcast(128)).then_inc(d_ln, 16)
                pool.dma_start(WR[:, :, 0:4], A["moe_w_group"][l].rearrange("(k p) n -> p k n", p=128)).then_inc(d_wr, 16)
                pool.dma_start(WR[:, :, 4:36], A["moe_w_expert"][l].rearrange("(k p) n -> p k n", p=128)).then_inc(d_wr, 16)
                for t in range(NT):
                    pool.wait_ge(h_ready, 5 * l + t + 1)
                    pool.dma_start(HD[t * 128:(t + 1) * 128, :], HB[:, t % 2, :]).then_inc(d_hst[t % 2], 16)
                pool.wait_ge(x_ready, 10 * l + 5)
                pool.dma_start(LNR[:, 0, :], A["ln_g"][l, 1].partition_broadcast(128)).then_inc(m["s0"], 16)
                pool.dma_start(LNR[:, 1, :], A["ln_b"][l, 1].partition_broadcast(128)).then_inc(m["s1"], 16)
                pool.wait_ge(d_init, 16 * (l + 1))
                pool.wait_ge(rt_slots, l + 1)
                for k in range(2):
                    for t in range(NT):
                        nc.gpsimd.indirect_dma_start(
                            out=TBL[:, :], out_offset=bass.IndirectOffsetOnAxis(ap=GI[:, k, t:t + 1], axis=0),
                            in_=PAY[:, k, t, :], in_offset=None,
                            bounds_check=NTILE * SL - 1, oob_is_err=False).then_inc(d_scat, 16)
                pool.wait_ge(d_scat, 160 * (l + 1))
                pool.dma_start(TBR, TBL.rearrange("(n s) c -> n (s c)", s=SL)).then_inc(d_tb, 16)
                pool.wait_ge(d_hst[0], 16 * 3 * (l + 1))
                pool.wait_ge(d_hst[1], 16 * 2 * (l + 1))

                def gather(e, par, cnt, landed=None):
                    if landed is not None:
                        pool.wait_ge(m[f"g{par}"], landed)
                        pool.sem_inc(m["pool_passed"], 1)
                    nc.gpsimd.tensor_copy(IXG[0:SL, par:par + 1], TI[0:SL, bass.ds(e, 1)]).then_inc(m["s_ix"], 1)
                    pool.wait_ge(m["s_ix"], cnt)
                    pool.sem_inc(m["pool_passed"], 1)
                    nc.gpsimd.indirect_dma_start(
                        out=XG[0:SL, par, :], out_offset=None, in_=HD[:, :],
                        in_offset=bass.IndirectOffsetOnAxis(ap=IXG[0:SL, par:par + 1], axis=0),
                        bounds_check=NTOK - 1, oob_is_err=False).then_inc(m[f"g{par}"], 16)

                def tiles(n0, h0, count):
                    for u in range(count):
                        par = u % 2
                        pool.wait_ge(m["t"], n0 + (u + 1))
                        gather(n0 + (u + 2), par, n0 + n0 + (2 * u + 3), h0 + 16 * ((u + 2) // 2))
                        pool.wait_ge(m["ya"], 2 + n0 + (u + 1))
                        pool.wait_ge(m["yv"], 2 + n0 + (u + 1))
                        pool.wait_ge(m[f"s{par}"], 16 + h0 + 16 * (u // 2))
                        pool.sem_inc(m["pool_passed"], 1)
                        nc.gpsimd.tensor_copy(IXY[0:SL, par:par + 1], TY[0:SL, bass.ds(n0 + u, 1)]).then_inc(m["s_ix"], 1)
                        pool.wait_ge(m["s_ix"], n0 + n0 + (2 * u + 4))
                        pool.sem_inc(m["pool_passed"], 1)
                        nc.gpsimd.indirect_dma_start(
                            out=YD[:, :], out_offset=bass.IndirectOffsetOnAxis(ap=IXY[0:SL, par:par + 1], axis=0),
                            in_=ZT[0:SL, par, :], in_offset=None,
                            bounds_check=2 * NTOK - 1, oob_is_err=False).then_inc(m[f"s{par}"], 16)

                emptied(pool, "tb", l)
                for e in range(2):
                    gather(e, e, e + 1)
                with pool.Fori(0, NI) as i:
                    tiles(i * U, i * (8 * U), U)
                pool.wait_ge(rt_ready, l + 1)
                pairs = pool.value_load(RI[0:1, 0:1], min_val=0, max_val=NEXTRA // 2)
                with pool.If(pairs > 0):
                    with pool.Fori(0, pairs) as j:
                        tiles(j * 2 + NE, j * 16 + 8 * NE, 2)
                pool.wait_ge(m["s0"], pairs * 16 + (16 + 8 * NE))
                pool.wait_ge(m["s1"], pairs * 16 + (16 + 8 * NE))
                pool.wait_ge(m["g0"], pairs * 16 + (16 + 8 * NE))
                pool.wait_ge(m["g1"], pairs * 16 + (16 + 8 * NE))
                pool.sem_inc(moe_done, 1)

                def affine(t):
                    b = (10 * l + 5 + t) % 2
                    pool.wait_ge(m["s0"], pairs * 16 + (16 + 8 * NE))
                    pool.wait_ge(ln_normed, 5 * l + t + 1)
                    chain(nc.gpsimd.tensor_tensor(ZT[:, b, :], ZT[:, b, :], LNR[:, 0, :], ALU.mult))
                    nc.gpsimd.tensor_tensor(X[:, t, :], ZT[:, b, :], LNR[:, 1, :], ALU.add).then_inc(x_ready, 1)
                for t in range(NT):
                    affine(t)
            pool.wait_ge(d_kv_out, 32)
            pool.wait_ge(d_state, 64)

        @block.scalar
        def _(act):
            steps = [0]

            def chain(ins):
                steps[0] += 1
                ins.then_inc(act_step, 1)
                act.wait_ge(act_step, steps[0])

            A_ = nc.scalar.activation

            def h_evac0():
                l = 0
                for c in range(4):
                    emptied(act, "modb", l, c)
                shift, scale = MC[:, l, 0], MC[:, l, 1]
                for k in range(0, KD, 2):
                    filled(act, "xT", l, k)
                    A_(HT[:, k, 0:512], ps("xT", l, k)[:, 0:512], ACT.Identity,
                       bias=shift[:, k, 0:1], scale=scale[:, k, 0:1])
                    release(A_(HT[:, k, 512:640], ps("xT", l, k)[:, 512:640], ACT.Identity,
                               bias=shift[:, k, 1:2], scale=scale[:, k, 1:2]), "xT", l, k)

            act.dma_start(V1[0:8, :], A["c"][0].rearrange("(k p) -> k p", p=128)).then_inc(d_vec_a, 16)
            act.dma_start(V1[8:16, :], A["c_ctx"].rearrange("(k p) -> k p", p=128)).then_inc(d_vec_a, 16)
            act.dma_start(V2[0:16, :], A["hgrn_lb_logits"].rearrange("r d (h p) -> (r d h) p", p=128)).then_inc(d_vec_a, 16)
            act.dma_start(V3[:, :], A["cf_conv_w"][0].rearrange("t (k p) -> (t k) p", p=128)).then_inc(d_vec_a, 16)
            act.wait_ge(d_vec_a, 16 * 4)
            A_(V1[:, :], V1[:, :], ACT.Silu).then_inc(c_silu, 1)
            act.wait_ge(lb_exp_in, 1)
            A_(LBS[:, 0:2, :], LBS[:, 0:2, :], ACT.Exp).then_inc(lb_exp, 1)

            def h_evac1(t):
                g = 0 if t < 4 else 1
                filled(act, "xT", 1, t)
                for k in range(KD):
                    ins = A_(HT[:, k, t * 128:t * 128 + 128], ps("xT", 1, t)[:, k * 128:k * 128 + 128], ACT.Identity,
                             bias=MC[:, 1, 0, k, g:g + 1], scale=MC[:, 1, 1, k, g:g + 1])
                release(ins, "xT", 1, t)

            h_evac0()
            for t in range(NT):
                filled(act, "cq", t)
                release(A_(CQ[:, t, :], ps("cq", t)[:, 0:672], ACT.Copy), "cq", t)
            for t in range(NT):
                emptied(act, "cq", t)
                A_(z(6816 + 640 * t, QR), CQ[:, t, 0:QR], ACT.Square, accum_out=SS[:, t, 0:1])
                A_(z(6816 + 640 * t + QR, KVR), CQ[:, t, QR:QR + KVR], ACT.Square, accum_out=SS[:, t, 1:2]).then_inc(sq_ready, 1)
            act.wait_ge(rms_in, 1)
            A_(RR[:, :, :], RR[:, :, :], ACT.Sqrt).then_inc(rms_sd, 1)
            for r in range(2):
                filled(act, "ckvT", r)
                release(A_(CKVT[:, r, :], ps("ckvT", r)[:, 0:768], ACT.Copy), "ckvT", r)
            for t in range(6):
                filled(act, "v", t)
                release(A_(VT[:, t, :], ps("v", t)[:, 0:512], ACT.Copy), "v", t)

            def kq_evac(h):
                b = h % 2
                filled(act, "k", h)
                release(A_(KT[0:64, b, :], ps("k", h)[0:64, 0:768], ACT.Copy), "k", h)
                filled(act, "q", h)
                ins = A_(QT[0:96, b, :], ps("q", h)[0:96, 0:640], ACT.Copy)
                release(ins, "q", h)

            kq_evac(0)
            n = 0
            for h in range(MH):
                for t in range(NT):
                    nk = 640 if t < 4 else 128
                    b = n % 2
                    if h + 1 < MH and t == 1:
                        kq_evac(h + 1)
                    act.wait_ge(max_ready, n + 1)
                    if n >= 2:
                        filled(act, "pt", *divmod(n - 2, NT))
                        emptied(act, "o", *divmod(n - 2, NT))
                    release(A_(PB[:, b, 0:nk], ps("s", h, t)[:, 0:nk], ACT.Exp, bias=MXS[:, b, 1:2], scale=SCALE,
                               accum_out=SUM[:, b, 0:1]), "s", h, t)
                    filled(act, "pt", h, t)
                    release(A_(PTS[:, b, 0:nk], ps("pt", h, t)[:, 0:nk], ACT.Copy), "pt", h, t)
                    n += 1
            for j in range(4):
                filled(act, "obT", j)
                release(A_(OT[:, 4 + j, :], ps("obT", j)[:, 0:640], ACT.Copy), "obT", j)

            act.wait_ge(d_kv_out, 32)
            for c in range(3):
                for j in range(4):
                    filled(act, "hq", c, j)
                    dst = [HQ, HF[0], HF[1]][c]
                    release(A_(dst[:, j, :], ps("hq", c, j)[:, 0:640], ACT.Silu if c == 0 else ACT.Sigmoid), "hq", c, j)
            for t in range(NT):
                filled(act, "hv", 1, t)
                ins = A_(HG[:, t, :], ps("hv", 1, t)[:, 0:512], ACT.Silu)
                release(ins, "hv", 1, t)
            for u in range(4):
                d, hp = u // 2, u % 2
                act.wait_ge(h_f, u + 1)
                A_(BUFL[:, :, :], HF[d][:, 2 * hp:2 * hp + 2, :], ACT.Ln).then_inc(h_l, 1)
                act.wait_ge(h_arg, u + 1)
                if u:
                    filled(act, "ho", u - 1, 4)
                mid, full = (BUFA, BUFB) if d == 0 else (BUFB, BUFA)
                A_(QHAT[:, :, :], mid[:, :, :], ACT.Exp).then_inc(h_exp, 1)
                A_(KHAT[:, :, :], mid[:, :, :], ACT.Exp, scale=-1.0).then_inc(h_exp, 1)
                A_(KTIL[:, :, :], BUFL[:, :, :], ACT.Exp).then_inc(h_exp, 1)
                A_(QTIL[:, :, :], full[:, :, :], ACT.Exp).then_inc(h_exp, 1)
                e = CH - 1 if d == 0 else 0
                A_(DEC[:, :, :], full[:, :, :].rearrange("p h (c s) -> p h c s", s=CH)[:, :, :, e], ACT.Exp).then_inc(h_exp, 1)
                for n in range(NT):
                    i = 5 * u + n
                    t = (n if d == 0 else 3 - n) if n < 4 else 4
                    filled(act, "hk", u, n)
                    if i >= 2:
                        filled(act, "hd", *divmod(i - 2, 5))
                    release(A_(KTT[:, i % 2, :], ps("hk", u, n)[:, 0:256], ACT.Copy), "hk", u, n)
                    if u == 3 and n == 2:
                        act.wait_ge(o_var, 1)
                        A_(HSS[:, 0, :], HSS[:, 0, :], ACT.Sqrt).then_inc(o_sd, 1)
                    if d == 0 and n >= 1:
                        tt = n - 1
                        filled(act, "ho", u, tt)
                        release(A_(HO[:, tt, 256 * hp:256 * hp + 256], ps("ho", u, tt)[:, 0:256], ACT.Copy), "ho", u, tt)
                if d == 0:
                    filled(act, "ho", u, 4)
                    release(A_(HO[:, 4, 256 * hp:256 * hp + 256], ps("ho", u, 4)[:, 0:256], ACT.Copy), "ho", u, 4)
            act.wait_ge(o_var, 2)
            A_(HSS[:, 1, :], HSS[:, 1, :], ACT.Sqrt).then_inc(o_sd, 1)
            act.wait_ge(d_state, 64)
            for j in range(4):
                filled(act, "oaT", j)
                release(A_(OT[:, j, :], ps("oaT", j)[:, 0:640], ACT.Copy), "oaT", j)

            def ln_sqrt(q):
                act.wait_ge(ln_var, q + 1)
                A_(RSD[:, q % 2, 0:1], RSD[:, q % 2, 0:1], ACT.Sqrt).then_inc(ln_sd, 1)

            for l in range(2):
                m = MS[l]
                if l == 1:
                    act.wait_ge(cd_pad, 2)
                    for c in CD_ORDER:
                        f = ACT.Sigmoid if c == 4 else ACT.Copy
                        for j in range(4):
                            filled(act, "cd", c, j)
                            src = ps("cd", c, j)
                            if c == 0:
                                release(A_(BG[:, j, :], src[:, 0:640], f), "cd", c, j)
                            elif c == 2:
                                release(A_(SQ[:, j, 0:640], src[:, 0:640], f), "cd", c, j)
                            elif c == 4:
                                ins = A_(CO[:, j, 0:640], src[:, 0:640], f)
                                release(ins, "cd", c, j)
                            else:
                                dst = CXP if c == 1 else UP
                                A_(dst[:, j, 15:527], src[:, 0:512], f)
                                release(A_(dst[:, j, 542:670], src[:, 512:640], f), "cd", c, j)
                    emptied(act, "mean")
                    A_(SQ[:, :, :], CO[:, :, :], ACT.Square).then_inc(cd_sq, 1)
                    emptied(act, "var")
                    A_(RST[:, :], RST[:, :], ACT.Sqrt).then_inc(cd_sd, 1)
                    for j in range(4):
                        act.wait_ge(cd_u, j + 1)
                        A_(OT[:, 4 + j, 0:512], CO[:, j, 0:512], ACT.Silu, bias=VC[:, 27 + j:28 + j], scale=VC[:, 23 + j:24 + j])
                        A_(OT[:, 4 + j, 512:640], CO[:, j, 527:655], ACT.Silu, bias=VC[:, 27 + j:28 + j],
                           scale=VC[:, 23 + j:24 + j]).then_inc(cd_out, 1)
                for t in range(NT + 2):
                    if t < NT:
                        ln_sqrt(10 * l + t)
                    if t < 2:
                        continue
                    t -= 2
                    filled(act, "hT", l, t)
                    release(A_(HT[:, :, t * 128:(t + 1) * 128],
                               ps("hT", l, t).rearrange("p (k c) -> p k c", k=8), ACT.Copy), "hT", l, t)
                act.wait_ge(rt_exp_in, 2 * l + 1)
                A_(RT[:, 0, 0:20], RT[:, 0, 0:20], ACT.Exp).then_inc(rt_exp, 1)
                act.wait_ge(rt_exp_in, 2 * l + 2)
                A_(RS[:, 5, 0:5], RS[:, 5, 0:5], ACT.Exp).then_inc(rt_exp, 1)
                def tiles(n0, h0, count):
                    def out_half(u):
                        act.wait_ge(m["down"], n0 + (u + 1))
                        act.wait_ge(m[f"s{u % 2}"], 16 + h0 + 16 * (u // 2))
                        A_(ZT[0:SL, u % 2, 0:512], result_bank(u, 0), ACT.Copy).then_inc(m["ya"], 1)

                    for u in range(count):
                        act.wait_ge(m["t"], n0 + (u + 1))
                        if u >= 2:
                            act.wait_ge(m["gu"], n0 + (u - 1))
                        A_(XGT[:, u % 2, 0:4 * SL], turned_bank(0), ACT.Copy).then_inc(m["xa"], 1)
                        if u >= 1:
                            out_half(u - 1)
                        act.wait_ge(m["gu"], n0 + (u + 1))
                        A_(SG[:, u % 2, 0:SL], bank(2 + u % 2)[:, 0:SL], ACT.Silu).then_inc(m["sg"], 1)
                    out_half(count - 1)
                emptied(act, "tb", l)
                act.sem_inc(m["xa"], 1)
                act.sem_inc(m["ya"], 2)
                with act.Fori(0, NI) as i:
                    tiles(i * U, i * (8 * U), U)
                act.wait_ge(rt_ready, l + 1)
                pairs = act.value_load(RI[0:1, 0:1], min_val=0, max_val=NEXTRA // 2)
                with act.If(pairs > 0):
                    with act.Fori(0, pairs) as j:
                        tiles(j * 2 + NE, j * 16 + 8 * NE, 2)
                def scale_first(t):
                    yb = t % 2
                    act.wait_ge(d_yl[yb], ((3 if yb == 0 else 2) * l + t // 2 + 1) * 32)
                    A_(YB[:, yb, 0, :], YB[:, yb, 0, :], ACT.Copy, scale=W12[:, 0, t:t + 1]).then_inc(y_scaled, 1)

                if l == 0:
                    for c in range(4):
                        emptied(act, "modb", 1, c)
                scale_first(0)
                for t in range(NT):
                    q, b = 10 * l + 5 + t, (10 * l + 5 + t) % 2
                    if t + 1 < NT:
                        scale_first(t + 1)
                    ln_sqrt(q)
                    act.wait_ge(ln_shift, 5 * l + t + 1)
                    A_(ZT[:, b, :], ZT[:, b, :], ACT.Identity, bias=NB[:, b:b + 1], scale=RSD[:, b, 1:2]).then_inc(ln_normed, 1)
                    if l == 0 and t >= 1:
                        h_evac1(t - 1)
                if l == 0:
                    h_evac1(4)

        @block.vector
        def _(dve):
            steps = [0]
            V = nc.vector

            def chain(ins):
                steps[0] += 1
                ins.then_inc(vec_step, 1)
                dve.wait_ge(vec_step, steps[0])

            def mod_row(l, c):
                filled(dve, "mod", l, c)
                s = WITEM[("mod", l, c)]["slot"]
                dve.wait_ge(w_full[s], WITEM[("mod", l, c)]["value"])
                if l or c >= 2:
                    pl, pc = divmod(12 * l + c - 2, 12)
                    if pc < 4:
                        filled(dve, "modb", pl, pc)
                    else:
                        dve.wait_ge(d_mr[c % 2], 16 * rows_stored(pl, pc))
                release(V.scalar_tensor_tensor(out=MR[:, c % 2, :], in0=ps("mod", l, c)[0:2, 0:512],
                                               scalar=float(c // 2 == 4), in1=MB[s], op0=ALU.add, op1=ALU.add), "mod", l, c)

            def mod_columns(l, c):
                filled(dve, "modb", l, c)
                i, half = c // 2, c % 2
                src = ps("modb", l, c)[:, 0:8].rearrange("p (k g) -> p k g", g=2)
                release(V.tensor_scalar(MC[:, l, i, 4 * half:4 * half + 4, :], src, float(i), None, ALU.add), "modb", l, c)

            def drain_mod(kind, l, c):
                (mod_row if kind == "mod" else mod_columns)(l, c)

            def h_evac0():
                l = 0
                for c in range(4):
                    emptied(dve, "modb", l, c)
                for k in range(1, KD, 2):
                    filled(dve, "xT", l, k)
                    for g, (a, b) in enumerate(((0, 512), (512, 640))):
                        ins = V.tensor_scalar(HT[:, k, a:b], ps("xT", l, k)[:, a:b], MC[:, l, 1, k, g:g + 1],
                                              MC[:, l, 0, k, g:g + 1], ALU.mult, ALU.add)
                    release(ins, "xT", l, k)

            filled(dve, "vec")
            chain(V.tensor_copy(CT[:, :], ps("vec")[:, 0:16]))
            chain(V.tensor_copy(VC[:, :], ps("vec")[:, 16:59]))
            ins = V.tensor_copy(CW[:, :], ps("vec")[:, 64:188])
            release(ins, "vec")
            chain(V.tensor_tensor(LBS[:, 2, :], VC[:, 0:8], VC[:, 8:16], ALU.max))
            chain(V.tensor_tensor(LBS[:, 0, :], VC[:, 0:8], LBS[:, 2, :], ALU.subtract))
            V.tensor_tensor(LBS[:, 1, :], VC[:, 8:16], LBS[:, 2, :], ALU.subtract).then_inc(lb_exp_in, 1)
            dve.wait_ge(lb_exp, 1)
            chain(V.tensor_tensor(LBS[:, 2, :], LBS[:, 0, :], LBS[:, 1, :], ALU.add))
            chain(V.reciprocal(LBS[:, 2, :], LBS[:, 2, :]))
            chain(V.tensor_tensor(LBT[:, 0, :], LBS[:, 0, :], LBS[:, 2, :], ALU.mult))
            chain(V.tensor_tensor(LBT[:, 1, :], LBS[:, 1, :], LBS[:, 2, :], ALU.mult))
            dve.wait_ge(d_const, 16)
            for k in range(2):
                for t in range(NT):
                    for c in range(2):
                        ins = V.tensor_scalar(PAY[:, k, t, c:c + 1], const("pidx"), 128.0 * t + k * c * NTOK, None, ALU.add)
            chain(ins)
            V.memset(NOR[:, :], NOROW).then_inc(const_ready, 1)
            for kind, c in FIRST_MODS:
                drain_mod(kind, 0, c)
            h_evac0()

            dve.wait_ge(sq_ready, NT)
            chain(V.tensor_scalar(RR[:, :, 0:1], SS[:, :, 0:1], 1.0 / QR, RMS_EPS, ALU.mult, ALU.add))
            V.tensor_scalar(RR[:, :, 1:2], SS[:, :, 1:2], 1.0 / KVR, RMS_EPS, ALU.mult, ALU.add).then_inc(rms_in, 1)
            dve.wait_ge(rms_sd, 1)
            chain(V.reciprocal(RR[:, :, :], RR[:, :, :]))
            dve.wait_ge(d_rows, 32)
            for t in (4, 0, 1, 2, 3):
                V.tensor_scalar(CQ[:, t, 0:QR], CQ[:, t, 0:QR], RR[:, t, 0:1], None, ALU.mult)
                V.scalar_tensor_tensor(out=CQ[:, t, QR:QR + KVR], in0=CQ[:, t, QR:QR + KVR], scalar=RR[:, t, 1:2],
                                       in1=CKG[:, :], op0=ALU.mult, op1=ALU.mult).then_inc(norm_ready, 1)
            for r in range(3):
                filled(dve, "cqT", r)
                release(V.tensor_scalar(CQT[:, r, :], ps("cqT", r)[:, 0:640], VC[:, 16 + r:17 + r], None, ALU.mult), "cqT", r)
            filled(dve, "krT")
            rp = slice(64, 96)
            chain(V.tensor_copy(KT[rp, 0, 512:768], ps("krT")[rp, 512:768]))
            chain(V.tensor_copy(KT[rp, 1, 512:768], ps("krT")[rp, 512:768]))
            release(V.tensor_copy(KRS[rp, :], ps("krT")[rp, 0:512]), "krT")
            emptied(dve, "krT")
            cosr, sinr = const("cos", rp), const("sin", rp)
            filled(dve, "krP")
            release(V.tensor_tensor(ROT1[rp, :], ps("krP")[rp, 0:512], sinr, ALU.mult), "krP")
            chain(V.tensor_tensor(ROT2[rp, :], KRS[rp, :], cosr, ALU.mult))
            emptied(dve, "krP")
            V.tensor_tensor(KT[rp, 0, 0:512], ROT1[rp, :], ROT2[rp, :], ALU.add).then_inc(kr_ready, 1)
            V.tensor_tensor(KT[rp, 1, 0:512], ROT1[rp, :], ROT2[rp, :], ALU.add).then_inc(kr_ready, 1)
            dve.wait_ge(kr_ready, 2)

            def rotate_q(h):
                b = h % 2
                filled(dve, "qP", h)
                release(V.tensor_tensor(ROT1[rp, :], ps("qP", h)[rp, 0:512], sinr, ALU.mult), "qP", h)
                emptied(dve, "q", h)
                chain(V.tensor_tensor(ROT2[rp, :], QT[rp, b, 0:512], cosr, ALU.mult))
                emptied(dve, "qP", h)
                V.tensor_tensor(QT[rp, b, 0:512], ROT1[rp, :], ROT2[rp, :], ALU.add).then_inc(q_rot, 1)
                dve.wait_ge(q_rot, h + 1)

            def attend_out(n):
                h, t = divmod(n, NT)
                b = n % 2
                filled(dve, "o", h, t)
                emptied(dve, "s", h, t)
                chain(V.reciprocal(SUM[:, b, 1:2], SUM[:, b, 0:1]))
                release(V.tensor_scalar(OB[:, t, h * 64:h * 64 + 64], ps("o", h, t)[:, 0:64], SUM[:, b, 1:2], None,
                                        ALU.mult), "o", h, t)

            rotate_q(0)
            n = 0
            for h in range(MH):
                for t in range(NT):
                    nk = 640 if t < 4 else 128
                    b = n % 2
                    filled(dve, "s", h, t)
                    if n >= 2:
                        emptied(dve, "s", *divmod(n - 2, NT))
                    chain(V.tensor_reduce(MXS[:, b, 0:1], ps("s", h, t)[:, 0:nk], AX.X, ALU.max, negate=True))
                    V.tensor_scalar(MXS[:, b, 1:2], MXS[:, b, 0:1], SCALE, None, ALU.mult).then_inc(max_ready, 1)
                    if n >= 1:
                        attend_out(n - 1)
                    if t == ATTN_MOD_TILE + 1:
                        mod_row(0, 4 + h)
                    if h + 1 < MH and t == 3:
                        rotate_q(h + 1)
                    n += 1
            attend_out(n - 1)

            for t in range(NT):
                filled(dve, "hv", 0, t)
                release(V.tensor_copy(HV[:, t, :], ps("hv", 0, t)[:, 0:512]), "hv", 0, t)
            dve.wait_ge(h_zero, 3)
            scan_mask = const("scan")

            SQB = [z(2560, 1280), HTF[:, 0:1280]]

            def two_heads(base, hp):
                return z(base, 2560).rearrange("p (t h v) -> p t h v", t=NT, h=4)[:, :, 2 * hp:2 * hp + 2, :]

            def head_norm_squares(hp):
                emptied(dve, "ho", 2 + hp, 4)
                ho = two_heads(12800, hp)
                chain(V.tensor_tensor(SQB[hp].rearrange("p (t h v) -> p t h v", t=NT, h=2), ho, ho, ALU.mult))
                chain(V.tensor_reduce(HSS[:, hp, :], SQB[hp].rearrange("p (g v) -> p g v", v=128), AX.X, ALU.add))
                V.tensor_scalar(HSS[:, hp, :], HSS[:, hp, :], 1.0 / DK, RMS_EPS, ALU.mult, ALU.add).then_inc(o_var, 1)

            def head_norm_scale(hp):
                ho = two_heads(12800, hp)
                dve.wait_ge(o_sd, hp + 1)
                chain(V.reciprocal(HSS[:, hp, :], HSS[:, hp, :]))
                scale = HSS[:, hp, :].rearrange("p (t h) -> p t h", t=NT).unsqueeze(3).to_broadcast([128, NT, 2, 128])
                chain(V.tensor_tensor(ho, ho, scale, ALU.mult))

            def head_norm_gate(hp):
                ho = two_heads(12800, hp)
                dve.wait_ge(o_gate, 1)
                V.tensor_tensor(ho, ho, two_heads(10240, hp), ALU.mult).then_inc(o_ready, 1)
            for u in range(4):
                d, hp = u // 2, u % 2
                F = HF[d][:, 2 * hp:2 * hp + 2, :]
                emptied(dve, "hq", 1 + d, 2 * hp + 1)
                for hh in range(2):
                    hd = d * 4 + 2 * hp + hh
                    ins = V.tensor_scalar(F[:, hh, :], F[:, hh, :], LBT[:, 1, hd:hd + 1], LBT[:, 0, hd:hd + 1], ALU.mult, ALU.add)
                    if hh == 0:
                        chain(ins)
                ins.then_inc(h_f, 1)
                dve.wait_ge(h_l, u + 1)
                if u >= 2:
                    emptied(dve, "ho", u - 2, 4)
                chain(V.tensor_scalar(F, F, -1.0, 1.0, ALU.mult, ALU.add))
                for hh in range(2):
                    ins = V.tensor_tensor_scan(BUFB[:, hh, :], scan_mask, BUFL[:, hh, :], 0.0, ALU.mult, ALU.add)
                    chain(ins)
                B4 = BUFB[:, :, :].rearrange("p h (c s) -> p (h c) s", s=CH)
                A4 = BUFA[:, :, :].rearrange("p h (c s) -> p (h c) s", s=CH)
                L4 = BUFL[:, :, :].rearrange("p h (c s) -> p (h c) s", s=CH)
                if d == 0:
                    chain(V.tensor_tensor(A4, B4, B4[:, :, 15:16].to_broadcast([128, 40, CH]), ALU.subtract))
                    V.tensor_tensor(L4, B4[:, :, 31:32].to_broadcast([128, 40, CH]), B4, ALU.subtract).then_inc(h_arg, 1)
                else:
                    chain(V.tensor_tensor(L4, B4, L4, ALU.subtract))
                    chain(V.tensor_tensor(A4, B4[:, :, 31:32].to_broadcast([128, 40, CH]), L4, ALU.subtract))
                    V.tensor_tensor(B4, A4, A4[:, :, 16:17].to_broadcast([128, 40, CH]), ALU.subtract).then_inc(h_arg, 1)
                drain_mod(*UNIT_MODS[u][0])
                Q = HQ[:, 2 * hp:2 * hp + 2, :]
                for k, (dst, src) in enumerate(((QHAT, Q), (KHAT, F), (KTIL, F), (QTIL, Q))):
                    dve.wait_ge(h_exp, 5 * u + k + 1)
                    V.tensor_tensor(dst[:, :, :], dst[:, :, :], src, ALU.mult).then_inc(h_mul, 1)
                drain_mod(*UNIT_MODS[u][1])
                dve.wait_ge(h_exp, 5 * u + 5)
                dve.wait_ge(h_s0, 16 * (u + 1))

                def out_add(n):
                    t = (3 - n) if n < 4 else 4
                    filled(dve, "ho", u, n)
                    dst = HO[:, t, 256 * hp:256 * hp + 256]
                    release(V.tensor_tensor(dst, ps("ho", u, n)[:, 0:256], dst, ALU.add), "ho", u, n)
                mask = const("mask_f" if d == 0 else "mask_b").bitcast(i32).unsqueeze(1).to_broadcast([128, 2, 128])
                for n in range(NT):
                    i = 5 * u + n
                    t = (n if d == 0 else 3 - n) if n < 4 else 4
                    if i >= 2:
                        filled(dve, "ho", *divmod(i - 2, 5))
                    filled(dve, "hs", u, n)
                    release(V.copy_predicated(SC[:, d, i % 2, :, :], mask,
                                              ps("hs", u, n)[:, 0:256].rearrange("p (h t) -> p h t", h=2)), "hs", u, n)
                    filled(dve, "hd", u, n)
                    if i >= 3:
                        if n == 2 and u >= 1:
                            dve.wait_ge(d_state, 16 * u)
                    for step in range(4):
                        j = step if d == 0 else 3 - step
                        for hh in range(2):
                            prev = state_before(i, n, step, hh)
                            nxt = ST[:, i % 2, hh, step, :] if step < 3 else CAR[:, i % 3, hh, :]
                            ins = V.scalar_tensor_tensor(out=nxt, in0=prev, scalar=DEC[:, hh, t * 4 + j:t * 4 + j + 1],
                                                         in1=ps("hd", u, n)[:, hh * 512 + j * 128:hh * 512 + (j + 1) * 128],
                                                         op0=ALU.mult, op1=ALU.add)
                            if step == 3 and hh == 1:
                                release(ins, "hd", u, n)
                            elif hh == 1 or step == 3:
                                chain(ins)
                            else:
                                steps[0] += 1
                                ins.then_inc(vec_step, 1)
                    emptied(dve, "hd", u, n)
                    if d == 1 and n >= 1:
                        out_add(n - 1)
                    for piece in STEP_MODS.get((u, n - 1), []):
                        drain_mod(*piece)
                    if u == 3 and n in (1, 3, 4):
                        {1: head_norm_squares, 3: head_norm_scale, 4: head_norm_gate}[n](0)
                if d == 1:
                    out_add(4)
            head_norm_squares(1)
            head_norm_scale(1)
            head_norm_gate(1)

            def ln_first(q):
                b = q % 2
                for s in range(2):
                    V.bn_stats(ST6[:, b, s, :], ZT[:, b, s * 512:s * 512 + 512]).then_inc(vec_step, 1)
                    steps[0] += 1
                dve.wait_ge(vec_step, steps[0])
                chain(V.bn_aggr(MV[:, b, :], ST6[:, b, :, :]))
                V.tensor_scalar(RSD[:, b, 0:1], MV[:, b, 1:2], LN_EPS, None, ALU.add).then_inc(ln_var, 1)

            def ln_second(q, t, l):
                b = q % 2
                dve.wait_ge(ln_sd, q + 1)
                chain(V.reciprocal(RSD[:, b, 1:2], RSD[:, b, 0:1]))
                chain(V.tensor_scalar(ZT[:, b, :], ZT[:, b, :], MV[:, b, 0:1], RSD[:, b, 1:2], ALU.subtract, ALU.mult))
                dve.wait_ge(d_ln, 32 * (l + 1))
                chain(V.tensor_tensor(ZT[:, b, :], ZT[:, b, :], LNR[:, 0, :], ALU.mult))
                V.tensor_tensor(X[:, t, :], ZT[:, b, :], LNR[:, 1, :], ALU.add).then_inc(x_ready, 1)
                dve.wait_ge(x_ready, q + 1)

            def first_max(src, n, prio, out, tmp, mx):
                chain(V.tensor_reduce(mx, src, AX.X, ALU.max))
                mb = mx.unsqueeze(2).to_broadcast([128, NT, n])
                chain(V.tensor_tensor(out, src, mb, ALU.is_equal))
                chain(V.tensor_tensor(out, out, prio.unsqueeze(1).to_broadcast([128, NT, n]), ALU.mult))
                chain(V.tensor_reduce(tmp, out, AX.X, ALU.max))
                chain(V.tensor_tensor(out, out, tmp.unsqueeze(2).to_broadcast([128, NT, n]), ALU.is_equal))

            def gated_convolutions():
                segs = ((0, 15, 512), (512, 542, 128))
                for j in range(4):
                    emptied(dve, "cd", 4, j)
                    for t0, p0, w in segs:
                        ins = V.tensor_tensor(UP[:, j, p0:p0 + w], UP[:, j, p0:p0 + w], CO[:, j, t0:t0 + w], ALU.mult)
                ins.then_inc(cd_up, 1)
                dve.wait_ge(cd_up, 1)
                V.memset(CO[:, :, 655:656], 0.0)
                for k in range(CFK - PE_TAPS):
                    for j in range(4):
                        src = UP[:, j, k:k + 655]
                        tap = CW[:, 4 * k + j:4 * k + j + 1]
                        dst = CO[:, j, 0:655]
                        if k == 0:
                            ins = V.tensor_scalar(dst, src, tap, VC[:, 19 + j:20 + j], ALU.mult, ALU.add)
                        else:
                            ins = V.scalar_tensor_tensor(out=dst, in0=src, scalar=tap, in1=dst, op0=ALU.mult, op1=ALU.add)
                    chain(ins)
                emptied(dve, "cd", 2, 3)
                for t0, p0, w in segs:
                    ins = V.tensor_tensor(CXP[:, :, p0:p0 + w], SQ[:, :, t0:t0 + w], CXP[:, :, p0:p0 + w], ALU.mult)
                chain(ins)
                for k in range(SCK):
                    for j in range(4):
                        for t0, p0, w in segs:
                            src = CXP[:, j, p0 + k - 1:p0 + k - 1 + w]
                            tap = VC[:, 31 + 4 * k + j:32 + 4 * k + j]
                            dst = OT[:, j, t0:t0 + w]
                            if k == 0:
                                ins = V.tensor_scalar(dst, src, tap, None, ALU.mult)
                            else:
                                ins = V.scalar_tensor_tensor(out=dst, in0=src, scalar=tap, in1=dst, op0=ALU.mult, op1=ALU.add)
                    chain(ins)
                V.tensor_tensor(OT[:, 0:4, :], OT[:, 0:4, :], BG[:, :, :], ALU.mult).then_inc(cd_out_v, 1)
                for j in range(4):
                    filled(dve, "cv", j)
                    V.tensor_tensor(CO[:, j, 0:512], ps("cv", j)[:, 0:512], CO[:, j, 0:512], ALU.add).then_inc(cd_conv, 1)
                    release(V.tensor_tensor(CO[:, j, 527:655], ps("cv", j)[:, 512:640], CO[:, j, 527:655], ALU.add), "cv", j)
                emptied(dve, "cv", 3)

                def two(ap):
                    return ap.rearrange("p (b c) -> p b c", b=2)
                filled(dve, "mean")
                mean = two(ps("mean"))[:, :, 0:328]
                dve.wait_ge(cd_conv, 4)
                for j in range(4):
                    ins = V.scalar_tensor_tensor(out=two(CO[:, j, :]), in0=mean, scalar=-1.0 / 512, in1=two(CO[:, j, :]),
                                                 op0=ALU.mult, op1=ALU.add)
                release(ins, "mean")
                emptied(dve, "mean")
                filled(dve, "var")
                release(V.tensor_scalar(two(RST), two(ps("var"))[:, :, 0:328], 1.0 / 512, LN_EPS, ALU.mult, ALU.add), "var")
                dve.wait_ge(cd_sd, 1)
                chain(V.reciprocal(RST, RST))
                for j in range(4):
                    V.tensor_tensor(CO[:, j, :], CO[:, j, :], RST, ALU.mult).then_inc(cd_u, 1)

            for l in range(2):
                m = MS[l]
                if l == 1:
                    dve.wait_ge(x_ready, 10)
                    V.memset(CXP[:, :, :], 0.0).then_inc(cd_pad, 1)
                    V.memset(UP[:, :, :], 0.0).then_inc(cd_pad, 1)
                    gated_convolutions()
                if l == 0:
                    dve.wait_ge(d_xr, 32)
                dve.wait_ge(d_g1, 16 * (l + 1))

                def mod_for_experts(t):
                    b, g = t % 2, (0 if t < 4 else 1)
                    if t == 0:
                        dve.wait_ge(d_r, 48 * (l + 1))
                    if t >= 2:
                        filled(dve, "hT", l, t - 2)
                        dve.wait_ge(d_hst[b], 16 * ((3 if b == 0 else 2) * l + (t - 2) // 2 + 1))
                    chain(V.tensor_tensor(HB[:, b, :], X[:, t, :], R4[:, g, :], ALU.mult))
                    V.tensor_tensor(HB[:, b, :], HB[:, b, :], R3[:, g, :], ALU.add).then_inc(h_ready, 1)

                def logits(t):
                    filled(dve, "lg", l, t)
                    release(V.tensor_copy(LG[:, t, :], ps("lg", l, t)[:, 0:36]), "lg", l, t)

                for t in range(NT):
                    q, g = 10 * l + t, (0 if t < 4 else 1)
                    b = q % 2
                    filled(dve, "y", l, t)
                    release(V.tensor_tensor(ZT[:, b, :], ps("y", l, t), G1[:, g, :], ALU.mult), "y", l, t)
                    emptied(dve, "y", l, t)
                    chain(V.scalar_tensor_tensor(out=ZT[:, b, :], in0=X[:, t, :], scalar=ALPHA, in1=ZT[:, b, :],
                                                 op0=ALU.mult, op1=ALU.add))
                    ln_first(q)
                    if t >= 1:
                        ln_second(q - 1, t - 1, l)
                        mod_for_experts(t - 1)
                    if t == 4:
                        logits(0)
                ln_second(10 * l + 4, 4, l)
                mod_for_experts(4)
                for t in range(1, NT):
                    logits(t)
                emptied(dve, "lg", l, 4)

                gl, el = LG[:, :, 0:4], LG[:, :, 4:36]
                gm, tmp, m1, m2, sume, ex, pg = [RS[:, i, 0:5] for i in range(7)]
                first_max(gl, 4, const("prio4"), O4[:, :, :], tmp, gm)
                D4 = RT[:, 0, 0:20].rearrange("p (t g) -> p t g", t=NT)
                V.tensor_tensor(D4, gl, gm.unsqueeze(2).to_broadcast([128, NT, 4]), ALU.subtract).then_inc(rt_exp_in, 1)
                E4 = RT[:, 1, :].rearrange("p (t g e) -> p t g e", t=NT, g=4)
                o4b = O4[:, :, :].unsqueeze(3).to_broadcast([128, NT, 4, 8])
                chain(V.tensor_tensor(E4, el.rearrange("p t (g e) -> p t g e", g=4), o4b, ALU.mult))
                EI = RT[:, 2, 0:40].rearrange("p (t e) -> p t e", t=NT)
                chain(V.tensor_reduce(EI, RT[:, 1, :].rearrange("p (t g e) -> p t e g", t=NT, g=4), AX.X, ALU.add))
                O1 = RT[:, 2, 40:80].rearrange("p (t e) -> p t e", t=NT)
                O2 = RT[:, 2, 80:120].rearrange("p (t e) -> p t e", t=NT)
                first_max(EI, 8, const("prio8"), O1, tmp, m1)
                chain(V.scalar_tensor_tensor(out=RT[:, 2, 0:40], in0=RT[:, 2, 40:80], scalar=-3.0e38, in1=RT[:, 2, 0:40],
                                             op0=ALU.mult, op1=ALU.add))
                first_max(EI, 8, const("prio8"), O2, tmp, m2)
                V.tensor_tensor(ex, m2, m1, ALU.subtract).then_inc(rt_exp_in, 1)
                dve.wait_ge(rt_exp, 2 * l + 2)
                chain(V.tensor_reduce(sume, D4, AX.X, ALU.add))
                chain(V.tensor_scalar(pg, ex, 1.0, None, ALU.add))
                chain(V.tensor_tensor(pg, pg, sume, ALU.mult))
                chain(V.reciprocal(W12[:, 0, :], pg))
                chain(V.tensor_tensor(W12[:, 1, :], W12[:, 0, :], ex, ALU.mult))
                M1 = RT[:, 3, :].rearrange("p (t g e) -> p t g e", t=NT, g=4)
                M2 = RT[:, 4, :].rearrange("p (t g e) -> p t g e", t=NT, g=4)
                chain(V.tensor_tensor(M1, o4b, O1.unsqueeze(2).to_broadcast([128, NT, 4, 8]), ALU.mult))
                chain(V.tensor_tensor(M2, o4b, O2.unsqueeze(2).to_broadcast([128, NT, 4, 8]), ALU.mult))
                V.tensor_tensor(RT[:, 5, :], RT[:, 3, :], RT[:, 4, :], ALU.add).then_inc(rt_mask, 1)
                filled(dve, "ct", l)
                chain(V.memset(RUN[:, :], 0.0))
                for t in range(NT):
                    chain(V.tensor_tensor(CM[:, t, :], ps("ct", l)[:, t * 32:t * 32 + 32], RUN[:, :], ALU.add))
                    ins = V.tensor_tensor(RUN[:, :], ps("ct", l)[:, 512 + t * 32:512 + t * 32 + 32], RUN[:, :], ALU.add)
                    if t == NT - 1:
                        release(ins, "ct", l)
                        emptied(dve, "ct", l)
                    else:
                        chain(ins)
                for k in range(1, NBLK + 1):
                    ins = V.tensor_scalar(IND[:, 32 * (k - 1):32 * k], RUN[:, :], float(SL * k), None, ALU.is_gt)
                chain(ins)
                chain(V.tensor_tensor_scan(INC, const("ones")[:, 0:NBLK * 32], IND, 0.0, ALU.mult, ALU.add))
                V.tensor_copy(BASE[:, 0:32], const("first_slot"))
                chain(V.tensor_tensor(BASE[:, 32:], INC, IND, ALU.subtract))
                for k in range(1, NBLK + 1):
                    blk = BASE[:, 32 * k:32 * k + 32]
                    ins = V.tensor_scalar(blk, blk, float(SL), float(SL * (NE - k)), ALU.mult, ALU.add)
                chain(ins)
                chain(V.tensor_tensor(DELTA, BASE[:, 32:], BASE[:, 0:NBLK * 32], ALU.subtract))
                G3 = GG.rearrange("p (t e) -> p t e", t=NT)
                T3 = GT.rearrange("p (t e) -> p t e", t=NT)
                chain(V.tensor_tensor(G3, CM[:, :, :], const("first_slot").unsqueeze(1).to_broadcast([128, NT, NE]), ALU.add))
                for k in range(1, NBLK + 1):
                    dk = DELTA[:, 32 * (k - 1):32 * k].unsqueeze(1).to_broadcast([128, NT, NE])
                    chain(V.scalar_tensor_tensor(out=T3, in0=CM[:, :, :], scalar=float(SL * k), in1=dk, op0=ALU.is_ge, op1=ALU.mult))
                    chain(V.tensor_tensor(GG, GG, GT, ALU.add))
                for k in range(2):
                    chain(V.tensor_tensor(GT, GG, RT[:, 3 + k, :], ALU.mult))
                    ins = V.tensor_reduce(GF[:, k, :], T3, AX.X, ALU.add)
                    chain(ins)
                V.tensor_copy(GI[:, :, :], GF[:, :, :]).then_inc(rt_slots, 1)
                ev = const("evens")
                last = NBLK * 32 - 1
                chain(V.tensor_tensor(RS[:, 8, 0:7], INC[:, last:last + 1].to_broadcast([128, 7]), ev, ALU.is_gt))
                chain(V.tensor_reduce(RS[:, 7, 0:1], RS[:, 8, 0:7], AX.X, ALU.add))
                chain(V.tensor_copy(RI[:, :], RS[:, 7, 0:1]))
                chain(V.tensor_tensor(DELTA, INC, IND, ALU.subtract))
                chain(V.tensor_tensor(EXW, DELTA.unsqueeze(1).to_broadcast([128, NEXTRA, NBLK * 32]),
                                      const("iota")[:, 0:NEXTRA].unsqueeze(2).to_broadcast([128, NEXTRA, NBLK * 32]), ALU.is_equal))
                chain(V.tensor_tensor(IND.rearrange("p (k e) -> p k e", e=NE), IND.rearrange("p (k e) -> p k e", e=NE),
                                      const("iota")[:, 0:NE].unsqueeze(1).to_broadcast([128, NBLK, NE]), ALU.mult))
                chain(V.tensor_tensor(EXW, EXW, IND.unsqueeze(1).to_broadcast([128, NEXTRA, NBLK * 32]), ALU.mult))
                chain(V.tensor_reduce(EXF, EXW, AX.X, ALU.add))
                V.tensor_copy(EXI[:, :], EXF).then_inc(rt_ready, 1)
                filled(dve, "tb", l)
                chain(V.tensor_copy(TI[0:SL, :], ps("tb", l)[0:SL, 0:NTILE]))
                release(V.tensor_copy(TY[0:SL, :], ps("tb", l)[0:SL, NTILE:2 * NTILE]), "tb", l)

                def tiles(n0, h0, count):
                    def out_half(u):
                        dve.wait_ge(m["down"], n0 + (u + 1))
                        dve.wait_ge(m[f"s{u % 2}"], 16 + h0 + 16 * (u // 2))
                        V.tensor_copy(ZT[0:SL, u % 2, 512:1024], result_bank(u, 1)).then_inc(m["yv"], 1)

                    for u in range(count):
                        dve.wait_ge(m["t"], n0 + (u + 1))
                        if u >= 2:
                            dve.wait_ge(m["gu"], n0 + (u - 1))
                        V.tensor_copy(XGT[:, u % 2, 4 * SL:8 * SL], turned_bank(1)).then_inc(m["xv"], 1)
                        if u >= 1:
                            out_half(u - 1)
                        dve.wait_ge(m["sg"], n0 + (u + 1))
                        V.tensor_tensor(HID[:, u % 2, 0:SL], bank(2 + u % 2)[:, SL:2 * SL], SG[:, u % 2, 0:SL],
                                        ALU.mult).then_inc(m["hid"], 1)
                    out_half(count - 1)
                dve.sem_inc(m["xv"], 1)
                dve.sem_inc(m["yv"], 2)
                dve.wait_ge(rt_ready, l + 1)
                pairs = dve.value_load(RI[0:1, 0:1], min_val=0, max_val=NEXTRA // 2)
                with dve.Fori(0, NI) as i:
                    tiles(i * U, i * (8 * U), U)
                with dve.If(pairs > 0):
                    with dve.Fori(0, pairs) as j:
                        tiles(j * 2 + NE, j * 16 + 8 * NE, 2)
                dve.wait_ge(moe_done, l + 1)
                def ln_scale_shift(t):
                    q = 10 * l + 5 + t
                    b = q % 2
                    dve.wait_ge(ln_sd, q + 1)
                    chain(V.reciprocal(RSD[:, b, 1:2], RSD[:, b, 0:1]))
                    V.scalar_tensor_tensor(out=NB[:, b:b + 1], in0=MV[:, b, 0:1], scalar=-1.0, in1=RSD[:, b, 1:2],
                                           op0=ALU.mult, op1=ALU.mult).then_inc(ln_shift, 1)

                for t in range(NT):
                    q, g = 10 * l + 5 + t, (0 if t < 4 else 1)
                    b, yb = q % 2, t % 2
                    cnt = ((3 if yb == 0 else 2) * l + t // 2 + 1) * 32
                    dve.wait_ge(d_yl[yb], cnt)
                    dve.wait_ge(y_scaled, 5 * l + t + 1)
                    chain(V.scalar_tensor_tensor(out=YB[:, yb, 0, :], in0=YB[:, yb, 1, :], scalar=W12[:, 1, t:t + 1],
                                                 in1=YB[:, yb, 0, :], op0=ALU.mult, op1=ALU.add))
                    if t >= 1:
                        ln_scale_shift(t - 1)
                    if t >= 2:
                        dve.wait_ge(x_ready, q - 1)
                    V.tensor_tensor(ZT[:, b, :], YB[:, yb, 0, :], R5[:, g, :], ALU.mult).then_inc(y_used, 1)
                    dve.wait_ge(y_used, 5 * l + t + 1)
                    chain(V.scalar_tensor_tensor(out=ZT[:, b, :], in0=X[:, t, :], scalar=ALPHA, in1=ZT[:, b, :],
                                                 op0=ALU.mult, op1=ALU.add))
                    ln_first(q)
                ln_scale_shift(4)

        @block.tensor
        def _(pe):
            T = nc.tensor

            def mod_product(l, c, lo=0, hi=KD):
                if lo == 0:
                    weights(pe, "mod", l, c)
                    open_group(pe, "mod", l, c)
                w = slot3(WITEM[("mod", l, c)]["slot"]).rearrange("p (k n) -> p k n", k=8)
                for k in range(lo, hi):
                    ins = T.matmul(ps("mod", l, c)[0:2, 0:512], CT[:, :].rearrange("p (g k) -> p k g", g=2)[:, k, :],
                                   w[:, k, :], start=(k == 0), stop=(k == KD - 1))
                if hi == KD:
                    close_group(ins, "mod", l, c)

            def mod_turn(l, c):
                emptied(pe, "mod", l, c)
                open_group(pe, "modb", l, c)
                for b in range(4):
                    ins = T.matmul(ps("modb", l, c)[:, 2 * b:2 * b + 2], MR[:, c % 2, b * 128:b * 128 + 128],
                                   C[0:2, 0:2], start=True, stop=True)
                close_group(ins, "modb", l, c)

            def side(kind, l, c):
                (mod_product if kind == "mod" else mod_turn)(l, c)

            def x_transposes0():
                for k in range(KD):
                    open_group(pe, "xT", 0, k)
                    for t in range(NT):
                        ins = T.transpose(ps("xT", 0, k)[:, t * 128:t * 128 + 128], X[:, t, k * 128:k * 128 + 128], ident)
                    close_group(ins, "xT", 0, k)
                for k in range(KD):
                    emptied(pe, "xT", 0, k)

            def x_transposes1():
                for t in range(NT):
                    pe.wait_ge(x_ready, 5 + t + 1)
                    open_group(pe, "xT", 1, t)
                    for k in range(KD):
                        ins = T.transpose(ps("xT", 1, t)[:, k * 128:k * 128 + 128], X[:, t, k * 128:k * 128 + 128], ident)
                    close_group(ins, "xT", 1, t)
                for t in range(NT):
                    emptied(pe, "xT", 1, t)

            def project_cm(name, w, col):
                open_group(pe, *name)
                for a, b in ((0, 512), (512, 640)):
                    for k in range(KD):
                        ins = T.matmul(ps(*name)[:, a:b], w[:, k, col:col + 128], HT[:, k, a:b],
                                       start=(k == 0), stop=(k == KD - 1))
                close_group(ins, *name)

            def project_tm(name, src, t, parts):
                open_group(pe, *name)
                for at, w in parts:
                    for k in range(KD):
                        ins = T.matmul(ps(*name)[:, at:at + w.shape[2]], src[:, k, t * 128:t * 128 + 128], w[:, k, :],
                                       start=(k == 0), stop=(k == KD - 1))
                close_group(ins, *name)

            def w8(words, n=512):
                return words[:, 0:8 * n].rearrange("p (k n) -> p k n", k=8)

            pe.wait_ge(d_const, 16)
            pe.wait_ge(d_vec, 16 * 5)
            pe.wait_ge(d_vec_a, 16 * 4)
            pe.wait_ge(c_silu, 1)
            v = ps("vec")
            T.matmul(v[:, 0:16], V1[:, :], C[0:16, 0:16], start=True, stop=True)
            T.matmul(v[:, 16:59], V2[:, :], C[0:43, 0:43], start=True, stop=True)
            close_group(T.matmul(v[:, 64:188], V3[:, :], C[0:124, 0:124], start=True, stop=True), "vec")
            emptied(pe, "vec")
            for kind, c in FIRST_MODS:
                side(kind, 0, c)
            pe.wait_ge(d_x, 32)
            x_transposes0()

            wa, wb = w8(weights(pe, "cqa")), w8(weights(pe, "cqb"), AB_IN - 3072)
            for t in range(NT):
                project_tm(("cq", t), HT, t, [(0, wa), (512, wb)])
            pe.wait_ge(norm_ready, NT)
            pe.wait_ge(d_cache, 32)
            for r in range(3):
                open_group(pe, "cqT", r)
                for t in range(NT):
                    ins = T.transpose(ps("cqT", r)[:, t * 128:t * 128 + 128], CQ[:, t, r * 128:r * 128 + 128], ident)
                close_group(ins, "cqT", r)
            for r in range(2):
                open_group(pe, "ckvT", r)
                srcs = [CQ[:, t, QR + r * 128:QR + r * 128 + 128] for t in range(4)]
                srcs += [CC[:, r * 128:r * 128 + 128], CQ[:, 4, QR + r * 128:QR + r * 128 + 128]]
                for t, src in enumerate(srcs):
                    ins = T.transpose(ps("ckvT", r)[:, t * 128:t * 128 + 128], src, ident)
                close_group(ins, "ckvT", r)
            open_group(pe, "krT")
            srcs = [CQ[:, t, 640:672] for t in range(4)] + [CC[:, KVR:288], CQ[:, 4, 640:672]]
            for t, src in enumerate(srcs):
                ins = T.matmul(ps("krT")[64:96, t * 128:t * 128 + 128], src, ident, start=True, stop=True)
            close_group(ins, "krT")
            perm = const("perm", slice(64, 96))
            emptied(pe, "krT")
            open_group(pe, "krP")
            close_group(T.matmul(ps("krP")[64:96, 0:512], perm, KRS[64:96, :], start=True, stop=True), "krP")
            uq = weights(pe, "uq")[:, 0:2304].rearrange("p (k n) -> p k n", k=3)
            ukv = weights(pe, "ukv")[:, 0:2048].rearrange("p (k n) -> p k n", k=2)
            for r in range(2):
                emptied(pe, "ckvT", r)
            wv = ukv.rearrange("p k (h c) -> p k h c", h=8)[:, :, :, 64:128]
            for t in range(6):
                open_group(pe, "v", t)
                for r in range(2):
                    ins = T.matmul(ps("v", t)[:, 0:512].rearrange("p (h c) -> p h c", h=8),
                                   CKVT[:, r, t * 128:t * 128 + 128], wv[:, r], start=(r == 0), stop=(r == 1))
                close_group(ins, "v", t)
            for r in range(3):
                emptied(pe, "cqT", r)

            def keys_queries(h):
                open_group(pe, "k", h)
                for a, b in ((0, 512), (512, 768)):
                    for r in range(2):
                        ins = T.matmul(ps("k", h)[0:64, a:b], ukv[:, r, h * 128:h * 128 + 64], CKVT[:, r, a:b],
                                       start=(r == 0), stop=(r == 1))
                close_group(ins, "k", h)
                open_group(pe, "q", h)
                for a, b in ((0, 512), (512, 640)):
                    for r in range(3):
                        ins = T.matmul(ps("q", h)[0:96, a:b], uq[:, r, h * 96:h * 96 + 96], CQT[:, r, a:b],
                                       start=(r == 0), stop=(r == 2))
                close_group(ins, "q", h)

            def swap_pairs(h):
                emptied(pe, "q", h)
                open_group(pe, "qP", h)
                close_group(T.matmul(ps("qP", h)[64:96, 0:512], perm, QT[64:96, h % 2, 0:512], start=True, stop=True), "qP", h)

            def scores(h, t):
                if t == 0:
                    emptied(pe, "k", h)
                    pe.wait_ge(q_rot, h + 1)
                    pe.wait_ge(kr_ready, 2)
                open_group(pe, "s", h, t)
                q = QT[0:96, h % 2, t * 128:t * 128 + 128]
                for a, b in (((0, 512), (512, 640)) if t < 4 else ((0, 128),)):
                    ka = a if t < 4 else 640
                    ins = T.matmul(ps("s", h, t)[:, a:b], q, KT[0:96, h % 2, ka:ka + b - a], start=True, stop=True)
                close_group(ins, "s", h, t)

            for t in range(6):
                emptied(pe, "v", t)
            keys_queries(0)
            swap_pairs(0)
            steps = [(h, t) for h in range(MH) for t in range(NT)]
            scores(0, 0)
            for n, (h, t) in enumerate(steps):
                if h + 1 < MH and t == 0:
                    keys_queries(h + 1)
                if h + 1 < MH and t == 2:
                    swap_pairs(h + 1)
                if n + 1 < len(steps):
                    scores(*steps[n + 1])
                if t == ATTN_MOD_TILE:
                    mod_product(0, 4 + h, 0, KD // 2)
                blocks = [0, 1, 2, 3, 4] if t < 4 else [5]
                emptied(pe, "s", h, t)
                open_group(pe, "pt", h, t)
                for j, kb in enumerate(blocks):
                    ins = T.transpose(ps("pt", h, t)[:, j * 128:j * 128 + 128], PB[:, n % 2, j * 128:j * 128 + 128], ident)
                close_group(ins, "pt", h, t)
                if t == ATTN_MOD_TILE:
                    mod_product(0, 4 + h, KD // 2, KD)
                emptied(pe, "pt", h, t)
                open_group(pe, "o", h, t)
                for j, kb in enumerate(blocks):
                    ins = T.matmul(ps("o", h, t)[:, 0:64], PTS[:, n % 2, j * 128:j * 128 + 128], VT[:, kb, h * 64:h * 64 + 64],
                                   start=(j == 0), stop=(j == len(blocks) - 1))
                close_group(ins, "o", h, t)
            emptied(pe, "o", MH - 1, NT - 1)
            for j in range(4):
                open_group(pe, "obT", j)
                for t in range(NT):
                    ins = T.transpose(ps("obT", j)[:, t * 128:t * 128 + 128], OB[:, t, j * 128:j * 128 + 128], ident)
                close_group(ins, "obT", j)

            for c in range(3):
                w = w8(weights(pe, "hq", c))
                for j in range(4):
                    project_cm(("hq", c, j), w, j * 128)
            for c in range(2):
                w = w8(weights(pe, "hv", c))
                for t in range(NT):
                    project_tm(("hv", c, t), HT, t, [(0, w)])
            emptied(pe, "hv", 0, 4)
            for u in range(4):
                d, hp = u // 2, u % 2

                def tile_at(n):
                    return (n if d == 0 else 3 - n) if n < 4 else 4

                def intra(n):
                    i, t = 5 * u + n, tile_at(n)
                    tc = slice(t * 128, t * 128 + 128)
                    open_group(pe, "hs", u, n)
                    for hh in range(2):
                        ins = T.matmul(ps("hs", u, n)[:, hh * 128:hh * 128 + 128], KHAT[:, hh, tc], QHAT[:, hh, tc],
                                       start=True, stop=True)
                    close_group(ins, "hs", u, n)
                    open_group(pe, "hk", u, n)
                    for hh in range(2):
                        ins = T.transpose(ps("hk", u, n)[:, hh * 128:hh * 128 + 128], KTIL[:, hh, tc], ident)
                    close_group(ins, "hk", u, n)
                    emptied(pe, "hk", u, n)
                    pe.wait_ge(h_vm, 4 * (i + 1))
                    open_group(pe, "hd", u, n)
                    for hh in range(2):
                        ins = T.matmul(ps("hd", u, n)[:, hh * 512:hh * 512 + 512], KTT[:, i % 2, hh * 128:hh * 128 + 128],
                                       VM[:, i % 2, hh, :, :].rearrange("p j v -> p (j v)"), start=True, stop=True)
                    close_group(ins, "hd", u, n)

                for piece in UNIT_MODS[u]:
                    side(*piece)
                pe.wait_ge(h_mul, 4 * (u + 1))
                intra(0)
                for n in range(NT):
                    if n + 1 < NT:
                        intra(n + 1)
                    i, t = 5 * u + n, tile_at(n)
                    emptied(pe, "hs", u, n)
                    emptied(pe, "hd", u, n)
                    open_group(pe, "ho", u, n)
                    for hh in range(2):
                        h = 2 * hp + hh
                        T.matmul(ps("ho", u, n)[:, hh * 128:hh * 128 + 128], SC[:, d, i % 2, hh, :],
                                 HV[:, t, h * 128:h * 128 + 128], start=True, stop=False, skip_group_check=True)
                        for step in range(4):
                            j = step if d == 0 else 3 - step
                            ins = T.matmul(ps("ho", u, n)[32 * j:32 * j + 32, hh * 128:hh * 128 + 128],
                                           QTIL[:, hh, t * 128 + 32 * j:t * 128 + 32 * j + 32], state_before(i, n, step, hh),
                                           start=False, stop=(step == 3), skip_group_check=True)
                    close_group(ins, "ho", u, n)
                    for piece in STEP_MODS.get((u, n), []):
                        side(*piece)
            pe.wait_ge(o_ready, 2)
            for j in range(4):
                open_group(pe, "oaT", j)
                for t in range(NT):
                    ins = T.transpose(ps("oaT", j)[:, t * 128:t * 128 + 128], HO[:, t, j * 128:j * 128 + 128], ident)
                close_group(ins, "oaT", j)

            for l in range(2):
                m = MS[l]
                if l == 1:
                    x_transposes1()
                    for c in CD_ORDER:
                        w = w8(weights(pe, "cd", c))
                        for j in range(4):
                            project_cm(("cd", c, j), w, j * 128)
                    pe.wait_ge(cd_up, 1)
                    for j in range(4):
                        pe.wait_ge(tap_diag, PE_TAPS * (j + 1))
                        open_group(pe, "cv", j)
                        for i in range(PE_TAPS):
                            k = CFK - PE_TAPS + i
                            for at, a, n in ((0, 0, 512), (512, 527, 128)):
                                ins = T.matmul(ps("cv", j)[:, at:at + n], DG[PE_TAPS * j + i], UP[:, j, a + k:a + k + n],
                                               start=(i == 0), stop=(i == PE_TAPS - 1))
                        close_group(ins, "cv", j)
                    emptied(pe, "cv", 3)
                    for name, src in (("mean", CO), ("var", SQ)):
                        pe.wait_ge(cd_conv if name == "mean" else cd_sq, 4 if name == "mean" else 1)
                        open_group(pe, name)
                        for b in range(2):
                            for j in range(4):
                                ins = T.matmul(ps(name)[:, b * 512:b * 512 + 328], const("ones")[:, 0:128], src[:, j, b * 328:b * 328 + 328],
                                               start=(j == 0), stop=(j == 3))
                        close_group(ins, name)
                if l == 0:
                    for j in range(4):
                        emptied(pe, "oaT", j)
                else:
                    pe.wait_ge(cd_out_v, 1)
                    pe.wait_ge(cd_out, 4)
                w0, w1 = w8(weights(pe, "wo", l, 0)), w8(weights(pe, "wo", l, 1))
                for kind, t in OUT_ORDER:
                    if kind == "y":
                        project_tm(("y", l, t), OT, t, [(0, w0), (512, w1)])
                    elif kind == "hT":
                        pe.wait_ge(h_ready, 5 * l + t + 1)
                        open_group(pe, "hT", l, t)
                        for k in range(KD):
                            ins = T.transpose(ps("hT", l, t)[:, k * 128:k * 128 + 128], HB[:, t % 2, k * 128:k * 128 + 128], ident)
                        close_group(ins, "hT", l, t)
                    else:
                        pe.wait_ge(d_wr, 32 * (l + 1))
                        emptied(pe, "hT", l, t)
                        open_group(pe, "lg", l, t)
                        for k in range(KD):
                            ins = T.matmul(ps("lg", l, t)[:, 0:36], HT[:, k, t * 128:t * 128 + 128], WR[:, k, :],
                                           start=(k == 0), stop=(k == KD - 1))
                        close_group(ins, "lg", l, t)
                pe.wait_ge(rt_mask, l + 1)
                open_group(pe, "ct", l)
                T.matmul(ps("ct", l)[:, 0:160], const("tri"), RT[:, 5, :], start=True, stop=True)
                close_group(T.matmul(ps("ct", l)[:, 512:672], const("ones")[:, 0:128], RT[:, 5, :], start=True, stop=True), "ct", l)
                pe.wait_ge(d_tb, 16 * (l + 1))
                open_group(pe, "tb", l)
                for c in range(2):
                    ins = T.matmul(ps("tb", l)[0:SL, NTILE * c:NTILE * (c + 1)], TBR.rearrange("n (s c) -> n c s", c=2)[:, c, :],
                                   C[0:NTILE, 0:NTILE], start=True, stop=True)
                close_group(ins, "tb", l)
                emptied(pe, "hT", l, 4)
                for t in range(1, NT):
                    emptied(pe, "lg", l, t)
                emptied(pe, "ct", l)
                emptied(pe, "tb", l)

                def tiles(n0, h0, count, arrived):
                    def transposes(u):
                        pe.wait_ge(m[f"g{u % 2}"], h0 + 16 * (u // 2 + 1))
                        pe.wait_ge(m["xa"], 1 + n0 + u)
                        pe.wait_ge(m["xv"], 1 + n0 + u)
                        rows = XG[0:SL, u % 2, :].rearrange("s (p k) -> s k p", k=KD)
                        for k in range(KD):
                            ins = T.transpose(turned_bank(k // 4)[:, (k % 4) * SL:(k % 4) * SL + SL],
                                              rows[:, k, :], ident[0:SL, 0:SL])
                        ins.then_inc(m["t"], 1)

                    def gate_up(u):
                        arrived(u)
                        pe.wait_ge(m["xa"], 1 + n0 + (u + 1))
                        pe.wait_ge(m["xv"], 1 + n0 + (u + 1))
                        if u >= 2:
                            pe.wait_ge(m["hid"], n0 + (u - 1))
                        for g in range(2):
                            w = expert_gu(u % 4, g)
                            for k in range(KD):
                                ins = T.matmul(bank(2 + u % 2)[:, SL * g:SL * g + SL], w[:, k * FF:k * FF + FF],
                                               XGT[:, u % 2, k * SL:k * SL + SL], start=(k == 0), stop=(k == KD - 1))
                        ins.then_inc(m["gu"], 1)

                    def down(u):
                        pe.wait_ge(m["hid"], n0 + (u + 1))
                        pe.wait_ge(m["ya"], n0 + (u + 1))
                        pe.wait_ge(m["yv"], n0 + (u + 1))
                        w = expert_down(u % 4)
                        for b in range(2):
                            ins = T.matmul(result_bank(u, b), HID[:, u % 2, 0:SL], w[:, b * 512:b * 512 + 512],
                                           start=True, stop=True)
                        ins.then_inc(m["down"], 1)

                    transposes(0)
                    gate_up(0)
                    for u in range(1, count):
                        transposes(u)
                        down(u - 1)
                        gate_up(u)
                    down(count - 1)

                pe.wait_ge(rt_ready, l + 1)
                pairs = pe.value_load(RI[0:1, 0:1], min_val=0, max_val=NEXTRA // 2)
                with pe.Fori(0, NI) as i:
                    tiles(i * U, i * (8 * U), U, lambda u: pe.wait_ge(m[f"w{u % 4}"], i * 96 + 48 * (u // 4 + 1)))
                with pe.If(pairs > 0):
                    with pe.Fori(0, pairs) as j:
                        tiles(j * 2 + NE, j * 16 + 8 * NE, 2, lambda u: pe.wait_ge(m[f"xw{u}"], j * 48 + 48))
                pe.wait_ge(moe_done, l + 1)

    return nc


_INS = ['x_prompt', 'x_sample', 'state_hgrn_fwd', 'state_hgrn_bwd', 'cache_mla_ckv', 'cache_mla_krope', 'c', 'c_ctx',
        'mod_w', 'mod_b', 'ln_g', 'ln_b', 'ab_w_in', 'ab_w_out', 'hgrn_lb_logits', 'hgrn_norm_g', 'mla_q_norm_g',
        'mla_w_uq', 'mla_kv_norm_g', 'mla_w_ukv', 'cd_w_in', 'cd_w_out', 'sc_conv_w', 'cf_conv_w', 'cf_conv_b',
        'cf_ln_g', 'cf_ln_b', 'moe_w_group', 'moe_w_expert', 'moe_w_gate', 'moe_w_up', 'moe_w_down']
_OUTS = [("y_prompt", (1, 128, D)), ("y_sample", (1, 512, D)), ("new_sf", (1, 1, HA, DK, DK)), ("new_sb", (1, 1, HA, DK, DK)),
         ("new_ckv", (1, 1, 128, KVR)), ("new_kr", (1, 1, 128, DR))]


def kernel(**inputs):
    import concourse.bacc as bacc
    from concourse.bass_utils import run_bass_kernel_spmd

    nc = bacc.Bacc("TRN2", target_bir_lowering=False, num_devices=1)
    arrays, A, O = {}, {}, {}
    for name in _INS:
        arrays["in_" + name] = np.ascontiguousarray(inputs[name])
    arrays["in_consts"] = constants()
    for name, a in arrays.items():
        A[name[3:]] = nc.dram_tensor(name, a.shape, mybir.dt.from_np(a.dtype), kind="ExternalInput").ap()
    for name, shape in _OUTS:
        O[name] = nc.dram_tensor("out_" + name, shape, mybir.dt.float32, kind="ExternalOutput").ap()
    build(nc, A, O)
    r = run_bass_kernel_spmd(nc, [arrays], core_ids=[0])
    return tuple(r.results[0]["out_" + name] for name, _ in _OUTS)
```
